# Optimizing a Trainium2 kernel written in Bass

```python
import jax
import jax.numpy as jnp
from jax import lax
import numpy as np

D_MODEL = 2048
BATCH = 1
SEQ = 256
DEPTH = 1

GRID_W = 64
CTX_LEN = 256

HA = 8
DK_A = 128
DV_A = 128
WK_A = HA * DK_A
WA = HA * DV_A
CHUNK_A = 64

POOL_WINDOWS = (2, 4, 8, 16)
N_POOL = 4
POOL_GW = 256
WB = N_POOL * POOL_GW

HQ = 8
HKV = 2
GQ = HQ // HKV
HD = 128
WC = HQ * HD
WINDOW = 128
BLOCK_Q = 128
ROPE_THETA = 10000.0

N_BRANCH = 3
BRANCH_W = 1024
D_FF = 4 * D_MODEL
N_ADA = 6
LN_EPS = 1e-5
RMS_EPS = 1e-6
ALPHA = (2.0 * DEPTH) ** 0.25
BETA = (8.0 * DEPTH) ** -0.25

COL_AQ = 0
COL_AI = COL_AQ + WK_A
COL_AG = COL_AI + WA
COL_AFF = COL_AG + WA
COL_AFB = COL_AFF + WK_A
COL_B = COL_AFB + WK_A
COL_CQ = COL_B + WB
COL_CK = COL_CQ + WC
COL_CV = COL_CK + HKV * HD
COL_GATE = COL_CV + HKV * HD
N_COLS = COL_GATE + N_BRANCH * D_MODEL

kernel_name = 'hybrid_dit_hgrn2_pool_swa_trunk'

def _layer_norm(x, g, b):
    xf = x.astype(jnp.float32)
    mu = jnp.mean(xf, -1, keepdims=True)
    var = jnp.mean(jnp.square(xf - mu), -1, keepdims=True)
    return ((xf - mu) * lax.rsqrt(var + LN_EPS)).astype(x.dtype) * g + b

def _head_rms_norm(o, g):
    B, T = o.shape[:2]
    o = o * lax.rsqrt(jnp.mean(jnp.square(o), -1, keepdims=True) + RMS_EPS)
    return o.reshape(B, T, -1).astype(g.dtype) * g

def _axial_rope(t_len):
    rows = t_len // GRID_W
    row = jnp.repeat(jnp.arange(rows, dtype=jnp.float32), GRID_W)
    col = jnp.tile(jnp.arange(GRID_W, dtype=jnp.float32), rows)
    n_freq = HD // 4
    inv_freq = ROPE_THETA ** (-jnp.arange(n_freq, dtype=jnp.float32) / n_freq)
    ang = jnp.concatenate([row[:, None] * inv_freq, col[:, None] * inv_freq], -1)
    return jnp.cos(ang), jnp.sin(ang)

def _apply_rope(x, cos, sin):
    shape = (1, x.shape[1]) + (1,) * (x.ndim - 3) + (HD // 2,)
    cos = cos.reshape(shape).astype(x.dtype)
    sin = sin.reshape(shape).astype(x.dtype)
    x1, x2 = x[..., : HD // 2], x[..., HD // 2:]
    return jnp.concatenate([x1 * cos - x2 * sin, x2 * cos + x1 * sin], -1)

def _hgrn_gates(z, lb):
    z = z.astype(jnp.float32)
    lb = lb.astype(jnp.float32)
    logf = jnp.logaddexp(jnp.log(lb), jnp.log1p(-lb) + jax.nn.log_sigmoid(z))
    k = (1.0 - lb) * jax.nn.sigmoid(-z)
    return logf, k

def _hgrn_chunk_scan(q, k, logf, v, s0):
    B, T, H, _ = q.shape
    n = T // CHUNK_A

    def chunks(a):
        a = a.astype(jnp.float32).reshape(B, n, CHUNK_A, H, a.shape[-1])
        return jnp.transpose(a, (1, 0, 3, 2, 4))

    lower = jnp.tril(jnp.ones((CHUNK_A, CHUNK_A), dtype=bool))[:, :, None]

    def step(s, inp):
        qc, kc, lfc, vc = inp
        b = jnp.cumsum(lfc, axis=-2)
        diff = b[..., :, None, :] - b[..., None, :, :]
        decay = jnp.exp(jnp.where(lower, diff, -jnp.inf))
        scores = jnp.einsum('bhtd,bhsd,bhtsd->bhts', qc, kc, decay)
        o = jnp.einsum('bhts,bhsv->bhtv', scores, vc) + jnp.einsum('bhtd,bhdv->bhtv', qc * jnp.exp(b), s)
        b_end = b[..., -1:, :]
        s_new = jnp.exp(b_end[..., 0, :])[..., None] * s + jnp.einsum('bhsd,bhsv->bhdv', kc * jnp.exp(b_end - b), vc)
        return s_new, o

    s_fin, o = lax.scan(step, s0, (chunks(q), chunks(k), chunks(logf), chunks(v)))
    o = jnp.transpose(o, (1, 0, 3, 2, 4)).reshape(B, T, H, -1)
    return o, s_fin

def _hgrn_split(u, lb_fwd, lb_bwd):
    B, T = u.shape[:2]
    q = u[..., COL_AQ:COL_AQ + WK_A].reshape(B, T, HA, DK_A)
    i = u[..., COL_AI:COL_AI + WA].reshape(B, T, HA, DV_A)
    g = u[..., COL_AG:COL_AG + WA]
    lf_f, k_f = _hgrn_gates(u[..., COL_AFF:COL_AFF + WK_A].reshape(B, T, HA, DK_A), lb_fwd.reshape(HA, DK_A))
    lf_b, k_b = _hgrn_gates(u[..., COL_AFB:COL_AFB + WK_A].reshape(B, T, HA, DK_A), lb_bwd.reshape(HA, DK_A))
    return q, i, g, lf_f, k_f, lf_b, k_b

def _hgrn_mixer(u_c, u_l, lb_fwd, lb_bwd, norm_g, need_ctx):
    qc, ic, gc, lfc_f, kc_f, lfc_b, kc_b = _hgrn_split(u_c, lb_fwd, lb_bwd)
    ql, il, gl, lfl_f, kl_f, lfl_b, kl_b = _hgrn_split(u_l, lb_fwd, lb_bwd)
    B = u_l.shape[0]
    s0 = jnp.zeros((B, HA, DK_A, DV_A), jnp.float32)
    flip = lambda a: jnp.flip(a, axis=1)
    oc_f, sc_f = _hgrn_chunk_scan(qc, kc_f, lfc_f, ic, s0)
    oc_b, sc_b = _hgrn_chunk_scan(flip(qc), flip(kc_b), flip(lfc_b), flip(ic), s0)
    ol_f, _ = _hgrn_chunk_scan(ql, kl_f, lfl_f, il, sc_f)
    ol_b, _ = _hgrn_chunk_scan(flip(ql), flip(kl_b), flip(lfl_b), flip(il), sc_b)
    y_l = _head_rms_norm(ol_f + flip(ol_b), norm_g) * jax.nn.silu(gl)
    y_c = _head_rms_norm(oc_f + flip(oc_b), norm_g) * jax.nn.silu(gc) if need_ctx else None
    return y_c, y_l

def _centred_mean(u, w):
    T = u.shape[1]
    cs = jnp.pad(jnp.cumsum(u.astype(jnp.float32), axis=1), ((0, 0), (1, 0), (0, 0)))
    t = jnp.arange(T)
    lo = jnp.clip(t - w // 2, 0, T)
    hi = jnp.clip(t + w // 2, 0, T)
    cnt = (hi - lo).astype(jnp.float32)[None, :, None]
    return ((cs[:, hi] - cs[:, lo]) / cnt).astype(u.dtype)

def _pool_mixer(u, w_grp, scale):
    B, T = u.shape[:2]
    ug = u[..., COL_B:COL_B + WB].reshape(B, T, N_POOL, POOL_GW)
    pooled = jnp.stack([_centred_mean(ug[:, :, j], w) for j, w in enumerate(POOL_WINDOWS)], axis=2)
    y = jnp.einsum('btgc,gcd->btgd', pooled - ug, w_grp).reshape(B, T, WB)
    return y * scale

def _attention_mixer(u_c, u_l, sink, need_ctx):
    B, T = u_l.shape[:2]
    nb = T // BLOCK_Q
    nw = 3 * BLOCK_Q

    def qkv(u):
        Tn = u.shape[1]
        q = u[..., COL_CQ:COL_CQ + WC].reshape(B, Tn, HKV, GQ, HD)
        k = u[..., COL_CK:COL_CK + HKV * HD].reshape(B, Tn, HKV, HD)
        v = u[..., COL_CV:COL_CV + HKV * HD].reshape(B, Tn, HKV, HD)
        return q, k, v

    qc, kc, vc = qkv(u_c)
    ql, kl, vl = qkv(u_l)
    nc = kc.shape[1]
    cos, sin = _axial_rope(T)
    ql = _apply_rope(ql, cos, sin)
    kl = _apply_rope(kl, cos, sin)
    scale = HD ** -0.5
    sink_l = sink.astype(jnp.float32).reshape(HKV, GQ)

    qb = ql.reshape(B, nb, BLOCK_Q, HKV, GQ, HD)

    def band(a):
        ap = jnp.pad(a, ((0, 0), (BLOCK_Q, BLOCK_Q), (0, 0), (0, 0))).reshape(B, nb + 2, BLOCK_Q, HKV, HD)
        return jnp.concatenate([ap[:, :-2], ap[:, 1:-1], ap[:, 2:]], axis=2)

    kw, vw = band(kl), band(vl)
    q_pos = jnp.arange(T).reshape(nb, BLOCK_Q)
    k_pos = jnp.arange(nb)[:, None] * BLOCK_Q + jnp.arange(nw)[None, :] - BLOCK_Q
    kp = k_pos[:, None, :]
    valid = (jnp.abs(q_pos[:, :, None] - kp) <= WINDOW) & (kp >= 0) & (kp < T)
    s_win = jnp.einsum('bnqkgd,bnskd->bnkgqs', qb, kw).astype(jnp.float32) * scale
    s_win = jnp.where(valid[None, :, None, None], s_win, -jnp.inf)
    s_ctx = jnp.einsum('bnqkgd,bskd->bnkgqs', qb, kc).astype(jnp.float32) * scale
    s_sink = jnp.broadcast_to(sink_l[None, None, :, :, None, None], s_ctx.shape[:-1] + (1,))
    p = jax.nn.softmax(jnp.concatenate([s_win, s_ctx, s_sink], -1), axis=-1).astype(u_l.dtype)
    o = jnp.einsum('bnkgqs,bnskd->bnqkgd', p[..., :nw], vw) + jnp.einsum('bnkgqs,bskd->bnqkgd', p[..., nw:nw + nc], vc)
    y_l = o.reshape(B, T, WC)

    y_c = None
    if need_ctx:
        s_cc = jnp.einsum('btkgd,bskd->bkgts', qc, kc).astype(jnp.float32) * scale
        s_sink_c = jnp.broadcast_to(sink_l[None, :, :, None, None], s_cc.shape[:-1] + (1,))
        p_c = jax.nn.softmax(jnp.concatenate([s_cc, s_sink_c], -1), axis=-1).astype(u_c.dtype)
        y_c = jnp.einsum('bkgts,bskd->btkgd', p_c[..., :nc], vc).reshape(B, nc, WC)
    return y_c, y_l

def _merge_branches(u, ys, w_branch, w_out):
    B, T = u.shape[:2]
    z = jnp.einsum('btjc,jcd->btjd', jnp.stack(ys, axis=2), w_branch)
    gates = jax.nn.sigmoid(u[..., COL_GATE:].reshape(B, T, N_BRANCH, D_MODEL))
    return jnp.sum(gates * z, axis=2) @ w_out

def _sq_relu_mlp(h, w1, w2):
    return jnp.square(jax.nn.relu(h @ w1)) @ w2

def _trunk_layer(xc, xl, c, c_ctx, w_ada, b_ada, w_in, lb_fwd, lb_bwd, hgrn_norm, pool_w, pool_scale,
                 attn_sink, w_branch, w_out, ln1_g, ln1_b, w_ff1, w_ff2, ln2_g, ln2_b, need_ctx):
    mod_l = (jax.nn.silu(c) @ w_ada + b_ada)[:, None, :]
    mod_c = (jax.nn.silu(c_ctx) @ w_ada + b_ada)[None, None, :]
    sh1_l, sc1_l, g1_l, sh2_l, sc2_l, g2_l = jnp.split(mod_l, N_ADA, axis=-1)
    sh1_c, sc1_c, g1_c, sh2_c, sc2_c, g2_c = jnp.split(mod_c, N_ADA, axis=-1)

    ul = (xl * (1 + sc1_l) + sh1_l) @ w_in
    uc = (xc * (1 + sc1_c) + sh1_c) @ w_in
    ya_c, ya_l = _hgrn_mixer(uc, ul, lb_fwd, lb_bwd, hgrn_norm, need_ctx)
    yc_c, yc_l = _attention_mixer(uc, ul, attn_sink, need_ctx)
    yb_l = _pool_mixer(ul, pool_w, pool_scale)
    xl = _layer_norm(ALPHA * xl + g1_l * _merge_branches(ul, (ya_l, yb_l, yc_l), w_branch, w_out), ln1_g, ln1_b)
    xl = _layer_norm(ALPHA * xl + g2_l * _sq_relu_mlp(xl * (1 + sc2_l) + sh2_l, w_ff1, w_ff2), ln2_g, ln2_b)

    if need_ctx:
        yb_c = _pool_mixer(uc, pool_w, pool_scale)
        xc = _layer_norm(ALPHA * xc + g1_c * _merge_branches(uc, (ya_c, yb_c, yc_c), w_branch, w_out), ln1_g, ln1_b)
        xc = _layer_norm(ALPHA * xc + g2_c * _sq_relu_mlp(xc * (1 + sc2_c) + sh2_c, w_ff1, w_ff2), ln2_g, ln2_b)
    return xc, xl

def setup_inputs(seed: int = 0) -> dict:
    key = jax.random.key(seed)
    ks = jax.random.split(key, 20)

    def nrm(k, shape, s):
        return jax.random.normal(k, shape, jnp.float32) * s

    return {
        'x': nrm(ks[0], (BATCH, SEQ, D_MODEL), 1.0),
        'c': nrm(ks[1], (BATCH, D_MODEL), 1.0),
        'ctx': nrm(ks[2], (BATCH, CTX_LEN, D_MODEL), 1.0),
        'c_ctx': nrm(ks[3], (D_MODEL,), 1.0),
        'w_ada': nrm(ks[4], (DEPTH, D_MODEL, N_ADA * D_MODEL), 0.3 * D_MODEL ** -0.5),
        'b_ada': nrm(ks[5], (DEPTH, N_ADA * D_MODEL), 0.02),
        'w_in': nrm(ks[6], (DEPTH, D_MODEL, N_COLS), D_MODEL ** -0.5),
        'hgrn_lb': nrm(ks[7], (DEPTH, 2, WK_A), 0.1),
        'hgrn_norm': 1.0 + nrm(ks[8], (DEPTH, WA), 0.1),
        'pool_w': nrm(ks[9], (DEPTH, N_POOL, POOL_GW, POOL_GW), POOL_GW ** -0.5),
        'pool_scale': 1.0 + nrm(ks[10], (DEPTH, WB), 0.1),
        'attn_sink': nrm(ks[11], (DEPTH, HQ), 0.5),
        'w_branch': nrm(ks[12], (DEPTH, N_BRANCH, BRANCH_W, D_MODEL), BRANCH_W ** -0.5),
        'w_out': nrm(ks[13], (DEPTH, D_MODEL, D_MODEL), BETA * D_MODEL ** -0.5),
        'ln1_g': 1.0 + nrm(ks[14], (DEPTH, D_MODEL), 0.1),
        'ln1_b': nrm(ks[15], (DEPTH, D_MODEL), 0.02),
        'w_ff1': nrm(ks[16], (DEPTH, D_MODEL, D_FF), D_MODEL ** -0.5),
        'w_ff2': nrm(ks[17], (DEPTH, D_FF, D_MODEL), BETA * D_FF ** -0.5),
        'ln2_g': 1.0 + nrm(ks[18], (DEPTH, D_MODEL), 0.1),
        'ln2_b': nrm(ks[19], (DEPTH, D_MODEL), 0.02),
    }

def reference(x, c, ctx, c_ctx, w_ada, b_ada, w_in, hgrn_lb, hgrn_norm, pool_w, pool_scale, attn_sink,
              w_branch, w_out, ln1_g, ln1_b, w_ff1, w_ff2, ln2_g, ln2_b):
    lb = jnp.cumsum(jax.nn.softmax(hgrn_lb.astype(jnp.float32), axis=0), axis=0)
    lb = lb - lb[0:1]
    xc, xl = ctx, x
    for l in range(DEPTH):
        xc, xl = _trunk_layer(xc, xl, c, c_ctx, w_ada[l], b_ada[l], w_in[l], lb[l, 0], lb[l, 1], hgrn_norm[l],
                              pool_w[l], pool_scale[l], attn_sink[l], w_branch[l], w_out[l], ln1_g[l], ln1_b[l],
                              w_ff1[l], w_ff2[l], ln2_g[l], ln2_b[l], l < DEPTH - 1)
    return xl


_drawn_inputs = setup_inputs


def setup_inputs(seed=0):
    import zlib

    import numpy as np

    out = dict(_drawn_inputs(seed))
    spreads = {}
    factors = {'ctx': 8.0,
     'c_ctx': 8.0,
     'b_ada': 3.76,
     'hgrn_norm': 23.758,
     'pool_scale': 8.0,
     'attn_sink': 8.0,
     'ln1_b': 2.745,
     'ln2_b': 2.931}
    for name, (base, spread) in spreads.items():
        noise = np.random.default_rng([zlib.crc32(name.encode()), seed]).standard_normal(out[name].shape)
        drawn = base * np.exp(spread * noise) if base else spread * noise
        out[name] = jnp.asarray(drawn.astype(out[name].dtype))
    for name, factor in factors.items():
        out[name] = (out[name] * factor).astype(out[name].dtype)
    return out
```

```python
from contextlib import ExitStack

import numpy as np

import concourse.bass as bass
from concourse import mybir

F32 = mybir.dt.float32
F32R = mybir.dt.float32r
U8 = mybir.dt.uint8
ALU = mybir.AluOpType
ACT = mybir.ActivationFunctionType
AX = mybir.AxisListType.X

P = 128
D = 2048
T = 256
C = 256
KT = D // P
PW = 512
CK = 4
HEADS = 8
HD = 128
GRID_W = 64
ALPHA = 2.0 ** 0.25
LN_EPS = 1e-5
RMS_EPS = 1e-6
SCALE = HD ** -0.5
NEG = -1e30
WINDOWS = (2, 4, 8, 16)
LEVELS = (128, 64, 32, 16, 8, 4, 2, 1, 0)

PAN_AQ, PAN_AI, PAN_AG, PAN_AF, PAN_B, PAN_CQ, PAN_CKV, PAN_GATE = 0, 2, 4, 6, 10, 12, 14, 15

V_C, V_CC, V_BADA, V_NORM, V_PSC, V_L1G, V_L1B, V_L2G, V_L2B, V_SINK, NV = (
    0, 16, 32, 128, 136, 144, 160, 176, 192, 208, 216)
K_ID, K_TRI, K_COS, K_SIN, K_SEL, NK = 0, 128, 384, 640, 896, 898

PAIRED = "sa" * 4
GATED = ("sa" * 4 + "ss") * 2
BRANCHES = (0, 2, 1)

PHASES = [
    ("ada", 1, "s" * 32, [(4, 1, "A")] * 8),
    ("vals", 1, "s" * 12, [(4, 4, "A")] * 3),
    ("forget", 4, PAIRED, [(4, 4, "V")]),
    ("query", 1, "s" * 8, [(4, 4, "A"), (4, 4, "V")]),
    ("mix", 2, "s" * 12, [(4, 4, "V"), (4, 4, "A"), (4, 4, "V")]),
    ("gates", 6, GATED, [(4, 4, "A"), (2, 4, "V")] * 2),
    ("out", 4, "ssss", [(4, 4, "V")]),
    ("mlp", 32, "ssss", [(4, 4, "V")]),
]


class Phase:

    former = None

    def __init__(self, name, n, body, panels, before):
        self.name, self.n, self.body, self.panels = name, n, body, panels
        (self.r0, self.c0, self.a0, self.g0, self.u0, self.f0) = before
        self.at = [l for l, kind in enumerate(body) if kind == "s"] + [len(body)]
        self.ns = body.count("s")
        self.na = body.count("a")
        self.blocks = sum(b for _, b, _ in panels)
        self.u = sum(c - 1 for c, _, _ in panels)
        self.f = {e: sum(b for _, b, x in panels if x == e) for e in "AV"}

    def after(self):
        n = self.n
        return (self.r0 + n * len(self.body), self.c0 + n * self.ns, self.a0 + n * self.na,
                self.g0 + n * self.blocks, self.u0 + n * self.u, {e: self.f0[e] + n * self.f[e] for e in "AV"})

    def raw(self, it, local):
        return (self.r0 + local) % 4, it * (4 * len(self.body)) + 16 * ((self.r0 + local) // 4 + 1)

    def parity(self, s):
        return (self.c0 + s) % 2

    def split_count(self, it, s):
        return it * self.ns + (self.c0 + s + 1)

    def blocks_before(self, it, panel):
        return it * self.blocks + (self.g0 + sum(b for _, b, _ in self.panels[:panel]))

    def released(self, it, s):
        s -= 2
        end, used = 0, 0
        for p, (n, _, _) in enumerate(self.panels):
            if s < end:
                break
            if s < end + n - 1:
                return "w_used", it * self.u + (self.u0 + used + s - end + 1)
            end += n
            used += n - 1
            if s == end - 1:
                return "blk_done", self.blocks_before(it, p + 1)
        return "blk_done", self.blocks_before(it, 0)

    def bank_free(self, it, panel, b):
        n = {e: self.f0[e] + sum(k for _, k, x in self.panels[:panel] if x == e) for e in "AV"}
        who = self.panels[panel - 1][2]
        if isinstance(it, int) and it + panel == 0:
            who = self.former
        return who, it * self.f[who] + (n[who] - 4 + b + 1)


def phases():
    out, before, former = {}, (0, 0, 0, 0, 0, {"A": 0, "V": 0}), None
    for name, n, body, panels in PHASES:
        out[name] = Phase(name, n, body, panels, before)
        out[name].former = former
        before, former = out[name].after(), panels[-1][2]
    return out


PH = phases()
KINDS = "".join(body * n for _, n, body, _ in PHASES)


def reuse_needs(ph, its, local):
    split, sums = [], []
    for it in its:
        before = KINDS[:max(0, ph.r0 + it * len(ph.body) + local - 3)]
        split.append(before.count("s") - it * ph.ns)
        sums.append(before.count("a") - it * ph.na)
    former = {KINDS[max(0, ph.r0 + it * len(ph.body) + local - 4)] for it in its}
    return max(split), max(sums), former


def build(nc, vecs, cst, rcnt, masks, xT, w_ada, w_in, pool_w, w_br, w_out, w_f1, w_f2, outT):
    with ExitStack() as ctx:
        KB = 1024
        SIZE = 222 * KB + 512
        arena = ctx.enter_context(nc.sbuf_tensor("arena", [P, SIZE // 4], F32))
        base = (nc.sbuf_base - SIZE) // 32 * 32

        def at(name, shape, off, dt=F32):
            return nc.alloc_sbuf_tensor_at(name, shape, dt, offset=base + int(off))

        raw = at("raw", [P, 4, CK, PW], 0)
        whi = at("whi", [P, 2, CK, PW], 32 * KB, F32R)
        wlo = at("wlo", [P, 2, CK, PW], 48 * KB, F32R)
        hL = at("hL", [P, KT, 2, T], 64 * KB, F32R)
        acc = at("acc", [P, KT, T], 64 * KB)
        hC = at("hC", [P, KT, 2, C], 96 * KB, F32R)
        mk_in = at("mk_in", [P, 7, P], 96 * KB)
        q_t = at("q_t", [P, HEADS, T], 96 * KB)
        ya = at("ya", [P, HEADS, T], 104 * KB)
        cq = at("cq", [P, HEADS, T], 112 * KB)
        xb = at("xb", [P, HEADS, T], 120 * KB)
        pw_sb = at("pw_sb", [P, 8, 256], 96 * KB)
        rc_sb = at("rc_sb", [P, 4, T], 104 * KB)
        ax = at("ax", [P, KT, T], 96 * KB)
        res = at("res", [P, KT, T], 112 * KB)
        xin = at("xin", [P, KT, 2, T], 128 * KB)
        kk = at("kk", [P, 2 * HEADS, T], 128 * KB)
        lf = at("lf", [P, 2 * HEADS, T], 144 * KB)
        mT = at("mT", [P, KT, T], 128 * KB)
        yR = [at("yR0", [P, HEADS, 2, T], 144 * KB, F32R), at("yR1", [P, HEADS, 2, T], 168 * KB, F32R)]
        h2 = at("h2", [P, KT, 2, T], 128 * KB, F32R)
        vl = at("vl", [P, 2, HEADS * HD], 160 * KB)
        vc = at("vc", [P, 2, HEADS * HD], 168 * KB)
        lv = [at("lv0", [P, 2, 4, T], 168 * KB), at("lv1", [P, 2, 4, T], 200 * KB)]
        st = at("st", [P, 2 * HEADS, HD], 176 * KB)
        sR = at("sR", [P, KT, P], 176 * KB, F32R)
        ak = at("ak", [P, 2, C + T], 184 * KB)
        av = at("av", [P, 4, 256], 188 * KB)
        mR = at("mR", [P, KT, 2, T], 160 * KB, F32R)
        hid = at("hid", [P, KT, 2, T], 160 * KB, F32R)
        am = at("am", [P, 2, PW], 192 * KB)
        ht = at("ht", [P, 2, 2, T], 196 * KB)
        zL = at("zL", [P, C + T], 192 * KB)
        zm = at("zm", [P, C + T], 194 * KB)
        zf = at("zf", [P, C + T], 196 * KB)
        kc = at("kc", [P, 4, C], 198 * KB)
        kcT = at("kcT", [P, 4 * C], 202 * KB)
        pT = at("pT", [P, 2, 4, T], 192 * KB)
        qr = at("qr", [P, 4, T], 192 * KB)
        qs = at("qs", [P, 4, T], 196 * KB)
        pr = at("pr", [P, 2, C + T], 196 * KB)
        prT = at("prT", [P, 2, 4, T], 200 * KB)
        ks = at("ks", [P, 2, T], 200 * KB)
        gz = at("gz", [P, 2, T], 192 * KB)
        pin = at("pin", [P, 2, 272], 192 * KB)
        win = [at("win0", [P, 2, 272], 192 * KB + 2304), at("win1", [P, 2, 272], 192 * KB + 4608)]
        pd = at("pd", [P, HEADS, T], 200 * KB)
        sqb = at("sqb", [P, KT, T], 192 * KB)
        x_t = at("x_t", [P, 2, T], 204 * KB)
        h_t = at("h_t", [P, 2, T], 206 * KB)
        vg = at("vg", [P, 2, PW], 208 * KB)
        sg_st = at("sg_st", [P, 2, PW], 212 * KB)
        avg = at("avg", [P, 4, HD], 208 * KB)
        asum = at("asum", [P, PW], 210 * KB)
        sg = at("sg", [P, 4, T], 212 * KB)
        mu = at("mu", [P, T], 208 * KB)
        rstd = at("rstd", [P, T], 209 * KB)
        cs = at("cs", [P, NK], 216 * KB)
        vv = at("vv", [P, NV], 216 * KB + 3616)
        mk = at("mk", [P, 7, P], 216 * KB + 4480, U8)
        sm = at("sm", [P, 2, KT], 216 * KB + 5376)
        mods1 = at("mods1", [P, 2 * KT, 2], 216 * KB + 5504)
        mods2 = at("mods2", [P, 4 * KT], 216 * KB + 5760)
        col = at("col", [P, 2, 8], 216 * KB + 6080)
        ones = at("ones", [P, P], 222 * KB)

        main = ctx.enter_context(nc.psum_tensor("main", [P, 4, 512], F32))
        side = ctx.enter_context(nc.psum_tensor("side", [P, 4, 512], F32))
        ADA_PS = 448

        def sem(name):
            return ctx.enter_context(nc.semaphore(name))

        raw_full = [sem(f"raw_full{i}") for i in range(4)]
        hi_made, lo_made, ada_used = sem("hi_made"), sem("lo_made"), sem("ada_used")
        released = {"w_used": sem("w_used"), "blk_done": sem("blk_done")}
        w_used, blk_done = released["w_used"], released["blk_done"]
        freed = {"A": sem("freed_by_act"), "V": sem("freed_by_dve")}
        (cst_in, x_in, pool_ld, ax_ld, stored, silu_sig, silu_in, silu_hi, silu_lo, mods_ps, h_tmp, h_hi, h_lo,
         am_used, z_log, z_arg, key_in, key_tr, key_cp, st_ps, st_cp, asum_done, asum_ps, lv_arg, lv_exp,
         lv_op, lv_sc, lv_cp, vg_in, o_exp, o_op, o_ps, o_sq, o_ms, o_rs, y_done, gs_sig, at_sw, at_rot, at_v,
         at_sc, at_max, at_exp, at_norm, at_tr, at_cp, at_o, at_y, y_hi, y_lo, sg_in, pool_diff, pool_ps,
         pool_y, m_done, m_hi, m_lo, ax_in, mean_ps, mu_in, cen_done, sq_done, var_ps, rstd_in, h2_tmp, h2_hi,
         h2_lo, hid_sq, hid_hi, hid_lo, passed, res_done, y_out, cleared) = (sem(x) for x in (
            "cst_in x_in pool_ld ax_ld stored silu_sig silu_in silu_hi silu_lo mods_ps h_tmp h_hi h_lo "
            "am_used z_log z_arg key_in key_tr key_cp st_ps st_cp asum_done asum_ps lv_arg lv_exp "
            "lv_op lv_sc lv_cp vg_in o_exp o_op o_ps o_sq o_ms o_rs y_done gs_sig at_sw at_rot at_v "
            "at_sc at_max at_exp at_norm at_tr at_cp at_o at_y y_hi y_lo sg_in pool_diff pool_ps "
            "pool_y m_done m_hi m_lo ax_in mean_ps mu_in cen_done sq_done var_ps rstd_in h2_tmp h2_hi "
            "h2_lo hid_sq hid_hi hid_lo passed res_done y_out cleared").split())

        def wait(eng, semaphore, value):
            eng.wait_ge(semaphore, value)
            if not isinstance(value, int):
                eng.sem_inc(passed, 1)

        def head_blocks(t, g, h):
            return t[:, bass.ts(g, 4)].rearrange("p e (n a h) -> p (e n) a h", a=2, h=h)

        def level_blocks(t, h):
            return t.rearrange("p e (n a h) -> p (e n) a h", a=2, h=h)

        def keys_of(unit):
            return slice(384, 512) if unit % 2 == 0 else slice(256, 384)

        block = ctx.enter_context(nc.Block())

        @block.sync
        def _(sp):
            def load(name, it, local, src, its=None):
                ph = PH[name]
                split, sums, former = reuse_needs(ph, its or (it,), local)
                slot, _ = ph.raw(0, local)
                first = its[0] if its else it
                if "s" in former and first * ph.ns + split > 0:
                    wait(sp, lo_made, it * ph.ns + split)
                if "a" in former:
                    wait(sp, ada_used, it * ph.na + sums)
                sp.dma_start(raw[:, slot].rearrange("p a b -> p (a b)"), src).then_inc(raw_full[slot], 16)

            for n in range(32):
                load("ada", 0, n, w_ada[n])
            for n, panel in enumerate((PAN_AI, PAN_AI + 1, PAN_CKV)):
                for k in range(4):
                    load("vals", 0, 4 * n + k, w_in[4 * panel + k])

            def forget(i, its):
                for k in range(4):
                    load("forget", i, 2 * k, w_in[i * 4 + (4 * PAN_AF + k)], its)
                    load("forget", i, 2 * k + 1, w_ada[i * 4 + (32 + k)], its)

            forget(0, None)
            with sp.Fori(1, 4) as i:
                forget(i, (1, 2, 3))
            for n in range(8):
                load("query", 0, n, w_in[4 * PAN_AQ + n])
            with sp.Fori(0, 2) as i:
                for n, panel in enumerate((PAN_AG, PAN_CQ, PAN_B)):
                    for k in range(4):
                        load("mix", i, 4 * n + k, w_in[i * 4 + (4 * panel + k)], (0, 1))
            for j, branch in enumerate(BRANCHES):
                its = (2 * j, 2 * j + 1)
                with sp.Fori(0, 2) as h:
                    for p in range(2):
                        for k in range(4):
                            load("gates", h + 2 * j, 10 * p + 2 * k,
                                 w_in[h * 8 + (4 * (PAN_GATE + 4 * branch + p) + k)], its)
                            load("gates", h + 2 * j, 10 * p + 2 * k + 1, w_ada[h * 8 + (48 + 16 * j + 4 * p + k)],
                                 its)
                        for k in range(2):
                            load("gates", h + 2 * j, 10 * p + 8 + k, w_br[h * 4 + (8 * branch + 2 * p + k)], its)
            with sp.Fori(0, 4) as i:
                for k in range(4):
                    load("out", i, k, w_out[i * 4 + k], range(4))
            with sp.Fori(0, 4) as f:
                for half, w in enumerate((w_f1, w_f2)):
                    with sp.Fori(0, 4) as i:
                        for k in range(4):
                            load("mlp", f * 8 + i + 4 * half, k, w[f * 16 + i * 4 + k], range(32))

        @block.scalar
        def _(act):
            A = nc.scalar.activation
            drain = nc.scalar.drain

            def split(name, it, s):
                ph = PH[name]
                slot, full = ph.raw(it, ph.at[s])
                wait(act, raw_full[slot], full)
                if name != "ada" or s >= 2:
                    which, count = ph.released(it, s)
                    wait(act, released[which], count)
                nc.scalar.copy(whi[:, ph.parity(s)], raw[:, slot]).then_inc(hi_made, 1)

            def blk(name, it, panel, b):
                wait(act, blk_done, PH[name].blocks_before(it, panel) + (b + 1))

            act.dma_start(vv[:], vecs).then_inc(cst_in, 16)
            act.dma_start(cs[:], cst).then_inc(cst_in, 16)
            act.dma_start(mk_in[:].rearrange("p a b -> p (a b)"), masks).then_inc(cst_in, 16)
            act.dma_start(xin[:].rearrange("p k v t -> p (k v t)"), xT).then_inc(x_in, 16)
            wait(act, cst_in, 48)
            A(sm[:].rearrange("p v k -> p (v k)"), vv[:, V_C:V_C + 2 * KT], ACT.Sigmoid).then_inc(silu_sig, 1)
            wait(act, silu_in, 1)
            nc.scalar.copy(sR[:, :, 0:2], sm[:].rearrange("p v k -> p k v")).then_inc(silu_hi, 1)

            split("ada", 0, 0)
            for t in range(8):
                for k in range(4):
                    split("ada", 0, 4 * t + k + 1)
                blk("ada", 0, t, 0)
                if t >= 2:
                    wait(act, am_used, t - 1)
                nc.scalar.copy(am[0:4, t % 2], main[0:4, t % 4]).then_inc(freed["A"], 1)

            for t in range(3):
                for k in range(4):
                    split("vals", 0, 4 * t + k + 1)
                    if t == 0 and k == 0:
                        for kt in range(KT):
                            wait(act, h_tmp, kt + 1)
                            nc.scalar.copy(hC[:, kt, 0], ht[:, kt % 2, 0])
                            nc.scalar.copy(hL[:, kt, 0], ht[:, kt % 2, 1]).then_inc(h_hi, 1)
                for b in range(4):
                    blk("vals", 0, t, b)
                    if t < 2:
                        dst = (vc, vl)[b // 2][:, b % 2, PW * t:PW * (t + 1)]
                    elif b < 2:
                        dst = ak[:, b]
                    else:
                        dst = av[:, 2 * (b - 2):2 * (b - 1)].rearrange("p a n -> p (a n)")
                    nc.scalar.copy(dst, main[:, b]).then_inc(freed["A"], 1)

            def key_copy(it):
                wait(act, key_tr, it + 1)
                nc.scalar.copy(kcT[:], side[:, 0:2].rearrange("p a b -> p (a b)")).then_inc(key_cp, 1)

            def state_copy(it):
                wait(act, st_ps, it + 1)
                nc.scalar.copy(st[:, bass.ts(it, 4)].rearrange("p a b -> p (a b)"), side[:, 2]).then_inc(st_cp, 1)

            def forget(it, former):
                for k in range(4):
                    split("forget", it, k + 1)
                    if former is not None and k == 2:
                        key_copy(former)
                    if former is not None and k == 3:
                        state_copy(former)
                for b in range(4):
                    drain()
                    blk("forget", it, 0, b)
                    z = main[:, b]
                    A(zL[:], z, ACT.Abs)
                    drain()
                    A(zL[:], zL[:], ACT.Exp, scale=-1.0)
                    drain()
                    A(zL[:], zL[:], ACT.Ln, bias=1.0).then_inc(z_log, 1)
                    wait(act, z_arg, it * 4 + (b + 1))
                    A(kk[:, it * 4 + b], zm[:, C:], ACT.Exp, scale=-1.0)
                    A(kc[:, b], zL[:, 0:C], ACT.Exp).then_inc(key_in, 1)

            forget(0, None)
            with act.Fori(1, 4) as i:
                forget(i, i - 1)

            for t in range(2):
                for k in range(4):
                    split("query", 0, 4 * t + k + 1)
                    if t == 0 and k == 2:
                        key_copy(3)
                    if t == 0 and k == 3:
                        state_copy(3)
                for b in range(4 if t == 0 else 0):
                    blk("query", 0, t, b)
                    nc.scalar.copy(q_t[:, b], main[:, b, 0:T]).then_inc(freed["A"], 1)

            with act.Fori(0, 2) as i:
                for k in range(12):
                    split("mix", i, k + 1)
                    if k < 8:
                        wait(act, lv_arg, i * 8 + (k + 1))
                        t = lv[k % 2][:].rearrange("p a e t -> p (a e t)")
                        A(t, t, ACT.Exp).then_inc(lv_exp, 1)
                    if k == 10:
                        wait(act, lv_sc, i * 9 + 9)
                        A(lv[0][:, 0], lf[:, bass.ts(i, 4)], ACT.Exp)
                        A(lv[0][:, 1], lf[:, bass.ts(i + 2, 4)], ACT.Exp).then_inc(o_exp, 1)
                    if k == 11:
                        wait(act, o_ps, i + 1)
                        A(lv[1][:, 0].rearrange("p e t -> p (e t)"), side[:, 2:4].rearrange("p a b -> p (a b)"),
                          ACT.Square).then_inc(o_sq, 1)
                    if k % 4 == 3 and k < 8:
                        for b in range(4):
                            blk("mix", i, k // 4, b)
                            if k == 3:
                                A(ya[:, i * 4 + b], main[:, b, 0:T], ACT.Sigmoid).then_inc(gs_sig, 1)
                            else:
                                nc.scalar.copy(cq[:, i * 4 + b], main[:, b, 0:T]).then_inc(freed["A"], 1)
                wait(act, o_ms, i + 1)
                A(lv[1][:, 1].rearrange("p e t -> p (e t)"), side[:, 0:2].rearrange("p a b -> p (a b)"),
                  ACT.Ln, scale=1.0 / HD, bias=RMS_EPS)
                drain()
                A(lv[1][:, 1], lv[1][:, 1], ACT.Exp, scale=-0.5).then_inc(o_rs, 1)

            def y_parts(src, j):
                nc.scalar.copy(yR[j % 2][:, :, 0], src[:]).then_inc(y_hi, 1)

            def gates(j, h, between):
                it = h + 2 * j
                for k in range(12):
                    split("gates", it, k + 1)
                    between(k)
                    if k in (3, 9):
                        p = k // 6
                        for b in range(4):
                            blk("gates", it, 2 * p, b)
                            A(sg[:, b], main[:, b, 0:T], ACT.Sigmoid).then_inc(freed["A"], 1)

            wait(act, y_done, 2)
            y_parts(ya, 0)
            wait(act, y_lo, 1)
            act.dma_start(pw_sb[:], pool_w).then_inc(pool_ld, 16)
            act.dma_start(rc_sb[:], rcnt).then_inc(pool_ld, 16)
            with act.Fori(0, 2) as h:
                def attend(k):
                    if k == 0:
                        g4 = cq[:, bass.ts(h, 4)]
                        nc.scalar.copy(qs[0:64], g4[64:128])
                        nc.scalar.copy(qs[64:128], g4[0:64])
                        nc.scalar.copy(ks[0:64, 0], ak[64:128, h, C:])
                        nc.scalar.copy(ks[64:128, 0], ak[0:64, h, C:]).then_inc(at_sw, 1)
                    if 5 <= k <= 11 and k % 2 == 1:
                        e = (k - 5) // 2
                        wait(act, at_o, h * 4 + (e + 1))
                        nc.scalar.copy(cq[:, h * 4 + e], side[:, 3, 0:T]).then_inc(at_y, 1)
                    u = k - 3
                    if 0 <= u < 8:
                        wait(act, at_tr, h * 8 + (u + 1))
                        nc.scalar.copy(prT[:, (u // 2) % 2, :, (u % 2) * P:(u % 2 + 1) * P],
                                       side[:, 2].rearrange("p (a b) -> p a b", a=4)).then_inc(at_cp, 1)
                    u = k - 2
                    if 0 <= u < 8:
                        wait(act, at_max, h * 8 + (u + 1))
                        c = col[:, u % 2]
                        A(pr[:, u % 2], side[:, u % 2], ACT.Exp, bias=c[:, 2:3], scale=SCALE,
                          accum_out=c[:, 3:4])
                        sink = h * 4 + (V_SINK + u // 2)
                        A(c[:, 4:5], vv[:, bass.ds(sink, 1)], ACT.Exp, bias=c[:, 2:3]).then_inc(at_exp, 1)
                gates(0, h, attend)
            drain()
            y_parts(cq, 1)
            with act.Fori(0, 2) as h:
                gates(1, h, lambda k: None)
            for b in range(8):
                wait(act, pool_ps, b // 2 * 2 + 2 if b < 6 else b + 1)
                A(xb[:, b], side[:, (b % 7) // 2, (b % 7) % 2 * T:(b % 7) % 2 * T + T], ACT.Identity,
                  scale=vv[:, V_PSC + b:V_PSC + b + 1]).then_inc(pool_y, 1)
            act.dma_start(ax[:], xT.rearrange("p (k v t) -> p k v t", v=2, t=T)[:, :, 1]).then_inc(ax_ld, 16)
            drain()
            y_parts(xb, 2)
            with act.Fori(0, 2) as h:
                gates(2, h, lambda k: None)

            for n in range(4):
                if n == 0:
                    wait(act, m_done, 1)
                nc.scalar.copy(mR[:, 4 * n:4 * n + 4, 0], mT[:, 4 * n:4 * n + 4]).then_inc(m_hi, 1)
            wait(act, ax_ld, 16)
            nc.scalar.mul(ax[:], ax[:], ALPHA).then_inc(ax_in, 1)
            with act.Fori(0, 4) as i:
                for k in range(4):
                    split("out", i, k + 1)

            def norm(n):
                wait(act, mean_ps, n + 1)
                A(mu[:], side[:, 0, 0:T], ACT.Copy, scale=1.0 / D).then_inc(mu_in, 1)
                for q in range(4):
                    wait(act, cen_done, 4 * n + q + 1)
                    A(sqb[:, 4 * q:4 * q + 4], res[:, 4 * q:4 * q + 4], ACT.Square).then_inc(sq_done, 1)
                wait(act, var_ps, n + 1)
                A(rstd[:], side[:, 1, 0:T], ACT.Ln, scale=1.0 / D, bias=LN_EPS)
                drain()
                A(rstd[:], rstd[:], ACT.Exp, scale=-0.5).then_inc(rstd_in, 1)

            norm(0)
            for k in range(KT):
                wait(act, h2_tmp, k + 1)
                nc.scalar.mul(ax[:, k], x_t[:, k % 2], ALPHA)
                nc.scalar.copy(h2[:, k, 0], h_t[:, k % 2]).then_inc(h2_hi, 1)

            def mlp(f, last):
                with act.Fori(0, 4) as i:
                    for k in range(4):
                        split("mlp", f * 8 + i, k + 1)
                    for b in range(4):
                        wait(act, hid_sq, f * 16 + i * 4 + (b + 1))
                        nc.scalar.copy(hid[:, i * 4 + b, 0], sqb[:, b]).then_inc(hid_hi, 1)
                with act.Fori(0, 3) as i:
                    for k in range(4):
                        split("mlp", f * 8 + i + 4, k + 1)
                for k in range(3 if last else 4):
                    split("mlp", f * 8 + 7, k + 1)

            with act.Fori(0, 3) as f:
                mlp(f, False)
            mlp(3, True)
            norm(1)
            wait(act, y_out, 4)
            for q in range(4):
                act.dma_start(outT[:, 4 * q:4 * q + 4], acc[:, 4 * q:4 * q + 4]).then_inc(stored, 16)
            wait(act, stored, 64)

        @block.gpsimd
        def _(pool):
            pool.wait_ge(cst_in, 48)
            nc.gpsimd.tensor_copy(mk[:], mk_in[:])
            nc.gpsimd.memset(sR[:].rearrange("p k n -> p (k n)").bitcast(F32), 0.0).then_inc(cleared, 1)
            with pool.Fori(0, 2) as i:
                wait(pool, lv_sc, i * 9 + 1)
                nc.gpsimd.tensor_copy(vg[:], vl[:, :, bass.ts(i, PW)])
                nc.gpsimd.tensor_copy(sg_st[:, 0], st[:, bass.ts(i, 4)].rearrange("p e d -> p (e d)"))
                nc.gpsimd.tensor_copy(sg_st[:, 1],
                                      st[:, bass.ts(i + 2, 4)].rearrange("p e d -> p (e d)")).then_inc(vg_in, 1)
            with pool.Fori(0, 2) as h:
                wait(pool, at_sw, h + 1)
                nc.gpsimd.tensor_copy(avg[:], av[:, :, bass.ts(h, HD)]).then_inc(at_v, 1)

        @block.vector
        def _(dve):
            TT, TS, STT = nc.vector.tensor_tensor, nc.vector.tensor_scalar, nc.vector.scalar_tensor_tensor
            drain = nc.vector.drain

            def split(name, it, s):
                ph = PH[name]
                dve.wait_ge(hi_made, ph.split_count(it, s))
                slot, par = ph.raw(0, ph.at[s])[0], ph.parity(s)
                TT(wlo[:, par], raw[:, slot], whi[:, par].bitcast(F32), ALU.subtract).then_inc(lo_made, 1)

            def blk(name, it, panel, b):
                dve.wait_ge(blk_done, PH[name].blocks_before(it, panel) + (b + 1))

            def ada_sum(name, it, local, n, k):
                slot, full = PH[name].raw(it, local)
                wait(dve, raw_full[slot], full)
                if k == 0:
                    dve.wait_ge(asum_ps, n + 1)
                for j in range(CK):
                    s = sm[:, 0, k * CK + j:k * CK + j + 1]
                    if k == 0 and j == 0:
                        last = TS(asum[:], raw[:, slot, j], s, None, ALU.mult)
                    else:
                        drain()
                        last = STT(asum[:], raw[:, slot, j], s, asum[:], ALU.mult, ALU.add)
                last.then_inc(ada_used, 1)

            nc.vector.memset(ones[:], 1.0)
            dve.wait_ge(silu_sig, 1)
            dve.wait_ge(cleared, 1)
            TT(sm[:].rearrange("p v k -> p (v k)"), sm[:].rearrange("p v k -> p (v k)"), vv[:, V_C:V_C + 2 * KT],
               ALU.mult).then_inc(silu_in, 1)
            dve.wait_ge(silu_hi, 1)
            TT(sR[:, :, 2:4], sm[:].rearrange("p v k -> p k v"), sR[:, :, 0:2].bitcast(F32),
               ALU.subtract).then_inc(silu_lo, 1)
            for s in range(33):
                split("ada", 0, s)

            def modulate():
                dve.wait_ge(mods_ps, 1)
                TT(mods1[:], side[:, 0, 0:64].rearrange("p (c v) -> p c v", v=2),
                   vv[:, V_BADA:V_BADA + 32].unsqueeze(2).to_broadcast([P, 32, 2]), ALU.add)
                drain()
                TS(mods1[:, KT:], mods1[:, KT:], 1.0, None, ALU.add)
                drain()
                dve.wait_ge(x_in, 16)

                def lo(k):
                    dve.wait_ge(h_hi, k + 1)
                    TT(hC[:, k, 1], ht[:, k % 2, 0], hC[:, k, 0].bitcast(F32), ALU.subtract)
                    TT(hL[:, k, 1], ht[:, k % 2, 1], hL[:, k, 0].bitcast(F32), ALU.subtract).then_inc(h_lo, 1)

                for k in range(KT):
                    if k >= 2:
                        drain()
                    TS(ht[:, k % 2, 0], xin[:, k, 0], mods1[:, KT + k, 1:2], mods1[:, k, 1:2], ALU.mult, ALU.add)
                    TS(ht[:, k % 2, 1], xin[:, k, 1], mods1[:, KT + k, 0:1], mods1[:, k, 0:1],
                       ALU.mult, ALU.add).then_inc(h_tmp, 1)
                    if k:
                        lo(k - 1)
                lo(KT - 1)

            for s in range(1, 13):
                split("vals", 0, s)
                if s == 1:
                    modulate()

            def forget(it, backward):
                for k in range(4):
                    split("forget", it, k + 1)
                    ada_sum("forget", it, 2 * k + 1, it, k)
                for b in range(4):
                    drain()
                    dve.wait_ge(z_log, it * 4 + (b + 1))
                    STT(zm[:], main[:, b], 0.0, zL[:], ALU.max, ALU.add)
                    STT(zf[:], main[:, b], 0.0, zL[:], ALU.min, ALU.subtract).then_inc(freed["V"], 1)
                    drain()
                    one = ones[:, 0:1].to_broadcast([P, C])
                    dst, lat, ctx_f = lf[:, it * 4 + b], zf[:, C:], zf[:, 0:C]
                    if backward:
                        back = h_t[:, 0]
                        nc.vector.tensor_tensor_scan(back[:, ::-1], one, lat[:, ::-1], 0.0, ALU.mult, ALU.add)
                        nc.vector.memset(zL[:, 0:1], 0.0)
                        nc.vector.tensor_tensor_scan(zL[:, 1:C], one[:, 1:], ctx_f[:, 0:C - 1], 0.0,
                                                     ALU.mult, ALU.add)
                    else:
                        nc.vector.tensor_tensor_scan(dst, one, lat, 0.0, ALU.mult, ALU.add)
                        nc.vector.memset(zL[:, C - 1:C], 0.0)
                        nc.vector.tensor_tensor_scan(zL[:, 0:C - 1][:, ::-1], one[:, 1:], ctx_f[:, 1:][:, ::-1], 0.0,
                                                     ALU.mult, ALU.add)
                    drain()
                    if backward:
                        nc.vector.tensor_copy(dst, back)
                    TT(zL[:, 0:C], zL[:, 0:C], zm[:, 0:C], ALU.subtract).then_inc(z_arg, 1)

            with dve.Fori(0, 2) as i:
                forget(i, False)
            with dve.Fori(2, 4) as i:
                forget(i, True)

            for s in range(1, 9):
                split("query", 0, s)
            for b in range(4):
                blk("query", 0, 1, b)
                nc.vector.tensor_copy(q_t[:, 4 + b], main[:, b, 0:T]).then_inc(freed["V"], 1)
            dve.wait_ge(asum_ps, 5)
            TT(mods2[:, 0:KT], side[:, 3, ADA_PS:ADA_PS + KT], vv[:, V_BADA + 32:V_BADA + 48], ALU.add)

            def level_args(i, k):
                h = LEVELS[k]
                f, w = head_blocks(lf, i, h), head_blocks(lf, i + 2, h)
                q, key = level_blocks(lv[k % 2][:, 0], h), level_blocks(lv[k % 2][:, 1], h)
                shape = [P, q.shape[1], h]
                f_mid = f[:, :, 0, h - 1:h].to_broadcast(shape)
                w_mid = w[:, :, 1, 0:1].to_broadcast(shape)
                drain()
                TT(q[:, :, 1], f[:, :, 1], f_mid, ALU.subtract)
                TT(q[:, :, 0], w[:, :, 0], w_mid, ALU.subtract)
                TT(key[:, :, 0], f_mid, f[:, :, 0], ALU.subtract)
                TT(key[:, :, 1], w_mid, w[:, :, 1], ALU.subtract).then_inc(lv_arg, 1)

            def level_operands(i, k):
                h = LEVELS[k]
                t = lv[k % 2]
                q4 = q_t[:, bass.ts(i, 4)]
                if h:
                    dve.wait_ge(lv_exp, i * 8 + (k + 1))
                    kf, kb = head_blocks(kk, i, h), head_blocks(kk, i + 2, h)
                    key = level_blocks(t[:, 1], h)
                    TT(t[:, 0], t[:, 0], q4, ALU.mult)
                    TT(key[:, :, 0], key[:, :, 0], kf[:, :, 0], ALU.mult)
                    TT(key[:, :, 1], key[:, :, 1], kb[:, :, 1], ALU.mult).then_inc(lv_op, 1)
                else:
                    drain()
                    nc.vector.tensor_copy(t[:, 0], q4)
                    TT(t[:, 1], kk[:, bass.ts(i, 4)], kk[:, bass.ts(i + 2, 4)], ALU.add).then_inc(lv_op, 1)

            def level_scores(i, k):
                h = LEVELS[k]
                drain()
                wait(dve, lv_sc, i * 9 + (k + 1))
                for tile in range(2):
                    src = side[:, tile].rearrange("p (e t) -> p e t", e=4)
                    cols = 1 - tile if h == 128 else tile
                    dst = pT[:, tile, :, cols * P:(cols + 1) * P]
                    if h >= 64:
                        last = nc.vector.tensor_copy(dst, src)
                    else:
                        last = nc.vector.copy_predicated(dst, mk[:, k - 2:k - 1].to_broadcast([P, 4, P]), src)
                last.then_inc(lv_cp, 1)

            with dve.Fori(0, 2) as i:
                for k in range(12):
                    split("mix", i, k + 1)
                    if 2 <= k < 11:
                        level_scores(i, k - 2)
                    if k < 8:
                        level_args(i, k)
                    if 1 <= k < 10:
                        level_operands(i, k - 1)
                    if k == 10:
                        dve.wait_ge(o_exp, i + 1)
                        q4 = q_t[:, bass.ts(i, 4)]
                        TT(lv[0][:, 0], lv[0][:, 0], q4, ALU.mult)
                        TT(lv[0][:, 1], lv[0][:, 1], q4, ALU.mult).then_inc(o_op, 1)
                    if k == 3:
                        for b in range(4):
                            blk("mix", i, 0, b)
                            dve.wait_ge(gs_sig, i * 4 + (b + 1))
                            TT(ya[:, i * 4 + b], ya[:, i * 4 + b], main[:, b, 0:T],
                               ALU.mult).then_inc(freed["V"], 1)
                    if k == 11:
                        for b in range(4):
                            blk("mix", i, 2, b)
                            dve.sem_inc(passed, 1)
                            nc.vector.tensor_copy(xb[:, i * 4 + b], main[:, b, 0:T]).then_inc(freed["V"], 1)
                wait(dve, o_rs, i + 1)
                t = lv[1][:, 1].rearrange("p e t -> p (e t)")
                TT(t, t, side[:, 2:4].rearrange("p a b -> p (a b)"), ALU.mult)
                drain()
                for e in range(4):
                    last = STT(ya[:, i * 4 + e], lv[1][:, 1, e], vv[:, bass.ds(i * 4 + (V_NORM + e), 1)],
                               ya[:, i * 4 + e], ALU.mult, ALU.mult)
                last.then_inc(y_done, 1)

            def y_rest(src, j):
                dve.wait_ge(y_hi, j + 1)
                TT(yR[j % 2][:, :, 1], src[:], yR[j % 2][:, :, 0].bitcast(F32), ALU.subtract).then_inc(y_lo, 1)

            def gates(j, h, between):
                it = h + 2 * j
                for k in range(12):
                    split("gates", it, k + 1)
                    p, q = k // 6, k % 6
                    if q < 4:
                        ada_sum("gates", it, 10 * p + 2 * q + 1, h * 2 + (4 + 4 * j + p), q)
                    between(k)
                    if q == 5:
                        for b in range(4):
                            blk("gates", it, 2 * p + 1, b)
                            dst = mT[:, h * 8 + (4 * p + b)]
                            if j == 0:
                                dve.wait_ge(freed["A"], it * 8 + (PH["gates"].f0["A"] + 4 * p + b + 1))
                                TT(dst, sg[:, b], main[:, b, 0:T], ALU.mult).then_inc(freed["V"], 1)
                            else:
                                dve.sem_inc(passed, 1)
                                drain()
                                dve.wait_ge(freed["A"], it * 8 + (PH["gates"].f0["A"] + 4 * p + b + 1))
                                TT(gz[:, b % 2], sg[:, b], main[:, b, 0:T], ALU.mult).then_inc(freed["V"], 1)
                                drain()
                                TT(dst, dst, gz[:, b % 2], ALU.add)

            drain()
            y_rest(ya, 0)
            with dve.Fori(0, 2) as h:
                def attend(k):
                    if k == 0:
                        g4 = cq[:, bass.ts(h, 4)]
                        cos, sin = cs[:, K_COS:K_COS + T], cs[:, K_SIN:K_SIN + T]
                        cos4 = cos.unsqueeze(1).to_broadcast([P, 4, T])
                        sin4 = sin.unsqueeze(1).to_broadcast([P, 4, T])
                        TT(qr[:], g4, cos4, ALU.mult)
                        dve.wait_ge(at_sw, h + 1)
                        TT(qs[:], qs[:], sin4, ALU.mult)
                        TT(ks[:, 1], ak[:, h, C:], cos, ALU.mult)
                        TT(ks[:, 0], ks[:, 0], sin, ALU.mult)
                        drain()
                        TT(qr[:], qr[:], qs[:], ALU.add)
                        TT(ak[:, h, C:], ks[:, 0], ks[:, 1], ALU.add).then_inc(at_rot, 1)
                    u = k - 2
                    if 0 <= u < 8:
                        c, s = col[:, u % 2], side[:, u % 2]
                        drain()
                        dve.wait_ge(at_sc, h * 8 + (u + 1))
                        TT(s[:, keys_of(u)], s[:, keys_of(u)],
                           cs[:, K_TRI + P * (u % 2):K_TRI + P * (u % 2 + 1)], ALU.add)
                        drain()
                        nc.vector.reduce_max(c[:, 0:1], s, AX)
                        drain()
                        TS(c[:, 1:2], c[:, 0:1], SCALE, vv[:, bass.ds(h * 4 + (V_SINK + u // 2), 1)],
                           ALU.mult, ALU.max)
                        drain()
                        TS(c[:, 2:3], c[:, 1:2], -1.0, None, ALU.mult).then_inc(at_max, 1)
                        dve.wait_ge(at_exp, h * 8 + (u + 1))
                        TT(c[:, 5:6], c[:, 3:4], c[:, 4:5], ALU.add)
                        drain()
                        nc.vector.reciprocal(c[:, 6:7], c[:, 5:6])
                        drain()
                        TS(pr[:, u % 2], pr[:, u % 2], c[:, 6:7], None, ALU.mult).then_inc(at_norm, 1)
                gates(0, h, attend)
            y_rest(cq, 1)

            dve.wait_ge(pool_ld, 32)
            drain()
            nc.vector.memset(pin[:], 0.0)
            for n in range(4):
                x2 = xb[:, 2 * n:2 * n + 2]
                drain()
                nc.vector.tensor_copy(pin[:, :, 8:8 + T], x2)
                src, lo, hi = pin, 0, 272
                for step in range(n + 1):
                    left = right = 1 << max(step - 1, 0)
                    if step == 0:
                        left, right = 1, 0
                    lo, hi = lo + left, hi - right
                    drain()
                    TT(win[step % 2][:, :, lo:hi], src[:, :, lo - left:hi - left], src[:, :, lo + right:hi + right],
                       ALU.add)
                    src = win[step % 2]
                drain()
                d2 = pd[:, 2 * n:2 * n + 2]
                TT(d2, src[:, :, 8:8 + T], rc_sb[:, n:n + 1].to_broadcast([P, 2, T]), ALU.mult)
                drain()
                last = TT(d2, d2, x2, ALU.subtract)
            last.then_inc(pool_diff, 1)
            with dve.Fori(0, 2) as h:
                gates(1, h, lambda k: None)
            dve.wait_ge(pool_y, 8)
            y_rest(xb, 2)
            with dve.Fori(0, 2) as h:
                gates(2, h, lambda k: None)

            dve.wait_ge(asum_ps, 17)
            drain()
            TT(mods2[:, KT:], side[:, 3, ADA_PS + KT:ADA_PS + 4 * KT], vv[:, V_BADA + 48:V_BADA + 96], ALU.add)
            drain()
            TS(mods2[:, 2 * KT:3 * KT], mods2[:, 2 * KT:3 * KT], 1.0, None, ALU.add)
            nc.vector.memset(mu[:], 0.0).then_inc(m_done, 1)
            for n in range(4):
                dve.wait_ge(m_hi, n + 1)
                TT(mR[:, 4 * n:4 * n + 4, 1], mT[:, 4 * n:4 * n + 4], mR[:, 4 * n:4 * n + 4, 0].bitcast(F32),
                   ALU.subtract).then_inc(m_lo, 1)
            dve.wait_ge(ax_in, 1)
            with dve.Fori(0, 4) as i:
                for k in range(4):
                    split("out", i, k + 1)
                for b in range(4):
                    blk("out", i, 0, b)
                    n = i * 4 + b
                    STT(res[:, n], main[:, b, 0:T], mods2[:, bass.ds(n, 1)], ax[:, n],
                        ALU.mult, ALU.add).then_inc(freed["V"], 1)

            def norm(n, gain, shift, then):
                dve.wait_ge(mu_in, n + 1)
                for q in range(4):
                    r4 = res[:, 4 * q:4 * q + 4]
                    TT(r4, r4, mu[:].unsqueeze(1).to_broadcast([P, 4, T]), ALU.subtract).then_inc(cen_done, 1)
                dve.wait_ge(rstd_in, n + 1)
                for q in range(4):
                    r4 = res[:, 4 * q:4 * q + 4]
                    drain()
                    TT(r4, r4, rstd[:].unsqueeze(1).to_broadcast([P, 4, T]), ALU.mult)
                    drain()
                    for k in range(4 * q, 4 * q + 4):
                        then(k, vv[:, gain + k:gain + k + 1], vv[:, shift + k:shift + k + 1])

            def h2_rest(k):
                dve.wait_ge(h2_hi, k + 1)
                TT(h2[:, k, 1], h_t[:, k % 2], h2[:, k, 0].bitcast(F32), ALU.subtract).then_inc(h2_lo, 1)

            def to_mlp(k, gain, shift):
                if k >= 2:
                    drain()
                TS(x_t[:, k % 2], res[:, k], gain, shift, ALU.mult, ALU.add)
                drain()
                TS(h_t[:, k % 2], x_t[:, k % 2], mods2[:, 2 * KT + k:2 * KT + k + 1], mods2[:, KT + k:KT + k + 1],
                   ALU.mult, ALU.add).then_inc(h2_tmp, 1)
                if k:
                    h2_rest(k - 1)

            norm(0, V_L1G, V_L1B, to_mlp)
            h2_rest(KT - 1)
            drain()
            nc.vector.memset(acc[:], 0.0)

            def mlp(f, last):
                with dve.Fori(0, 4) as i:
                    for k in range(4):
                        split("mlp", f * 8 + i, k + 1)
                    for b in range(4):
                        drain()
                        blk("mlp", f * 8 + i, 0, b)
                        nc.vector.tensor_scalar_max(sqb[:, b], main[:, b, 0:T], 0.0).then_inc(freed["V"], 1)
                        drain()
                        TT(sqb[:, b], sqb[:, b], sqb[:, b], ALU.mult).then_inc(hid_sq, 1)
                        if b:
                            hid_rest(f, i, b - 1)
                    hid_rest(f, i, 3)

                def second(i, n):
                    for k in range(n):
                        split("mlp", f * 8 + i + 4, k + 1)
                    for b in range(4):
                        dst = acc[:, i * 4 + b]
                        drain()
                        blk("mlp", f * 8 + i + 4, 0, b)
                        TT(dst, dst, main[:, b, 0:T], ALU.add).then_inc(freed["V"], 1)

                with dve.Fori(0, 3) as i:
                    second(i, 4)
                second(3, 3 if last else 4)

            def hid_rest(f, i, b):
                dve.wait_ge(hid_hi, f * 16 + i * 4 + (b + 1))
                TT(hid[:, i * 4 + b, 1], sqb[:, b], hid[:, i * 4 + b, 0].bitcast(F32),
                   ALU.subtract).then_inc(hid_lo, 1)

            with dve.Fori(0, 3) as f:
                mlp(f, False)
            mlp(3, True)

            drain()
            for k in range(KT):
                STT(res[:, k], acc[:, k], mods2[:, 3 * KT + k:3 * KT + k + 1], ax[:, k],
                    ALU.mult, ALU.add).then_inc(res_done, 1)
            drain()

            def to_out(k, gain, shift):
                last = TS(acc[:, k], res[:, k], gain, shift, ALU.mult, ALU.add)
                if k % 4 == 3:
                    last.then_inc(y_out, 1)

            norm(1, V_L2G, V_L2B, to_out)

        @block.tensor
        def _(pe):
            mm = nc.tensor.matmul

            def bank(name, it, panel, b):
                ph = PH[name]
                who, count = ph.bank_free(it, panel, b)
                pe.wait_ge(freed[who], count)

            def weights(name, it, s):
                ph = PH[name]
                pe.wait_ge(lo_made, ph.split_count(it, s))
                return ph.parity(s)

            def three(out, w_hi, w_lo, x_hi, x_lo, start, stop, skip=False):
                mm(out, w_hi, x_hi, start=start, stop=False, skip_group_check=skip)
                mm(out, w_hi, x_lo, start=False, stop=False, skip_group_check=skip)
                return mm(out, w_lo, x_hi, start=False, stop=stop, skip_group_check=skip)

            def panel(name, it, n, first, x, with_ctx=False, ready=None, between=lambda k: None):
                chunks = PH[name].panels[n][0]
                for k in range(chunks):
                    par = weights(name, it, first + k)
                    if ready is not None:
                        ready(k)
                    for b in range(4):
                        if k == 0:
                            bank(name, it, n, b)
                        for j in range(CK):
                            kt = k * CK + j
                            w_hi, w_lo = (w[:, par, j, P * b:P * (b + 1)] for w in (whi, wlo))
                            start, stop = kt == 0, kt == chunks * CK - 1
                            if with_ctx:
                                mm(main[:, b, 0:C], w_hi, hC[:, kt, 0], start=start, stop=False)
                                mm(main[:, b, 0:C], w_hi, hC[:, kt, 1], start=False, stop=False)
                                mm(main[:, b, 0:C], w_lo, hC[:, kt, 0], start=False, stop=stop)
                                last = three(main[:, b, C:], w_hi, w_lo, hL[:, kt, 0], hL[:, kt, 1],
                                             False, stop, skip=True)
                            else:
                                last = three(main[:, b, 0:T], w_hi, w_lo, x[:, kt, 0], x[:, kt, 1], start, stop)
                        if k == chunks - 1:
                            last.then_inc(blk_done, 1)
                    if k < chunks - 1:
                        last.then_inc(w_used, 1)
                    between(k)

            def turn(t):
                pe.wait_ge(freed["A"], t + 1)
                for b in range(4):
                    last = mm(side[:, 0, (4 * t + b) * 2:(4 * t + b) * 2 + 2], am[0:4, t % 2, P * b:P * (b + 1)],
                              cs[0:4, K_SEL:K_SEL + 2], start=True, stop=True)
                return last

            pe.wait_ge(silu_lo, 1)
            for t in range(8):
                for k in range(4):
                    par = weights("ada", 0, 4 * t + k)
                    if k == 0 and t >= 4:
                        bank("ada", 0, t, 0)
                    for j in range(CK):
                        kt = k * CK + j
                        mm(main[:, t % 4], sR[:, kt], whi[:, par, j], start=kt == 0, stop=False)
                        last = mm(main[:, t % 4], sR[:, kt], wlo[:, par, j], start=False, stop=kt == KT - 1)
                    if k < 3:
                        last.then_inc(w_used, 1)
                last.then_inc(blk_done, 1)
                if t:
                    turn(t - 1).then_inc(am_used, 1)
            turn(7).then_inc(mods_ps, 1)

            def inputs_ready(k):
                pe.wait_ge(h_lo, 4 * k + 4)

            for t in range(2):
                for k in range(4):
                    par = weights("vals", 0, 4 * t + k)
                    inputs_ready(k)
                    for b in range(4):
                        if k == 0:
                            bank("vals", 0, t, b)
                        x, tile = (hC, hL)[b // 2], slice(P * (b % 2), P * (b % 2) + P)
                        for j in range(CK):
                            kt = k * CK + j
                            mm(main[:, b], x[:, kt, 0, tile], whi[:, par, j], start=kt == 0, stop=False)
                            mm(main[:, b], x[:, kt, 0, tile], wlo[:, par, j], start=False, stop=False)
                            last = mm(main[:, b], x[:, kt, 1, tile], whi[:, par, j], start=False, stop=kt == KT - 1)
                        if k == 3:
                            last.then_inc(blk_done, 1)
                    if k < 3:
                        last.then_inc(w_used, 1)
            for k in range(4):
                par = weights("vals", 0, 8 + k)
                for b in range(4):
                    if k == 0:
                        bank("vals", 0, 2, b)
                    for j in range(CK):
                        kt = k * CK + j
                        start, stop = kt == 0, kt == KT - 1
                        if b < 2:
                            w_hi, w_lo = (w[:, par, j, P * b:P * (b + 1)] for w in (whi, wlo))
                            three(main[:, b, 0:C], w_hi, w_lo, hC[:, kt, 0], hC[:, kt, 1], start, stop)
                            last = three(main[:, b, C:], w_hi, w_lo, hL[:, kt, 0], hL[:, kt, 1], False, stop, True)
                        else:
                            x = (hC, hL)[b - 2]
                            for tile in range(2):
                                out, cols = main[:, b, 256 * tile:256 * (tile + 1)], slice(P * tile, P * (tile + 1))
                                w_hi, w_lo = whi[:, par, j, 256:512], wlo[:, par, j, 256:512]
                                mm(out, x[:, kt, 0, cols], w_hi, start=start and tile == 0, stop=False,
                                   skip_group_check=tile == 1)
                                mm(out, x[:, kt, 0, cols], w_lo, start=False, stop=False,
                                   skip_group_check=tile == 1)
                                last = mm(out, x[:, kt, 1, cols], w_hi, start=False, stop=stop,
                                          skip_group_check=tile == 1)
                    if k == 3:
                        last.then_inc(blk_done, 1)
                if k < 3:
                    last.then_inc(w_used, 1)

            def ada_turn(n):
                pe.wait_ge(ada_used, n * 4 + 4)
                for b in range(4):
                    last = mm(side[:, 3, bass.ds(n * 4 + (ADA_PS + b), 1)], asum[:, P * b:P * (b + 1)],
                              ones[:, 0:1], start=True, stop=True)
                last.then_inc(asum_ps, 1)

            def keys_and_states(it, k):
                if k == 1:
                    pe.wait_ge(key_in, it * 4 + 4)
                    for n in range(8):
                        last = nc.tensor.transpose(side[:, n // 4, P * (n % 4):P * (n % 4 + 1)],
                                                   kc[:, n // 2, P * (n % 2):P * (n % 2 + 1)], cs[:, K_ID:K_ID + P])
                    last.then_inc(key_tr, 1)
                    ada_turn(it)
                if k == 2:
                    pe.wait_ge(key_cp, it + 1)
                    for b in range(4):
                        head = HEADS_OF(it, b)
                        for tile in range(2):
                            last = mm(side[:, 2, HD * b:HD * (b + 1)], kcT[:, C * b + P * tile:C * b + P * (tile + 1)],
                                      vc[:, tile, head], start=tile == 0, stop=tile == 1)
                    last.then_inc(st_ps, 1)

            def HEADS_OF(it, b):
                return bass.ds((it % 2) * PW + HD * b, HD)

            mm(side[0:1, 3, 511:512], ones[:, 0:1], ones[:, 0:1], start=True, stop=True).then_inc(asum_ps, 1)
            panel("forget", 0, 0, 0, None, with_ctx=True)
            with pe.Fori(1, 4) as i:
                panel("forget", i, 0, 0, None, with_ctx=True, between=lambda k: keys_and_states(i - 1, k))
            panel("query", 0, 0, 0, hL, between=lambda k: keys_and_states(3, k))
            panel("query", 0, 1, 4, hL)

            def level(i, k):
                h = LEVELS[k]
                pe.wait_ge(lv_op, i * 9 + (k + 1))
                if k:
                    pe.wait_ge(lv_cp, i * 9 + k)
                for tile in range(2):
                    other = 1 - tile if h == 128 else tile
                    for e in range(4):
                        last = mm(side[:, tile, P * e:P * (e + 1)], lv[k % 2][:, 1, e, P * tile:P * (tile + 1)],
                                  lv[k % 2][:, 0, e, P * other:P * (other + 1)], start=True, stop=True)
                last.then_inc(lv_sc, 1)

            def outputs(i):
                pe.wait_ge(lv_cp, i * 9 + 9)
                pe.wait_ge(o_op, i + 1)
                pe.wait_ge(vg_in, i + 1)
                for e in range(4):
                    out = side[:, 2 + e // 2, T * (e % 2):T * (e % 2 + 1)]
                    cols = slice(HD * e, HD * (e + 1))
                    mm(out, vg[:, 0, cols], pT[:, 0, e], start=True, stop=False)
                    mm(out, vg[:, 1, cols], pT[:, 1, e], start=False, stop=False)
                    mm(out, sg_st[:, 0, cols], lv[0][:, 0, e], start=False, stop=False)
                    last = mm(out, sg_st[:, 1, cols], lv[0][:, 1, e], start=False, stop=True)
                last.then_inc(o_ps, 1)

            with pe.Fori(0, 2) as i:
                def beside(k):
                    if 1 <= k < 10:
                        level(i, k - 1)
                    if k == 10:
                        outputs(i)
                    if k == 11:
                        pe.wait_ge(o_sq, i + 1)
                        for n in range(2):
                            last = mm(side[:, n], ones[:], lv[1][:, 0].rearrange("p e t -> p (e t)")[:, PW * n:PW * (n + 1)],
                                      start=True, stop=True)
                        last.then_inc(o_ms, 1)
                for n in range(3):
                    panel("mix", i, n, 4 * n, hL, between=lambda k, n=n: beside(4 * n + k))

            def branch(j, h, between):
                it = h + 2 * j
                for p in range(2):
                    panel("gates", it, 2 * p, 6 * p, hL, between=lambda k: between(6 * p + k))

                    def after(k):
                        between(6 * p + 4 + k)
                        if k == 1:
                            if j == 0:
                                pe.wait_ge(at_y, h * 4 + (1 + 3 * p))
                            ada_turn(h * 2 + (4 + 4 * j + p))

                    panel("gates", it, 2 * p + 1, 6 * p + 4, yR[j % 2], ready=lambda k: pe.wait_ge(y_lo, j + 1),
                          between=after)

            with pe.Fori(0, 2) as h:
                def attend(k):
                    u = k
                    if u < 8:
                        if u == 0:
                            pe.wait_ge(at_rot, h + 1)
                        if u >= 2:
                            pe.wait_ge(at_exp, h * 8 + (u - 1))
                        mm(side[:, u % 2], qr[:, u // 2, P * (u % 2):P * (u % 2 + 1)], ak[:, h],
                           start=True, stop=True).then_inc(at_sc, 1)
                    u = k - 2
                    if 0 <= u < 8:
                        pe.wait_ge(at_norm, h * 8 + (u + 1))
                        if u:
                            pe.wait_ge(at_cp, h * 8 + u)
                        for n in range(4):
                            last = nc.tensor.transpose(side[:, 2, P * n:P * (n + 1)], pr[:, u % 2, P * n:P * (n + 1)],
                                                       cs[:, K_ID:K_ID + P])
                        last.then_inc(at_tr, 1)
                    u = k - 3
                    if 0 <= u < 8 and u % 2:
                        e = u // 2
                        pe.wait_ge(at_cp, h * 8 + (u + 1))
                        if u == 1:
                            pe.wait_ge(at_v, h + 1)
                        if e:
                            pe.wait_ge(at_y, h * 4 + e)
                        for n in range(4):
                            last = mm(side[:, 3, 0:T], avg[:, n], prT[:, e % 2, n], start=n == 0, stop=n == 3)
                        last.then_inc(at_o, 1)
                branch(0, h, attend)
            with pe.Fori(0, 2) as h:
                branch(1, h, lambda k: None)
            pe.wait_ge(pool_diff, 1)
            for b in range(8):
                if b == 7:
                    pe.wait_ge(pool_y, 2)
                out = side[:, (b % 7) // 2, (b % 7) % 2 * T:(b % 7) % 2 * T + T]
                for n in range(2):
                    last = mm(out, pw_sb[:, b // 2 * 2 + n, P * (b % 2):P * (b % 2 + 1)], pd[:, b // 2 * 2 + n],
                              start=n == 0, stop=n == 1)
                last.then_inc(pool_ps, 1)
            with pe.Fori(0, 2) as h:
                branch(2, h, lambda k: None)

            def sums(b, src, start, stop):
                return mm(side[:, b, 0:T], ones[:], src, start=start, stop=stop)

            def squares(n):
                for k in range(KT):
                    if k % 4 == 0:
                        pe.wait_ge(sq_done, 4 * n + k // 4 + 1)
                    last = sums(1, sqb[:, k], k == 0, k == KT - 1)
                last.then_inc(var_ps, 1)

            pe.wait_ge(m_done, 1)
            sums(0, mu[:], True, False)
            with pe.Fori(0, 4) as i:
                panel("out", i, 0, 0, mR, ready=lambda k: pe.wait_ge(m_lo, k + 1))
                for b in range(4):
                    pe.wait_ge(freed["V"], i * 4 + (PH["out"].f0["V"] + b + 1))
                    sums(0, res[:, i * 4 + b], False, False)
            sums(0, mu[:], False, True).then_inc(mean_ps, 1)
            squares(0)

            with pe.Fori(0, 4) as f:
                with pe.Fori(0, 4) as i:
                    panel("mlp", f * 8 + i, 0, 0, h2, ready=lambda k: pe.wait_ge(h2_lo, 4 * k + 4))
                with pe.Fori(0, 4) as i:
                    panel("mlp", f * 8 + i + 4, 0, 0, hid, ready=lambda k: pe.wait_ge(hid_lo, f * 16 + (4 * k + 4)))
            for k in range(KT):
                pe.wait_ge(res_done, k + 1)
                last = sums(0, res[:, k], k == 0, k == KT - 1)
            last.then_inc(mean_ps, 1)
            squares(1)


def constants():
    cst = np.zeros((P, NK), np.float32)
    cst[:, K_ID:K_ID + P] = np.eye(P)
    q, k = np.arange(P)[:, None], np.arange(P)[None, :]
    cst[:, K_TRI:K_TRI + P] = np.where(k <= q, 0.0, NEG)
    cst[:, K_TRI + P:K_TRI + 2 * P] = np.where(k >= q, 0.0, NEG)
    freq = (10000.0 ** (-np.arange(HD // 4, dtype=np.float32) / (HD // 4))).astype(np.float32)
    t = np.arange(T)
    ang = np.concatenate([(t // GRID_W).astype(np.float32)[:, None] * freq,
                          (t % GRID_W).astype(np.float32)[:, None] * freq], -1).T
    cst[:, K_COS:K_COS + T] = np.concatenate([np.cos(ang)] * 2)
    cst[:, K_SIN:K_SIN + T] = np.concatenate([-np.sin(ang), np.sin(ang)])
    cst[0:4, K_SEL:K_SEL + 2] = np.eye(2)[[0, 1, 0, 1]]
    rcnt = np.zeros((P, 4, T), np.float32)
    for n, w in enumerate(WINDOWS):
        rcnt[:, n] = 1.0 / (np.clip(t + w // 2, 0, T) - np.clip(t - w // 2, 0, T))
    masks = np.zeros((P, 7, P), np.float32)
    for n, size in enumerate((64, 32, 16, 8, 4, 2, 1)):
        masks[:, n] = q // size == k // size
    return cst, rcnt, masks.reshape(P, 7 * P)


def chunks(w):
    K, N = w.shape
    w = w.reshape(K // (CK * P), CK, P, N // PW, PW).transpose(3, 0, 2, 1, 4)
    return np.ascontiguousarray(w).reshape(-1, P, CK * PW)


def columns(v):
    return v.reshape(-1, P).T


def kernel(**inputs):
    import concourse.bacc as bacc
    from concourse.bass_utils import run_bass_kernel_spmd

    a = {k: np.asarray(v) for k, v in inputs.items()}
    cst, rcnt, masks = constants()
    vecs = np.concatenate([columns(a["c"][0]), columns(a["c_ctx"]), columns(a["b_ada"][0]),
                           columns(a["hgrn_norm"][0]), columns(a["pool_scale"][0]), columns(a["ln1_g"][0]),
                           columns(a["ln1_b"][0]), columns(a["ln2_g"][0]), columns(a["ln2_b"][0]),
                           np.broadcast_to(a["attn_sink"][0], (P, HEADS))], axis=1)
    x2 = np.stack([a["ctx"][0], a["x"][0]])
    xT = x2.reshape(2, T, KT, P).transpose(3, 2, 0, 1).reshape(P, KT * 2 * T)
    f2 = a["w_ff2"][0].reshape(4, D, D)
    arrays = {
        "vecs": vecs, "cst": cst, "rcnt": rcnt, "masks": masks, "xT": xT,
        "w_ada": chunks(a["w_ada"][0]), "w_in": chunks(a["w_in"][0]),
        "pool_w": a["pool_w"][0].reshape(8, P, 256).transpose(1, 0, 2),
        "w_br": np.concatenate([chunks(w) for w in a["w_branch"][0]]),
        "w_out": chunks(a["w_out"][0]), "w_f1": chunks(a["w_ff1"][0]),
        "w_f2": np.concatenate([chunks(w) for w in f2]),
    }
    arrays = {f"in_{k}": np.ascontiguousarray(v) for k, v in arrays.items()}
    nc = bacc.Bacc("TRN2", target_bir_lowering=False, num_devices=1, dynamic_dma_scratch_size=1024)
    args = [nc.dram_tensor(k, v.shape, mybir.dt.from_np(v.dtype), kind="ExternalInput").ap()
            for k, v in arrays.items()]
    args.append(nc.dram_tensor("out_0", (P, KT, T), F32, kind="ExternalOutput").ap())
    build(nc, *args)
    r = run_bass_kernel_spmd(nc, [arrays], core_ids=[0])
    out = np.asarray(r.results[0]["out_0"])
    return out.transpose(2, 1, 0).reshape(1, T, D)
```

```python
from contextlib import ExitStack

import numpy as np

import concourse.bass as bass
from concourse import mybir

F32 = mybir.dt.float32
F32R = mybir.dt.float32r
U8 = mybir.dt.uint8
ALU = mybir.AluOpType
ACT = mybir.ActivationFunctionType
AX = mybir.AxisListType.X

P = 128
D = 2048
T = 256
C = 256
KT = D // P
PW = 512
CK = 4
HEADS = 8
HD = 128
GRID_W = 64
ALPHA = 2.0 ** 0.25
LN_EPS = 1e-5
RMS_EPS = 1e-6
SCALE = HD ** -0.5
NEG = -1e30
WINDOWS = (2, 4, 8, 16)
LEVELS = (128, 64, 32, 16, 8, 4, 2, 1, 0)

PAN_AQ, PAN_AI, PAN_AG, PAN_AF, PAN_B, PAN_CQ, PAN_CKV, PAN_GATE = 0, 2, 4, 6, 10, 12, 14, 15

V_C, V_CC, V_BADA, V_NORM, V_PSC, V_L1G, V_L1B, V_L2G, V_L2B, V_SINK, NV = (
    0, 16, 32, 128, 136, 144, 160, 176, 192, 208, 216)
K_ID, K_TRI, K_COS, K_SIN, K_SEL, NK = 0, 128, 384, 640, 896, 898

PAIRED = "sa" * 4
GATED = ("sa" * 4 + "ss") * 2
BRANCHES = (0, 2, 1)

PHASES = [
    ("ada", 1, "s" * 32, [(4, 1, "A")] * 8),
    ("vals", 1, "s" * 12, [(4, 4, "A")] * 3),
    ("forget", 4, PAIRED, [(4, 4, "A")]),
    ("query", 1, "s" * 8, [(4, 4, "A"), (4, 4, "V")]),
    ("mix", 2, "s" * 12, [(4, 4, "V"), (4, 4, "A"), (4, 4, "V")]),
    ("gates", 6, GATED, [(4, 4, "A"), (2, 4, "V")] * 2),
    ("out", 4, "ssss", [(4, 4, "V")]),
    ("mlp", 32, "ssss", [(4, 4, "V")]),
]


class Phase:

    former = None

    def __init__(self, name, n, body, panels, before):
        self.name, self.n, self.body, self.panels = name, n, body, panels
        (self.r0, self.c0, self.a0, self.g0, self.u0, self.f0) = before
        self.at = [l for l, kind in enumerate(body) if kind == "s"] + [len(body)]
        self.ns = body.count("s")
        self.na = body.count("a")
        self.blocks = sum(b for _, b, _ in panels)
        self.u = sum(c - 1 for c, _, _ in panels)
        self.f = {e: sum(b for _, b, x in panels if x == e) for e in "AV"}

    def after(self):
        n = self.n
        return (self.r0 + n * len(self.body), self.c0 + n * self.ns, self.a0 + n * self.na,
                self.g0 + n * self.blocks, self.u0 + n * self.u, {e: self.f0[e] + n * self.f[e] for e in "AV"})

    def raw(self, it, local):
        return (self.r0 + local) % 4, it * (4 * len(self.body)) + 16 * ((self.r0 + local) // 4 + 1)

    def parity(self, s):
        return (self.c0 + s) % 2

    def split_count(self, it, s):
        return it * self.ns + (self.c0 + s + 1)

    def blocks_before(self, it, panel):
        return it * self.blocks + (self.g0 + sum(b for _, b, _ in self.panels[:panel]))

    def released(self, it, s):
        s -= 2
        end, used = 0, 0
        for p, (n, _, _) in enumerate(self.panels):
            if s < end:
                break
            if s < end + n - 1:
                return "w_used", it * self.u + (self.u0 + used + s - end + 1)
            end += n
            used += n - 1
            if s == end - 1:
                return "blk_done", self.blocks_before(it, p + 1)
        return "blk_done", self.blocks_before(it, 0)

    def bank_free(self, it, panel, b):
        n = {e: self.f0[e] + sum(k for _, k, x in self.panels[:panel] if x == e) for e in "AV"}
        who = self.panels[panel - 1][2]
        if isinstance(it, int) and it + panel == 0:
            who = self.former
        return who, it * self.f[who] + (n[who] - 4 + b + 1)


def phases():
    out, before, former = {}, (0, 0, 0, 0, 0, {"A": 0, "V": 0}), None
    for name, n, body, panels in PHASES:
        out[name] = Phase(name, n, body, panels, before)
        out[name].former = former
        before, former = out[name].after(), panels[-1][2]
    return out


PH = phases()
KINDS = "".join(body * n for _, n, body, _ in PHASES)


def reuse_needs(ph, its, local):
    split, sums = [], []
    for it in its:
        before = KINDS[:max(0, ph.r0 + it * len(ph.body) + local - 3)]
        split.append(before.count("s") - it * ph.ns)
        sums.append(before.count("a") - it * ph.na)
    former = {KINDS[max(0, ph.r0 + it * len(ph.body) + local - 4)] for it in its}
    return max(split), max(sums), former


def build(nc, vecs, cst, rcnt, masks, xT, w_ada, w_in, pool_w, w_br, w_out, w_f1, w_f2, outT):
    with ExitStack() as ctx:
        KB = 1024
        SIZE = 222 * KB + 512
        arena = ctx.enter_context(nc.sbuf_tensor("arena", [P, SIZE // 4], F32))
        base = (nc.sbuf_base - SIZE) // 32 * 32

        def at(name, shape, off, dt=F32):
            return nc.alloc_sbuf_tensor_at(name, shape, dt, offset=base + int(off))

        raw = at("raw", [P, 4, CK, PW], 0)
        whi = at("whi", [P, 2, CK, PW], 32 * KB, F32R)
        wlo = at("wlo", [P, 2, CK, PW], 48 * KB, F32R)
        hL = at("hL", [P, KT, 2, T], 64 * KB, F32R)
        acc = at("acc", [P, KT, T], 64 * KB)
        hC = at("hC", [P, KT, 2, C], 96 * KB, F32R)
        mk_in = at("mk_in", [P, 7, P], 96 * KB)
        q_t = at("q_t", [P, HEADS, T], 96 * KB)
        ya = at("ya", [P, HEADS, T], 104 * KB)
        cq = at("cq", [P, HEADS, T], 112 * KB)
        xb = at("xb", [P, HEADS, T], 120 * KB)
        pw_sb = at("pw_sb", [P, 8, 256], 96 * KB)
        rc_sb = at("rc_sb", [P, 4, T], 104 * KB)
        ax = at("ax", [P, KT, T], 96 * KB)
        res = at("res", [P, KT, T], 112 * KB)
        xin = at("xin", [P, KT, 2, T], 128 * KB)
        kk = at("kk", [P, 2 * HEADS, T], 128 * KB)
        lf = at("lf", [P, 2 * HEADS, T], 144 * KB)
        mT = at("mT", [P, KT, T], 128 * KB)
        yR = [at("yR0", [P, HEADS, 2, T], 144 * KB, F32R), at("yR1", [P, HEADS, 2, T], 168 * KB, F32R)]
        h2 = at("h2", [P, KT, 2, T], 128 * KB, F32R)
        vl = at("vl", [P, 2, HEADS * HD], 160 * KB)
        vc = at("vc", [P, 2, HEADS * HD], 168 * KB)
        lv = [at("lv0", [P, 2, 4, T], 168 * KB), at("lv1", [P, 2, 4, T], 200 * KB)]
        st = at("st", [P, 2 * HEADS, HD], 176 * KB)
        sR = at("sR", [P, KT, P], 176 * KB, F32R)
        ak = at("ak", [P, 2, C + T], 184 * KB)
        av = at("av", [P, 4, 256], 188 * KB)
        mR = at("mR", [P, KT, 2, T], 160 * KB, F32R)
        hid = at("hid", [P, KT, 2, T], 160 * KB, F32R)
        am = at("am", [P, 2, PW], 192 * KB)
        ht = at("ht", [P, 2, 2, T], 196 * KB)
        z4 = at("z4", [P, 4, C + T], 192 * KB)
        kc = at("kc", [P, 4, C], 200 * KB)
        kcT = at("kcT", [P, 4 * C], 204 * KB)
        zLs = [at("zL0", [P, C + T], 208 * KB), at("zL1", [P, C + T], 212 * KB)]
        zm = at("zm", [P, C + T], 214 * KB)
        pT = at("pT", [P, 2, 4, T], 192 * KB)
        qr = at("qr", [P, 4, T], 192 * KB)
        qs = at("qs", [P, 4, T], 162 * KB)
        pr = at("pr", [P, 2, C + T], 196 * KB)
        prT = at("prT", [P, 2, 4, T], 200 * KB)
        ks = at("ks", [P, 2, T], 160 * KB)
        gz = at("gz", [P, 2, T], 192 * KB)
        pin = at("pin", [P, 2, 272], 160 * KB)
        win = [at("win0", [P, 2, 272], 160 * KB + 2304), at("win1", [P, 2, 272], 160 * KB + 4608)]
        pd = at("pd", [P, HEADS, T], 200 * KB)
        sqb = at("sqb", [P, KT, T], 192 * KB)
        x_t = at("x_t", [P, 2, T], 204 * KB)
        h_t = at("h_t", [P, 2, T], 206 * KB)
        vg = at("vg", [P, 2, PW], 208 * KB)
        sg_st = at("sg_st", [P, 2, PW], 212 * KB)
        avg = at("avg", [P, 4, HD], 208 * KB)
        asum = at("asum", [P, PW], 210 * KB)
        sg = at("sg", [P, 4, T], 212 * KB)
        mu = at("mu", [P, T], 208 * KB)
        rstd = at("rstd", [P, T], 209 * KB)
        cs = at("cs", [P, NK], 216 * KB)
        vv = at("vv", [P, NV], 216 * KB + 3616)
        mk = at("mk", [P, 7, P], 216 * KB + 4480, U8)
        sm = at("sm", [P, 2, KT], 216 * KB + 5376)
        mods1 = at("mods1", [P, 2 * KT, 2], 216 * KB + 5504)
        mods2 = at("mods2", [P, 4 * KT], 216 * KB + 5760)
        col = at("col", [P, 2, 8], 216 * KB + 6080)
        ones = at("ones", [P, P], 222 * KB)

        main = ctx.enter_context(nc.psum_tensor("main", [P, 4, 512], F32))
        side = ctx.enter_context(nc.psum_tensor("side", [P, 4, 512], F32))
        ADA_PS = 448

        def sem(name):
            return ctx.enter_context(nc.semaphore(name))

        raw_full = [sem(f"raw_full{i}") for i in range(4)]
        hi_made, lo_made, ada_used = sem("hi_made"), sem("lo_made"), sem("ada_used")
        released = {"w_used": sem("w_used"), "blk_done": sem("blk_done")}
        w_used, blk_done = released["w_used"], released["blk_done"]
        freed = {"A": sem("freed_by_act"), "V": sem("freed_by_dve")}
        (cst_in, x_in, pool_ld, ax_ld, stored, silu_sig, silu_in, silu_hi, silu_lo, mods_ps, h_tmp, h_hi, h_lo,
         am_used, z_log, z_arg, key_in, key_tr, key_cp, st_ps, st_cp, asum_done, asum_ps, lv_arg, lv_exp,
         lv_op, lv_sc, lv_cp, vg_in, o_exp, o_op, o_ps, o_sq, o_ms, o_rs, y_done, gs_sig, at_sw, at_rot, at_v,
         at_sc, at_max, at_exp, at_norm, at_tr, at_cp, at_o, at_y, zero_set, y_lo, sg_in, pool_diff, pool_ps,
         pool_y, m_done, m_hi, m_lo, ax_in, mean_ps, mu_in, cen_done, sq_done, var_ps, rstd_in, h2_tmp, h2_hi,
         h2_lo, hid_sq, hid_hi, hid_lo, passed, res_done, y_out, cleared) = (sem(x) for x in (
            "cst_in x_in pool_ld ax_ld stored silu_sig silu_in silu_hi silu_lo mods_ps h_tmp h_hi h_lo "
            "am_used z_log z_arg key_in key_tr key_cp st_ps st_cp asum_done asum_ps lv_arg lv_exp "
            "lv_op lv_sc lv_cp vg_in o_exp o_op o_ps o_sq o_ms o_rs y_done gs_sig at_sw at_rot at_v "
            "at_sc at_max at_exp at_norm at_tr at_cp at_o at_y zero_set y_lo sg_in pool_diff pool_ps "
            "pool_y m_done m_hi m_lo ax_in mean_ps mu_in cen_done sq_done var_ps rstd_in h2_tmp h2_hi "
            "h2_lo hid_sq hid_hi hid_lo passed res_done y_out cleared").split())

        def wait(eng, semaphore, value):
            eng.wait_ge(semaphore, value)
            if not isinstance(value, int):
                eng.sem_inc(passed, 1)

        def head_blocks(t, g, h):
            return t[:, bass.ts(g, 4)].rearrange("p e (n a h) -> p (e n) a h", a=2, h=h)

        def level_blocks(t, h):
            return t.rearrange("p e (n a h) -> p (e n) a h", a=2, h=h)

        def keys_of(unit):
            return slice(384, 512) if unit % 2 == 0 else slice(256, 384)

        block = ctx.enter_context(nc.Block())

        @block.sync
        def _(sp):
            def load(name, it, local, src, its=None):
                ph = PH[name]
                split, sums, former = reuse_needs(ph, its or (it,), local)
                slot, _ = ph.raw(0, local)
                first = its[0] if its else it
                if "s" in former and first * ph.ns + split > 0:
                    wait(sp, lo_made, it * ph.ns + split)
                if "a" in former:
                    wait(sp, ada_used, it * ph.na + sums)
                sp.dma_start(raw[:, slot].rearrange("p a b -> p (a b)"), src).then_inc(raw_full[slot], 16)

            for n in range(32):
                load("ada", 0, n, w_ada[n])
            for n, panel in enumerate((PAN_AI, PAN_AI + 1, PAN_CKV)):
                for k in range(4):
                    load("vals", 0, 4 * n + k, w_in[4 * panel + k])

            def forget(i, its):
                for k in range(4):
                    load("forget", i, 2 * k, w_in[i * 4 + (4 * PAN_AF + k)], its)
                    load("forget", i, 2 * k + 1, w_ada[i * 4 + (32 + k)], its)

            forget(0, None)
            with sp.Fori(1, 4) as i:
                forget(i, (1, 2, 3))
            for n in range(8):
                load("query", 0, n, w_in[4 * PAN_AQ + n])
            with sp.Fori(0, 2) as i:
                for n, panel in enumerate((PAN_AG, PAN_CQ, PAN_B)):
                    for k in range(4):
                        load("mix", i, 4 * n + k, w_in[i * 4 + (4 * panel + k)], (0, 1))
            for j, branch in enumerate(BRANCHES):
                its = (2 * j, 2 * j + 1)
                with sp.Fori(0, 2) as h:
                    for p in range(2):
                        for k in range(4):
                            load("gates", h + 2 * j, 10 * p + 2 * k,
                                 w_in[h * 8 + (4 * (PAN_GATE + 4 * branch + p) + k)], its)
                            load("gates", h + 2 * j, 10 * p + 2 * k + 1, w_ada[h * 8 + (48 + 16 * j + 4 * p + k)],
                                 its)
                        for k in range(2):
                            load("gates", h + 2 * j, 10 * p + 8 + k, w_br[h * 4 + (8 * branch + 2 * p + k)], its)
            with sp.Fori(0, 4) as i:
                for k in range(4):
                    load("out", i, k, w_out[i * 4 + k], range(4))
            with sp.Fori(0, 4) as f:
                for half, w in enumerate((w_f1, w_f2)):
                    with sp.Fori(0, 4) as i:
                        for k in range(4):
                            load("mlp", f * 8 + i + 4 * half, k, w[f * 16 + i * 4 + k], range(32))

        @block.scalar
        def _(act):
            A = nc.scalar.activation
            drain = nc.scalar.drain

            def split(name, it, s):
                ph = PH[name]
                slot, full = ph.raw(it, ph.at[s])
                wait(act, raw_full[slot], full)
                if name != "ada" or s >= 2:
                    which, count = ph.released(it, s)
                    wait(act, released[which], count)
                nc.scalar.copy(whi[:, ph.parity(s)], raw[:, slot]).then_inc(hi_made, 1)

            def blk(name, it, panel, b):
                wait(act, blk_done, PH[name].blocks_before(it, panel) + (b + 1))

            act.dma_start(vv[:], vecs).then_inc(cst_in, 16)
            act.dma_start(cs[:], cst).then_inc(cst_in, 16)
            act.dma_start(mk_in[:].rearrange("p a b -> p (a b)"), masks).then_inc(cst_in, 16)
            act.dma_start(xin[:].rearrange("p k v t -> p (k v t)"), xT).then_inc(x_in, 16)
            wait(act, cst_in, 48)
            A(sm[:].rearrange("p v k -> p (v k)"), vv[:, V_C:V_C + 2 * KT], ACT.Sigmoid).then_inc(silu_sig, 1)
            wait(act, silu_in, 1)
            nc.scalar.copy(sR[:, :, 0:2], sm[:].rearrange("p v k -> p k v")).then_inc(silu_hi, 1)

            split("ada", 0, 0)
            for t in range(8):
                for k in range(4):
                    split("ada", 0, 4 * t + k + 1)
                blk("ada", 0, t, 0)
                if t >= 2:
                    wait(act, am_used, t - 1)
                nc.scalar.copy(am[0:4, t % 2], main[0:4, t % 4]).then_inc(freed["A"], 1)

            for t in range(3):
                for k in range(4):
                    split("vals", 0, 4 * t + k + 1)
                    if t == 0 and k == 0:
                        for kt in range(KT):
                            wait(act, h_tmp, kt + 1)
                            nc.scalar.copy(hC[:, kt, 0], ht[:, kt % 2, 0])
                            nc.scalar.copy(hL[:, kt, 0], ht[:, kt % 2, 1]).then_inc(h_hi, 1)
                for b in range(4):
                    blk("vals", 0, t, b)
                    if t < 2:
                        dst = (vc, vl)[b // 2][:, b % 2, PW * t:PW * (t + 1)]
                    elif b < 2:
                        dst = ak[:, b]
                    else:
                        dst = av[:, 2 * (b - 2):2 * (b - 1)].rearrange("p a n -> p (a n)")
                    nc.scalar.copy(dst, main[:, b]).then_inc(freed["A"], 1)

            def key_copy(it):
                wait(act, key_tr, it + 1)
                nc.scalar.copy(kcT[:], side[:, 0:2].rearrange("p a b -> p (a b)")).then_inc(key_cp, 1)

            def state_copy(it):
                wait(act, st_ps, it + 1)
                nc.scalar.copy(st[:, bass.ts(it, 4)].rearrange("p a b -> p (a b)"), side[:, 2]).then_inc(st_cp, 1)

            def gate_pair(it, n):
                for b in (2 * n, 2 * n + 1):
                    L = zLs[b % 2]
                    drain()
                    A(L[:], z4[:, b], ACT.Abs)
                    drain()
                    A(L[:], L[:], ACT.Exp, scale=-1.0)
                    drain()
                    A(L[:], L[:], ACT.Ln, bias=1.0).then_inc(z_log, 1)
                for b in (2 * n, 2 * n + 1):
                    wait(act, z_arg, it * 4 + (b + 1))
                    A(kk[:, it * 4 + b], zm[:, C:], ACT.Exp, scale=-1.0)
                    A(kc[:, b], zLs[b % 2][:, 0:C], ACT.Exp).then_inc(key_in, 1)

            def logits_out(it):
                drain()
                for b in range(4):
                    blk("forget", it, 0, b)
                    nc.scalar.copy(z4[:, b], main[:, b]).then_inc(freed["A"], 1)

            nc.scalar.preload_act_table_set("natural_log_exp_and_others")
            for k in range(4):
                split("forget", 0, k + 1)
            logits_out(0)
            with act.Fori(1, 4) as i:
                for k in range(4):
                    split("forget", i, k + 1)
                    if k < 2:
                        gate_pair(i - 1, k)
                    if k == 3:
                        key_copy(i - 1)
                logits_out(i)
                state_copy(i - 1)

            for k in range(8):
                split("query", 0, k + 1)
                if k in (0, 2):
                    gate_pair(3, k // 2)
                if k == 3:
                    for b in range(4):
                        blk("query", 0, 0, b)
                        nc.scalar.copy(q_t[:, b], main[:, b, 0:T]).then_inc(freed["A"], 1)
                if k == 5:
                    key_copy(3)
                if k == 6:
                    state_copy(3)

            def inverse_rms(i):
                wait(act, o_ms, i + 1)
                A(lv[1][:, 1].rearrange("p e t -> p (e t)"), side[:, 0:2].rearrange("p a b -> p (a b)"),
                  ACT.Ln, scale=1.0 / HD, bias=RMS_EPS)
                drain()
                A(lv[1][:, 1], lv[1][:, 1], ACT.Exp, scale=-0.5).then_inc(o_rs, 1)

            def swap(h):
                g4 = cq[:, 4 * h:4 * h + 4]
                drain()
                nc.scalar.copy(qs[0:64], g4[64:128])
                nc.scalar.copy(qs[64:128], g4[0:64])
                nc.scalar.copy(ks[0:64, 0], ak[64:128, h, C:])
                nc.scalar.copy(ks[64:128, 0], ak[0:64, h, C:]).then_inc(at_sw, 1)

            for i in range(2):
                for k in range(12):
                    split("mix", i, k + 1)
                    if i and k == 0:
                        inverse_rms(0)
                    if k < 8:
                        wait(act, lv_arg, i * 8 + (k + 1))
                        t = lv[k % 2][:].rearrange("p a e t -> p (a e t)")
                        A(t, t, ACT.Exp).then_inc(lv_exp, 1)
                    if k == 10:
                        wait(act, lv_sc, i * 9 + 9)
                        A(lv[0][:, 0], lf[:, bass.ts(i, 4)], ACT.Exp)
                        A(lv[0][:, 1], lf[:, bass.ts(i + 2, 4)], ACT.Exp).then_inc(o_exp, 1)
                    if k == 11:
                        wait(act, o_ps, i + 1)
                        A(lv[1][:, 0].rearrange("p e t -> p (e t)"), side[:, 2:4].rearrange("p a b -> p (a b)"),
                          ACT.Square).then_inc(o_sq, 1)
                    if k % 4 == 3 and k < 8:
                        for b in range(4):
                            blk("mix", i, k // 4, b)
                            if k == 3:
                                A(ya[:, i * 4 + b], main[:, b, 0:T], ACT.Sigmoid).then_inc(gs_sig, 1)
                            else:
                                nc.scalar.copy(cq[:, i * 4 + b], main[:, b, 0:T]).then_inc(freed["A"], 1)
            wait(act, vg_in, 2)
            swap(0)

            def gates(j, h, between):
                it = h + 2 * j
                for k in range(12):
                    split("gates", it, k + 1)
                    between(k)
                    if k in (3, 9):
                        p = k // 6
                        for b in range(4):
                            blk("gates", it, 2 * p, b)
                            A(sg[:, b], main[:, b, 0:T], ACT.Sigmoid).then_inc(freed["A"], 1)

            for h in range(2):
                def attend(k):
                    if h == 0 and k == 0:
                        inverse_rms(1)
                    if h == 0 and k == 5:
                        wait(act, y_lo, 1)
                        act.dma_start(pw_sb[:], pool_w).then_inc(pool_ld, 16)
                        act.dma_start(rc_sb[:], rcnt).then_inc(pool_ld, 16)
                    if h == 0 and k == 8:
                        wait(act, at_rot, 1)
                        swap(1)
                    if 5 <= k <= 11 and k % 2 == 1:
                        e = (k - 5) // 2
                        wait(act, at_o, h * 4 + (e + 1))
                        nc.scalar.copy(cq[:, h * 4 + e], side[:, 3, 0:T]).then_inc(at_y, 1)
                    u = k - 3
                    if 0 <= u < 8:
                        wait(act, at_tr, h * 8 + (u + 1))
                        nc.scalar.copy(prT[:, (u // 2) % 2, :, (u % 2) * P:(u % 2 + 1) * P],
                                       side[:, 2].rearrange("p (a b) -> p a b", a=4)).then_inc(at_cp, 1)
                    u = k - 2
                    if 0 <= u < 8:
                        wait(act, at_max, h * 8 + (u + 1))
                        c = col[:, u % 2]
                        A(pr[:, u % 2], side[:, u % 2], ACT.Exp, bias=c[:, 2:3], scale=SCALE,
                          accum_out=c[:, 3:4])
                        sink = h * 4 + (V_SINK + u // 2)
                        A(c[:, 4:5], vv[:, bass.ds(sink, 1)], ACT.Exp, bias=c[:, 2:3]).then_inc(at_exp, 1)
                gates(0, h, attend)
            with act.Fori(0, 2) as h:
                gates(1, h, lambda k: None)
            for b in range(8):
                wait(act, pool_ps, b // 2 * 2 + 2 if b < 6 else b + 1)
                A(xb[:, b], side[:, (b % 7) // 2, (b % 7) % 2 * T:(b % 7) % 2 * T + T], ACT.Identity,
                  scale=vv[:, V_PSC + b:V_PSC + b + 1]).then_inc(pool_y, 1)
            act.dma_start(ax[:], xT.rearrange("p (k v t) -> p k v t", v=2, t=T)[:, :, 1]).then_inc(ax_ld, 16)
            with act.Fori(0, 2) as h:
                def residual(k):
                    if k == 5:
                        wait(act, ax_ld, 16)
                        nc.scalar.mul(ax[:, bass.ts(h, 8)], ax[:, bass.ts(h, 8)], ALPHA).then_inc(ax_in, 1)
                gates(2, h, residual)

            with act.Fori(0, 4) as i:
                for k in range(4):
                    split("out", i, k + 1)

            def norm(n):
                wait(act, mean_ps, n + 1)
                A(mu[:], side[:, 0, 0:T], ACT.Copy, scale=1.0 / D).then_inc(mu_in, 1)
                for q in range(4):
                    wait(act, cen_done, 4 * n + q + 1)
                    A(sqb[:, 4 * q:4 * q + 4], res[:, 4 * q:4 * q + 4], ACT.Square).then_inc(sq_done, 1)
                wait(act, var_ps, n + 1)
                A(rstd[:], side[:, 1, 0:T], ACT.Ln, scale=1.0 / D, bias=LN_EPS)
                drain()
                A(rstd[:], rstd[:], ACT.Exp, scale=-0.5).then_inc(rstd_in, 1)

            norm(0)
            for k in range(KT):
                wait(act, h2_tmp, k + 1)
                nc.scalar.mul(ax[:, k], x_t[:, k % 2], ALPHA)
                nc.scalar.copy(h2[:, k, 0], h_t[:, k % 2]).then_inc(h2_hi, 1)

            def mlp(f, last):
                with act.Fori(0, 4) as i:
                    for k in range(4):
                        split("mlp", f * 8 + i, k + 1)
                with act.Fori(0, 3) as i:
                    for k in range(4):
                        split("mlp", f * 8 + i + 4, k + 1)
                for k in range(3 if last else 4):
                    split("mlp", f * 8 + 7, k + 1)

            with act.Fori(0, 3) as f:
                mlp(f, False)
            mlp(3, True)
            norm(1)
            wait(act, y_out, 4)
            for q in range(4):
                act.dma_start(outT[:, 4 * q:4 * q + 4], acc[:, 4 * q:4 * q + 4]).then_inc(stored, 16)
            wait(act, stored, 64)

        @block.gpsimd
        def _(pool):
            pool.wait_ge(cst_in, 48)
            nc.gpsimd.tensor_copy(mk[:], mk_in[:])
            nc.gpsimd.memset(sR[:].rearrange("p k n -> p (k n)").bitcast(F32), 0.0).then_inc(cleared, 1)
            TT = nc.gpsimd.tensor_tensor
            drain = nc.gpsimd.drain

            def two_parts(out, src, count):
                one = ones[:, 0:1] if len(src.shape) == 2 else ones[:, 0:1].unsqueeze(2)
                one = one.to_broadcast(list(src.shape))
                TT(out[0], src, one, ALU.mult)
                drain()
                TT(out[1], src, out[0].bitcast(F32), ALU.subtract).then_inc(count, 1)

            def level_args(i, k):
                h = LEVELS[k]
                f, w = head_blocks(lf, i, h), head_blocks(lf, i + 2, h)
                q, key = level_blocks(lv[k % 2][:, 0], h), level_blocks(lv[k % 2][:, 1], h)
                shape = [P, q.shape[1], h]
                f_mid = f[:, :, 0, h - 1:h].to_broadcast(shape)
                w_mid = w[:, :, 1, 0:1].to_broadcast(shape)
                TT(q[:, :, 1], f[:, :, 1], f_mid, ALU.subtract)
                TT(q[:, :, 0], w[:, :, 0], w_mid, ALU.subtract)
                TT(key[:, :, 0], f_mid, f[:, :, 0], ALU.subtract)
                TT(key[:, :, 1], w_mid, w[:, :, 1], ALU.subtract).then_inc(lv_arg, 1)

            pool.wait_ge(st_cp, 4)
            for i in range(2):
                for k in range(8):
                    if k >= 2:
                        pool.wait_ge(lv_sc, i * 9 + (k - 1))
                    elif i:
                        pool.wait_ge((o_ps, y_done)[k], i)
                    level_args(i, k)
                drain()
                if i == 0:
                    pool.wait_ge(asum_ps, 5)
                nc.gpsimd.tensor_copy(vg[:], vl[:, :, bass.ts(i, PW)])
                nc.gpsimd.tensor_copy(sg_st[:, 0], st[:, bass.ts(i, 4)].rearrange("p e d -> p (e d)"))
                nc.gpsimd.tensor_copy(sg_st[:, 1],
                                      st[:, bass.ts(i + 2, 4)].rearrange("p e d -> p (e d)")).then_inc(vg_in, 1)

            def rotate(h):
                cos, sin = cs[:, K_COS:K_COS + T], cs[:, K_SIN:K_SIN + T]
                cos4 = cos.unsqueeze(1).to_broadcast([P, 4, T])
                sin4 = sin.unsqueeze(1).to_broadcast([P, 4, T])
                pool.wait_ge(at_sw, h + 1)
                if h:
                    pool.wait_ge(at_sc, 8)
                TT(qr[:], cq[:, 4 * h:4 * h + 4], cos4, ALU.mult)
                TT(qs[:], qs[:], sin4, ALU.mult)
                TT(ks[:, 1], ak[:, h, C:], cos, ALU.mult)
                TT(ks[:, 0], ks[:, 0], sin, ALU.mult)
                drain()
                TT(qr[:], qr[:], qs[:], ALU.add)
                TT(ak[:, h, C:], ks[:, 0], ks[:, 1], ALU.add).then_inc(at_rot, 1)

            def group_values(h):
                nc.gpsimd.tensor_copy(avg[:], av[:, :, HD * h:HD * (h + 1)]).then_inc(at_v, 1)

            rotate(0)
            pool.wait_ge(o_ps, 2)
            group_values(0)
            pool.wait_ge(y_done, 2)
            two_parts([yR[0][:, :, n] for n in range(2)], ya[:], y_lo)
            rotate(1)
            pool.wait_ge(at_o, 4)
            group_values(1)
            pool.wait_ge(at_y, 8)
            drain()
            two_parts([yR[1][:, :, n] for n in range(2)], cq[:], y_lo)

            pool.wait_ge(pool_ld, 32)
            nc.gpsimd.memset(pin[:], 0.0)
            for n in range(4):
                x2 = xb[:, 2 * n:2 * n + 2]
                drain()
                nc.gpsimd.tensor_copy(pin[:, :, 8:8 + T], x2)
                src, lo, hi = pin, 0, 272
                for step in range(n + 1):
                    left = right = 1 << max(step - 1, 0)
                    if step == 0:
                        left, right = 1, 0
                    lo, hi = lo + left, hi - right
                    drain()
                    TT(win[step % 2][:, :, lo:hi], src[:, :, lo - left:hi - left], src[:, :, lo + right:hi + right],
                       ALU.add)
                    src = win[step % 2]
                drain()
                d2 = pd[:, 2 * n:2 * n + 2]
                TT(d2, src[:, :, 8:8 + T], rc_sb[:, n:n + 1].to_broadcast([P, 2, T]), ALU.mult)
                drain()
                last = TT(d2, d2, x2, ALU.subtract)
            last.then_inc(pool_diff, 1)
            pool.wait_ge(pool_y, 8)
            two_parts([yR[0][:, :, n] for n in range(2)], xb[:], y_lo)

            with pool.Fori(0, 2) as h:
                for p in range(2):
                    rows = bass.ds(h * 8 + 4 * p, 4)
                    drain()
                    wait(pool, m_done, h * 8 + (4 * p + 4))
                    two_parts([mR[:, rows, n] for n in range(2)], mT[:, rows], m_lo)

            pool.sem_inc(hid_lo, 4)
            with pool.Fori(0, 4) as f:
                with pool.Fori(0, 4) as i:
                    for b in range(4):
                        drain()
                        wait(pool, freed["V"], f * 32 + i * 4 + (PH["mlp"].f0["V"] + b + 1))
                        TT(sqb[:, b], sqb[:, b], sqb[:, b], ALU.mult)
                        drain()
                        two_parts([hid[:, i * 4 + b, n] for n in range(2)], sqb[:, b], hid_lo)

        @block.vector
        def _(dve):
            TT, TS, STT = nc.vector.tensor_tensor, nc.vector.tensor_scalar, nc.vector.scalar_tensor_tensor
            drain = nc.vector.drain

            def split(name, it, s):
                ph = PH[name]
                dve.wait_ge(hi_made, ph.split_count(it, s))
                slot, par = ph.raw(0, ph.at[s])[0], ph.parity(s)
                TT(wlo[:, par], raw[:, slot], whi[:, par].bitcast(F32), ALU.subtract).then_inc(lo_made, 1)

            def blk(name, it, panel, b):
                dve.wait_ge(blk_done, PH[name].blocks_before(it, panel) + (b + 1))

            def ada_sum(name, it, local, n, k):
                slot, full = PH[name].raw(it, local)
                wait(dve, raw_full[slot], full)
                if k == 0:
                    dve.wait_ge(asum_ps, n + 1)
                for j in range(CK):
                    s = sm[:, 0, k * CK + j:k * CK + j + 1]
                    if k == 0 and j == 0:
                        last = TS(asum[:], raw[:, slot, j], s, None, ALU.mult)
                    else:
                        drain()
                        last = STT(asum[:], raw[:, slot, j], s, asum[:], ALU.mult, ALU.add)
                last.then_inc(ada_used, 1)

            nc.vector.memset(ones[:], 1.0)
            dve.wait_ge(silu_sig, 1)
            dve.wait_ge(cleared, 1)
            TT(sm[:].rearrange("p v k -> p (v k)"), sm[:].rearrange("p v k -> p (v k)"), vv[:, V_C:V_C + 2 * KT],
               ALU.mult).then_inc(silu_in, 1)
            dve.wait_ge(silu_hi, 1)
            TT(sR[:, :, 2:4], sm[:].rearrange("p v k -> p k v"), sR[:, :, 0:2].bitcast(F32),
               ALU.subtract).then_inc(silu_lo, 1)
            for s in range(33):
                split("ada", 0, s)

            def modulate():
                dve.wait_ge(mods_ps, 1)
                TT(mods1[:], side[:, 0, 0:64].rearrange("p (c v) -> p c v", v=2),
                   vv[:, V_BADA:V_BADA + 32].unsqueeze(2).to_broadcast([P, 32, 2]), ALU.add)
                drain()
                TS(mods1[:, KT:], mods1[:, KT:], 1.0, None, ALU.add)
                drain()
                dve.wait_ge(x_in, 16)

                def lo(k):
                    dve.wait_ge(h_hi, k + 1)
                    TT(hC[:, k, 1], ht[:, k % 2, 0], hC[:, k, 0].bitcast(F32), ALU.subtract)
                    TT(hL[:, k, 1], ht[:, k % 2, 1], hL[:, k, 0].bitcast(F32), ALU.subtract).then_inc(h_lo, 1)

                for k in range(KT):
                    if k >= 2:
                        drain()
                    TS(ht[:, k % 2, 0], xin[:, k, 0], mods1[:, KT + k, 1:2], mods1[:, k, 1:2], ALU.mult, ALU.add)
                    TS(ht[:, k % 2, 1], xin[:, k, 1], mods1[:, KT + k, 0:1], mods1[:, k, 0:1],
                       ALU.mult, ALU.add).then_inc(h_tmp, 1)
                    if k:
                        lo(k - 1)
                lo(KT - 1)

            for s in range(1, 13):
                split("vals", 0, s)
                if s == 1:
                    modulate()

            def gate_pair(it, n, backward):
                for b in (2 * n, 2 * n + 1):
                    L, z = zLs[b % 2], z4[:, b]
                    drain()
                    dve.wait_ge(z_log, it * 4 + (b + 1))
                    if b:
                        dve.wait_ge(key_in, it * 4 + b)
                    STT(zm[:], z, 0.0, L[:], ALU.max, ALU.add)
                    STT(z, z, 0.0, L[:], ALU.min, ALU.subtract)
                    drain()
                    one = ones[:, 0:1].to_broadcast([P, C])
                    dst, lat, ctx_f = lf[:, it * 4 + b], z4[:, b, C:], z4[:, b, 0:C]
                    if backward:
                        back = L[:, C:]
                        nc.vector.tensor_tensor_scan(back[:, ::-1], one, lat[:, ::-1], 0.0, ALU.mult, ALU.add)
                        nc.vector.memset(L[:, 0:1], 0.0)
                        nc.vector.tensor_tensor_scan(L[:, 1:C], one[:, 1:], ctx_f[:, 0:C - 1], 0.0,
                                                     ALU.mult, ALU.add)
                    else:
                        nc.vector.tensor_tensor_scan(dst, one, lat, 0.0, ALU.mult, ALU.add)
                        nc.vector.memset(L[:, C - 1:C], 0.0)
                        nc.vector.tensor_tensor_scan(L[:, 0:C - 1][:, ::-1], one[:, 1:], ctx_f[:, 1:][:, ::-1], 0.0,
                                                     ALU.mult, ALU.add)
                    drain()
                    if backward:
                        nc.vector.tensor_copy(dst, back)
                    TT(L[:, 0:C], L[:, 0:C], zm[:, 0:C], ALU.subtract).then_inc(z_arg, 1)

            def forget(it, backward):
                for k in range(4):
                    split("forget", it, k + 1)
                    ada_sum("forget", it, 2 * k + 1, it, k)
                    if k < 2 and backward is not None:
                        gate_pair(it - 1, k, backward)

            forget(0, None)
            with dve.Fori(1, 3) as i:
                forget(i, False)
            forget(3, True)

            for k in range(8):
                split("query", 0, k + 1)
                if k in (0, 2):
                    gate_pair(3, k // 2, True)
            for b in range(4):
                blk("query", 0, 1, b)
                nc.vector.tensor_copy(q_t[:, 4 + b], main[:, b, 0:T]).then_inc(freed["V"], 1)
            dve.wait_ge(asum_ps, 5)
            TT(mods2[:, 0:KT], side[:, 3, ADA_PS:ADA_PS + KT], vv[:, V_BADA + 32:V_BADA + 48], ALU.add)

            def level_operands(i, k):
                h = LEVELS[k]
                t = lv[k % 2]
                q4 = q_t[:, bass.ts(i, 4)]
                if h:
                    dve.wait_ge(lv_exp, i * 8 + (k + 1))
                    kf, kb = head_blocks(kk, i, h), head_blocks(kk, i + 2, h)
                    key = level_blocks(t[:, 1], h)
                    TT(t[:, 0], t[:, 0], q4, ALU.mult)
                    TT(key[:, :, 0], key[:, :, 0], kf[:, :, 0], ALU.mult)
                    TT(key[:, :, 1], key[:, :, 1], kb[:, :, 1], ALU.mult).then_inc(lv_op, 1)
                else:
                    drain()
                    nc.vector.tensor_copy(t[:, 0], q4)
                    TT(t[:, 1], kk[:, bass.ts(i, 4)], kk[:, bass.ts(i + 2, 4)], ALU.add).then_inc(lv_op, 1)

            def level_scores(i, k):
                h = LEVELS[k]
                drain()
                wait(dve, lv_sc, i * 9 + (k + 1))
                for tile in range(2):
                    src = side[:, tile].rearrange("p (e t) -> p e t", e=4)
                    cols = 1 - tile if h == 128 else tile
                    dst = pT[:, tile, :, cols * P:(cols + 1) * P]
                    if h >= 64:
                        last = nc.vector.tensor_copy(dst, src)
                    else:
                        last = nc.vector.copy_predicated(dst, mk[:, k - 2:k - 1].to_broadcast([P, 4, P]), src)
                last.then_inc(lv_cp, 1)

            def outputs(i):
                wait(dve, o_rs, i + 1)
                t = lv[1][:, 1].rearrange("p e t -> p (e t)")
                TT(t, t, side[:, 2:4].rearrange("p a b -> p (a b)"), ALU.mult)
                drain()
                for e in range(4):
                    last = STT(ya[:, i * 4 + e], lv[1][:, 1, e], vv[:, i * 4 + (V_NORM + e):i * 4 + (V_NORM + e + 1)],
                               ya[:, i * 4 + e], ALU.mult, ALU.mult)
                last.then_inc(y_done, 1)

            for i in range(2):
                for k in range(12):
                    split("mix", i, k + 1)
                    if i and k == 0:
                        outputs(0)
                    if 2 <= k < 11:
                        level_scores(i, k - 2)
                    if 1 <= k < 10:
                        level_operands(i, k - 1)
                    if k == 10:
                        dve.wait_ge(o_exp, i + 1)
                        q4 = q_t[:, bass.ts(i, 4)]
                        TT(lv[0][:, 0], lv[0][:, 0], q4, ALU.mult)
                        TT(lv[0][:, 1], lv[0][:, 1], q4, ALU.mult).then_inc(o_op, 1)
                    if k == 3:
                        for b in range(4):
                            blk("mix", i, 0, b)
                            dve.wait_ge(gs_sig, i * 4 + (b + 1))
                            TT(ya[:, i * 4 + b], ya[:, i * 4 + b], main[:, b, 0:T],
                               ALU.mult).then_inc(freed["V"], 1)
                    if k == 11:
                        for b in range(4):
                            blk("mix", i, 2, b)
                            nc.vector.tensor_copy(xb[:, i * 4 + b], main[:, b, 0:T]).then_inc(freed["V"], 1)

            def gates(j, h, between):
                it = h + 2 * j
                for k in range(12):
                    split("gates", it, k + 1)
                    p, q = k // 6, k % 6
                    if q < 4:
                        ada_sum("gates", it, 10 * p + 2 * q + 1, h * 2 + (4 + 4 * j + p), q)
                    between(k)
                    if q == 5:
                        for b in range(4):
                            blk("gates", it, 2 * p + 1, b)
                            dst = mT[:, h * 8 + (4 * p + b)]
                            if j == 0:
                                dve.wait_ge(freed["A"], it * 8 + (PH["gates"].f0["A"] + 4 * p + b + 1))
                                TT(dst, sg[:, b], main[:, b, 0:T], ALU.mult).then_inc(freed["V"], 1)
                            else:
                                dve.sem_inc(passed, 1)
                                drain()
                                dve.wait_ge(freed["A"], it * 8 + (PH["gates"].f0["A"] + 4 * p + b + 1))
                                TT(gz[:, b % 2], sg[:, b], main[:, b, 0:T], ALU.mult).then_inc(freed["V"], 1)
                                drain()
                                last = TT(dst, dst, gz[:, b % 2], ALU.add)
                                if j == 2:
                                    last.then_inc(m_done, 1)

            for h in range(2):
                def attend(k):
                    if h == 0 and k == 0:
                        outputs(1)
                    u = k - 2
                    if 0 <= u < 8:
                        c, s = col[:, u % 2], side[:, u % 2]
                        drain()
                        dve.wait_ge(at_sc, h * 8 + (u + 1))
                        TT(s[:, keys_of(u)], s[:, keys_of(u)],
                           cs[:, K_TRI + P * (u % 2):K_TRI + P * (u % 2 + 1)], ALU.add)
                        drain()
                        nc.vector.reduce_max(c[:, 0:1], s, AX)
                        drain()
                        TS(c[:, 1:2], c[:, 0:1], SCALE, vv[:, bass.ds(h * 4 + (V_SINK + u // 2), 1)],
                           ALU.mult, ALU.max)
                        drain()
                        TS(c[:, 2:3], c[:, 1:2], -1.0, None, ALU.mult).then_inc(at_max, 1)
                        dve.wait_ge(at_exp, h * 8 + (u + 1))
                        TT(c[:, 5:6], c[:, 3:4], c[:, 4:5], ALU.add)
                        drain()
                        nc.vector.reciprocal(c[:, 6:7], c[:, 5:6])
                        drain()
                        TS(pr[:, u % 2], pr[:, u % 2], c[:, 6:7], None, ALU.mult).then_inc(at_norm, 1)
                gates(0, h, attend)
            with dve.Fori(0, 2) as h:
                gates(1, h, lambda k: None)
            with dve.Fori(0, 2) as h:
                gates(2, h, lambda k: None)

            dve.wait_ge(asum_ps, 17)
            drain()
            TT(mods2[:, KT:], side[:, 3, ADA_PS + KT:ADA_PS + 4 * KT], vv[:, V_BADA + 48:V_BADA + 96], ALU.add)
            drain()
            TS(mods2[:, 2 * KT:3 * KT], mods2[:, 2 * KT:3 * KT], 1.0, None, ALU.add)
            nc.vector.memset(mu[:], 0.0).then_inc(zero_set, 1)
            dve.wait_ge(ax_in, 2)
            with dve.Fori(0, 4) as i:
                for k in range(4):
                    split("out", i, k + 1)
                for b in range(4):
                    blk("out", i, 0, b)
                    n = i * 4 + b
                    STT(res[:, n], main[:, b, 0:T], mods2[:, bass.ds(n, 1)], ax[:, n],
                        ALU.mult, ALU.add).then_inc(freed["V"], 1)

            def norm(n, gain, shift, then):
                dve.wait_ge(mu_in, n + 1)
                for q in range(4):
                    r4 = res[:, 4 * q:4 * q + 4]
                    TT(r4, r4, mu[:].unsqueeze(1).to_broadcast([P, 4, T]), ALU.subtract).then_inc(cen_done, 1)
                dve.wait_ge(rstd_in, n + 1)
                for q in range(4):
                    r4 = res[:, 4 * q:4 * q + 4]
                    drain()
                    TT(r4, r4, rstd[:].unsqueeze(1).to_broadcast([P, 4, T]), ALU.mult)
                    drain()
                    for k in range(4 * q, 4 * q + 4):
                        then(k, vv[:, gain + k:gain + k + 1], vv[:, shift + k:shift + k + 1])

            def h2_rest(k):
                dve.wait_ge(h2_hi, k + 1)
                TT(h2[:, k, 1], h_t[:, k % 2], h2[:, k, 0].bitcast(F32), ALU.subtract).then_inc(h2_lo, 1)

            def to_mlp(k, gain, shift):
                if k >= 2:
                    drain()
                TS(x_t[:, k % 2], res[:, k], gain, shift, ALU.mult, ALU.add)
                drain()
                TS(h_t[:, k % 2], x_t[:, k % 2], mods2[:, 2 * KT + k:2 * KT + k + 1], mods2[:, KT + k:KT + k + 1],
                   ALU.mult, ALU.add).then_inc(h2_tmp, 1)
                if k:
                    h2_rest(k - 1)

            norm(0, V_L1G, V_L1B, to_mlp)
            h2_rest(KT - 1)
            drain()
            nc.vector.memset(acc[:], 0.0)

            def mlp(f, last):
                with dve.Fori(0, 4) as i:
                    for k in range(4):
                        split("mlp", f * 8 + i, k + 1)
                    for b in range(4):
                        dve.wait_ge(hid_lo, f * 16 + i * 4 + (b + 1))
                        blk("mlp", f * 8 + i, 0, b)
                        nc.vector.tensor_scalar_max(sqb[:, b], main[:, b, 0:T], 0.0).then_inc(freed["V"], 1)

                def second(i, n):
                    for k in range(n):
                        split("mlp", f * 8 + i + 4, k + 1)
                    for b in range(4):
                        dst = acc[:, i * 4 + b]
                        drain()
                        blk("mlp", f * 8 + i + 4, 0, b)
                        TT(dst, dst, main[:, b, 0:T], ALU.add).then_inc(freed["V"], 1)

                with dve.Fori(0, 3) as i:
                    second(i, 4)
                second(3, 3 if last else 4)

            with dve.Fori(0, 3) as f:
                mlp(f, False)
            mlp(3, True)

            drain()
            for k in range(KT):
                STT(res[:, k], acc[:, k], mods2[:, 3 * KT + k:3 * KT + k + 1], ax[:, k],
                    ALU.mult, ALU.add).then_inc(res_done, 1)
            drain()

            def to_out(k, gain, shift):
                last = TS(acc[:, k], res[:, k], gain, shift, ALU.mult, ALU.add)
                if k % 4 == 3:
                    last.then_inc(y_out, 1)

            norm(1, V_L2G, V_L2B, to_out)

        @block.tensor
        def _(pe):
            mm = nc.tensor.matmul

            def bank(name, it, panel, b):
                ph = PH[name]
                who, count = ph.bank_free(it, panel, b)
                pe.wait_ge(freed[who], count)

            def weights(name, it, s):
                ph = PH[name]
                pe.wait_ge(lo_made, ph.split_count(it, s))
                return ph.parity(s)

            def three(out, w_hi, w_lo, x_hi, x_lo, start, stop, skip=False):
                mm(out, w_hi, x_hi, start=start, stop=False, skip_group_check=skip)
                mm(out, w_hi, x_lo, start=False, stop=False, skip_group_check=skip)
                return mm(out, w_lo, x_hi, start=False, stop=stop, skip_group_check=skip)

            def panel(name, it, n, first, x, with_ctx=False, ready=None, between=lambda k: None):
                chunks = PH[name].panels[n][0]
                for k in range(chunks):
                    par = weights(name, it, first + k)
                    if ready is not None:
                        ready(k)
                    for b in range(4):
                        if k == 0:
                            bank(name, it, n, b)
                        for j in range(CK):
                            kt = k * CK + j
                            w_hi, w_lo = (w[:, par, j, P * b:P * (b + 1)] for w in (whi, wlo))
                            start, stop = kt == 0, kt == chunks * CK - 1
                            if with_ctx:
                                mm(main[:, b, 0:C], w_hi, hC[:, kt, 0], start=start, stop=False)
                                mm(main[:, b, 0:C], w_hi, hC[:, kt, 1], start=False, stop=False)
                                mm(main[:, b, 0:C], w_lo, hC[:, kt, 0], start=False, stop=stop)
                                last = three(main[:, b, C:], w_hi, w_lo, hL[:, kt, 0], hL[:, kt, 1],
                                             False, stop, skip=True)
                            else:
                                last = three(main[:, b, 0:T], w_hi, w_lo, x[:, kt, 0], x[:, kt, 1], start, stop)
                        if k == chunks - 1:
                            last.then_inc(blk_done, 1)
                    if k < chunks - 1:
                        last.then_inc(w_used, 1)
                    between(k)

            def turn(t):
                pe.wait_ge(freed["A"], t + 1)
                for b in range(4):
                    last = mm(side[:, 0, (4 * t + b) * 2:(4 * t + b) * 2 + 2], am[0:4, t % 2, P * b:P * (b + 1)],
                              cs[0:4, K_SEL:K_SEL + 2], start=True, stop=True)
                return last

            pe.wait_ge(silu_lo, 1)
            for t in range(8):
                for k in range(4):
                    par = weights("ada", 0, 4 * t + k)
                    if k == 0 and t >= 4:
                        bank("ada", 0, t, 0)
                    for j in range(CK):
                        kt = k * CK + j
                        mm(main[:, t % 4], sR[:, kt], whi[:, par, j], start=kt == 0, stop=False)
                        last = mm(main[:, t % 4], sR[:, kt], wlo[:, par, j], start=False, stop=kt == KT - 1)
                    if k < 3:
                        last.then_inc(w_used, 1)
                last.then_inc(blk_done, 1)
                if t:
                    turn(t - 1).then_inc(am_used, 1)
            turn(7).then_inc(mods_ps, 1)

            def inputs_ready(k):
                pe.wait_ge(h_lo, 4 * k + 4)

            for t in range(2):
                for k in range(4):
                    par = weights("vals", 0, 4 * t + k)
                    inputs_ready(k)
                    for b in range(4):
                        if k == 0:
                            bank("vals", 0, t, b)
                        x, tile = (hC, hL)[b // 2], slice(P * (b % 2), P * (b % 2) + P)
                        for j in range(CK):
                            kt = k * CK + j
                            mm(main[:, b], x[:, kt, 0, tile], whi[:, par, j], start=kt == 0, stop=False)
                            mm(main[:, b], x[:, kt, 0, tile], wlo[:, par, j], start=False, stop=False)
                            last = mm(main[:, b], x[:, kt, 1, tile], whi[:, par, j], start=False, stop=kt == KT - 1)
                        if k == 3:
                            last.then_inc(blk_done, 1)
                    if k < 3:
                        last.then_inc(w_used, 1)
            for k in range(4):
                par = weights("vals", 0, 8 + k)
                for b in range(4):
                    if k == 0:
                        bank("vals", 0, 2, b)
                    for j in range(CK):
                        kt = k * CK + j
                        start, stop = kt == 0, kt == KT - 1
                        if b < 2:
                            w_hi, w_lo = (w[:, par, j, P * b:P * (b + 1)] for w in (whi, wlo))
                            three(main[:, b, 0:C], w_hi, w_lo, hC[:, kt, 0], hC[:, kt, 1], start, stop)
                            last = three(main[:, b, C:], w_hi, w_lo, hL[:, kt, 0], hL[:, kt, 1], False, stop, True)
                        else:
                            x = (hC, hL)[b - 2]
                            for tile in range(2):
                                out, cols = main[:, b, 256 * tile:256 * (tile + 1)], slice(P * tile, P * (tile + 1))
                                w_hi, w_lo = whi[:, par, j, 256:512], wlo[:, par, j, 256:512]
                                mm(out, x[:, kt, 0, cols], w_hi, start=start and tile == 0, stop=False,
                                   skip_group_check=tile == 1)
                                mm(out, x[:, kt, 0, cols], w_lo, start=False, stop=False,
                                   skip_group_check=tile == 1)
                                last = mm(out, x[:, kt, 1, cols], w_hi, start=False, stop=stop,
                                          skip_group_check=tile == 1)
                    if k == 3:
                        last.then_inc(blk_done, 1)
                if k < 3:
                    last.then_inc(w_used, 1)

            def ada_turn(n):
                pe.wait_ge(ada_used, n * 4 + 4)
                for b in range(4):
                    last = mm(side[:, 3, bass.ds(n * 4 + (ADA_PS + b), 1)], asum[:, P * b:P * (b + 1)],
                              ones[:, 0:1], start=True, stop=True)
                last.then_inc(asum_ps, 1)

            def keys_and_states(it, k):
                if k == 0:
                    ada_turn(it)
                if k == 2:
                    pe.wait_ge(key_in, it * 4 + 4)
                    for n in range(8):
                        last = nc.tensor.transpose(side[:, n // 4, P * (n % 4):P * (n % 4 + 1)],
                                                   kc[:, n // 2, P * (n % 2):P * (n % 2 + 1)], cs[:, K_ID:K_ID + P])
                    last.then_inc(key_tr, 1)
                if k == 3:
                    pe.wait_ge(key_cp, it + 1)
                    for b in range(4):
                        head = HEADS_OF(it, b)
                        for tile in range(2):
                            last = mm(side[:, 2, HD * b:HD * (b + 1)], kcT[:, C * b + P * tile:C * b + P * (tile + 1)],
                                      vc[:, tile, head], start=tile == 0, stop=tile == 1)
                    last.then_inc(st_ps, 1)

            def HEADS_OF(it, b):
                return bass.ds((it % 2) * PW + HD * b, HD)

            mm(side[0:1, 3, 511:512], ones[:, 0:1], ones[:, 0:1], start=True, stop=True).then_inc(asum_ps, 1)
            panel("forget", 0, 0, 0, None, with_ctx=True)
            with pe.Fori(1, 4) as i:
                panel("forget", i, 0, 0, None, with_ctx=True, between=lambda k: keys_and_states(i - 1, k))
            panel("query", 0, 0, 0, hL, between=lambda k: keys_and_states(3, k) if k == 0 else None)
            panel("query", 0, 1, 4, hL, between=lambda k: keys_and_states(3, k + 2) if k < 2 else None)

            def level(i, k):
                h = LEVELS[k]
                pe.wait_ge(lv_op, i * 9 + (k + 1))
                if k:
                    pe.wait_ge(lv_cp, i * 9 + k)
                for tile in range(2):
                    other = 1 - tile if h == 128 else tile
                    for e in range(4):
                        last = mm(side[:, tile, P * e:P * (e + 1)], lv[k % 2][:, 1, e, P * tile:P * (tile + 1)],
                                  lv[k % 2][:, 0, e, P * other:P * (other + 1)], start=True, stop=True)
                last.then_inc(lv_sc, 1)

            def outputs(i):
                pe.wait_ge(lv_cp, i * 9 + 9)
                pe.wait_ge(o_op, i + 1)
                pe.wait_ge(vg_in, i + 1)
                for e in range(4):
                    out = side[:, 2 + e // 2, T * (e % 2):T * (e % 2 + 1)]
                    cols = slice(HD * e, HD * (e + 1))
                    mm(out, vg[:, 0, cols], pT[:, 0, e], start=True, stop=False)
                    mm(out, vg[:, 1, cols], pT[:, 1, e], start=False, stop=False)
                    mm(out, sg_st[:, 0, cols], lv[0][:, 0, e], start=False, stop=False)
                    last = mm(out, sg_st[:, 1, cols], lv[0][:, 1, e], start=False, stop=True)
                last.then_inc(o_ps, 1)

            with pe.Fori(0, 2) as i:
                def beside(k):
                    if 1 <= k < 10:
                        level(i, k - 1)
                    if k == 10:
                        outputs(i)
                    if k == 11:
                        pe.wait_ge(o_sq, i + 1)
                        for n in range(2):
                            last = mm(side[:, n], ones[:], lv[1][:, 0].rearrange("p e t -> p (e t)")[:, PW * n:PW * (n + 1)],
                                      start=True, stop=True)
                        last.then_inc(o_ms, 1)
                for n in range(3):
                    panel("mix", i, n, 4 * n, hL, between=lambda k, n=n: beside(4 * n + k))

            def branch(j, h, between):
                it = h + 2 * j
                for p in range(2):
                    panel("gates", it, 2 * p, 6 * p, hL, between=lambda k: between(6 * p + k))

                    def after(k):
                        between(6 * p + 4 + k)
                        if k == 1:
                            if j == 0:
                                pe.wait_ge(at_y, h * 4 + (1 + 3 * p))
                            ada_turn(h * 2 + (4 + 4 * j + p))

                    panel("gates", it, 2 * p + 1, 6 * p + 4, yR[j % 2], ready=lambda k: pe.wait_ge(y_lo, j + 1),
                          between=after)

            with pe.Fori(0, 2) as h:
                def attend(k):
                    u = k
                    if u < 8:
                        if u == 0:
                            pe.wait_ge(at_rot, h + 1)
                            pe.wait_ge(o_rs, 2)
                        if u >= 2:
                            pe.wait_ge(at_exp, h * 8 + (u - 1))
                        mm(side[:, u % 2], qr[:, u // 2, P * (u % 2):P * (u % 2 + 1)], ak[:, h],
                           start=True, stop=True).then_inc(at_sc, 1)
                    u = k - 2
                    if 0 <= u < 8:
                        pe.wait_ge(at_norm, h * 8 + (u + 1))
                        if u:
                            pe.wait_ge(at_cp, h * 8 + u)
                        for n in range(4):
                            last = nc.tensor.transpose(side[:, 2, P * n:P * (n + 1)], pr[:, u % 2, P * n:P * (n + 1)],
                                                       cs[:, K_ID:K_ID + P])
                        last.then_inc(at_tr, 1)
                    u = k - 3
                    if 0 <= u < 8 and u % 2:
                        e = u // 2
                        pe.wait_ge(at_cp, h * 8 + (u + 1))
                        if u == 1:
                            pe.wait_ge(at_v, h + 1)
                        if e:
                            pe.wait_ge(at_y, h * 4 + e)
                        for n in range(4):
                            last = mm(side[:, 3, 0:T], avg[:, n], prT[:, e % 2, n], start=n == 0, stop=n == 3)
                        last.then_inc(at_o, 1)
                branch(0, h, attend)
            with pe.Fori(0, 2) as h:
                branch(1, h, lambda k: None)
            pe.wait_ge(pool_diff, 1)
            for b in range(8):
                if b == 7:
                    pe.wait_ge(pool_y, 2)
                out = side[:, (b % 7) // 2, (b % 7) % 2 * T:(b % 7) % 2 * T + T]
                for n in range(2):
                    last = mm(out, pw_sb[:, b // 2 * 2 + n, P * (b % 2):P * (b % 2 + 1)], pd[:, b // 2 * 2 + n],
                              start=n == 0, stop=n == 1)
                last.then_inc(pool_ps, 1)
            with pe.Fori(0, 2) as h:
                branch(2, h, lambda k: None)

            def sums(b, src, start, stop):
                return mm(side[:, b, 0:T], ones[:], src, start=start, stop=stop)

            def squares(n):
                for k in range(KT):
                    if k % 4 == 0:
                        pe.wait_ge(sq_done, 4 * n + k // 4 + 1)
                    last = sums(1, sqb[:, k], k == 0, k == KT - 1)
                last.then_inc(var_ps, 1)

            pe.wait_ge(zero_set, 1)
            sums(0, mu[:], True, False)
            with pe.Fori(0, 4) as i:
                panel("out", i, 0, 0, mR, ready=lambda k: pe.wait_ge(m_lo, k + 1))
                for b in range(4):
                    pe.wait_ge(freed["V"], i * 4 + (PH["out"].f0["V"] + b + 1))
                    sums(0, res[:, i * 4 + b], False, False)
            sums(0, mu[:], False, True).then_inc(mean_ps, 1)
            squares(0)

            with pe.Fori(0, 4) as f:
                with pe.Fori(0, 4) as i:
                    panel("mlp", f * 8 + i, 0, 0, h2, ready=lambda k: pe.wait_ge(h2_lo, 4 * k + 4))
                with pe.Fori(0, 4) as i:
                    panel("mlp", f * 8 + i + 4, 0, 0, hid, ready=lambda k: pe.wait_ge(hid_lo, f * 16 + (4 * k + 8)))
            for k in range(KT):
                pe.wait_ge(res_done, k + 1)
                last = sums(0, res[:, k], k == 0, k == KT - 1)
            last.then_inc(mean_ps, 1)
            squares(1)


def constants():
    cst = np.zeros((P, NK), np.float32)
    cst[:, K_ID:K_ID + P] = np.eye(P)
    q, k = np.arange(P)[:, None], np.arange(P)[None, :]
    cst[:, K_TRI:K_TRI + P] = np.where(k <= q, 0.0, NEG)
    cst[:, K_TRI + P:K_TRI + 2 * P] = np.where(k >= q, 0.0, NEG)
    freq = (10000.0 ** (-np.arange(HD // 4, dtype=np.float32) / (HD // 4))).astype(np.float32)
    t = np.arange(T)
    ang = np.concatenate([(t // GRID_W).astype(np.float32)[:, None] * freq,
                          (t % GRID_W).astype(np.float32)[:, None] * freq], -1).T
    cst[:, K_COS:K_COS + T] = np.concatenate([np.cos(ang)] * 2)
    cst[:, K_SIN:K_SIN + T] = np.concatenate([-np.sin(ang), np.sin(ang)])
    cst[0:4, K_SEL:K_SEL + 2] = np.eye(2)[[0, 1, 0, 1]]
    rcnt = np.zeros((P, 4, T), np.float32)
    for n, w in enumerate(WINDOWS):
        rcnt[:, n] = 1.0 / (np.clip(t + w // 2, 0, T) - np.clip(t - w // 2, 0, T))
    masks = np.zeros((P, 7, P), np.float32)
    for n, size in enumerate((64, 32, 16, 8, 4, 2, 1)):
        masks[:, n] = q // size == k // size
    return cst, rcnt, masks.reshape(P, 7 * P)


def chunks(w):
    K, N = w.shape
    w = w.reshape(K // (CK * P), CK, P, N // PW, PW).transpose(3, 0, 2, 1, 4)
    return np.ascontiguousarray(w).reshape(-1, P, CK * PW)


def columns(v):
    return v.reshape(-1, P).T


def kernel(**inputs):
    import concourse.bacc as bacc
    from concourse.bass_utils import run_bass_kernel_spmd

    a = {k: np.asarray(v) for k, v in inputs.items()}
    cst, rcnt, masks = constants()
    vecs = np.concatenate([columns(a["c"][0]), columns(a["c_ctx"]), columns(a["b_ada"][0]),
                           columns(a["hgrn_norm"][0]), columns(a["pool_scale"][0]), columns(a["ln1_g"][0]),
                           columns(a["ln1_b"][0]), columns(a["ln2_g"][0]), columns(a["ln2_b"][0]),
                           np.broadcast_to(a["attn_sink"][0], (P, HEADS))], axis=1)
    x2 = np.stack([a["ctx"][0], a["x"][0]])
    xT = x2.reshape(2, T, KT, P).transpose(3, 2, 0, 1).reshape(P, KT * 2 * T)
    f2 = a["w_ff2"][0].reshape(4, D, D)
    arrays = {
        "vecs": vecs, "cst": cst, "rcnt": rcnt, "masks": masks, "xT": xT,
        "w_ada": chunks(a["w_ada"][0]), "w_in": chunks(a["w_in"][0]),
        "pool_w": a["pool_w"][0].reshape(8, P, 256).transpose(1, 0, 2),
        "w_br": np.concatenate([chunks(w) for w in a["w_branch"][0]]),
        "w_out": chunks(a["w_out"][0]), "w_f1": chunks(a["w_ff1"][0]),
        "w_f2": np.concatenate([chunks(w) for w in f2]),
    }
    arrays = {f"in_{k}": np.ascontiguousarray(v) for k, v in arrays.items()}
    nc = bacc.Bacc("TRN2", target_bir_lowering=False, num_devices=1, dynamic_dma_scratch_size=1024)
    args = [nc.dram_tensor(k, v.shape, mybir.dt.from_np(v.dtype), kind="ExternalInput").ap()
            for k, v in arrays.items()]
    args.append(nc.dram_tensor("out_0", (P, KT, T), F32, kind="ExternalOutput").ap())
    build(nc, *args)
    r = run_bass_kernel_spmd(nc, [arrays], core_ids=[0])
    out = np.asarray(r.results[0]["out_0"])
    return out.transpose(2, 1, 0).reshape(1, T, D)
```

```python
from contextlib import ExitStack

import numpy as np

import concourse.bass as bass
from concourse import mybir

F32 = mybir.dt.float32
F32R = mybir.dt.float32r
U8 = mybir.dt.uint8
ALU = mybir.AluOpType
ACT = mybir.ActivationFunctionType
AX = mybir.AxisListType.X

P = 128
D = 2048
T = 256
C = 256
KT = D // P
PW = 512
CK = 4
HEADS = 8
HD = 128
GRID_W = 64
ALPHA = 2.0 ** 0.25
LN_EPS = 1e-5
RMS_EPS = 1e-6
SCALE = HD ** -0.5
NEG = -1e30
WINDOWS = (2, 4, 8, 16)
LEVELS = (128, 64, 32, 16, 8, 4, 2, 1, 0)

PAN_AQ, PAN_AI, PAN_AG, PAN_AF, PAN_B, PAN_CQ, PAN_CKV, PAN_GATE = 0, 2, 4, 6, 10, 12, 14, 15

V_C, V_CC, V_BADA, V_NORM, V_PSC, V_L1G, V_L1B, V_L2G, V_L2B, V_SINK, NV = (
    0, 16, 32, 128, 136, 144, 160, 176, 192, 208, 216)
K_ID, K_TRI, K_COS, K_SIN, K_SEL, NK = 0, 128, 384, 640, 896, 898

PAIRED = "sa" * 4
SUMMED = {"gates": (1, 3, 7, 9), "last": (0, 1, 3, 4, 6, 7, 8, 9)}


def gated(name):
    return "".join("sa" if k in SUMMED[name] else "s" for k in range(12))


BRANCHES = (0, 2, 1)

PHASES = [
    ("ada", 1, "s" * 32, [(4, 1, "A")] * 8),
    ("vals", 1, "sa" * 12, [(4, 4, "A")] * 3),
    ("forget", 4, PAIRED, [(4, 4, "A")]),
    ("query", 1, "sss" + "sa" * 4 + "s", [(4, 4, "A"), (4, 4, "V")]),
    ("mix", 2, "s" * 12, [(4, 4, "V"), (4, 4, "A"), (4, 4, "V")]),
    ("gates", 4, gated("gates"), [(4, 4, "A"), (2, 4, "V")] * 2),
    ("last", 2, gated("last"), [(4, 4, "A"), (2, 4, "V")] * 2),
    ("out", 4, "ssss", [(4, 4, "V")]),
    ("mlp", 32, "ssss", [(4, 4, "V")]),
]


class Phase:

    former = None

    def __init__(self, name, n, body, panels, before):
        self.name, self.n, self.body, self.panels = name, n, body, panels
        (self.r0, self.c0, self.a0, self.g0, self.u0, self.f0) = before
        self.at = [l for l, kind in enumerate(body) if kind == "s"] + [len(body)]
        self.ns = body.count("s")
        self.na = body.count("a")
        self.blocks = sum(b for _, b, _ in panels)
        self.u = sum(c - 1 for c, _, _ in panels)
        self.f = {e: sum(b for _, b, x in panels if x == e) for e in "AV"}

    def after(self):
        n = self.n
        return (self.r0 + n * len(self.body), self.c0 + n * self.ns, self.a0 + n * self.na,
                self.g0 + n * self.blocks, self.u0 + n * self.u, {e: self.f0[e] + n * self.f[e] for e in "AV"})

    def raw(self, it, local):
        return (self.r0 + local) % 4, it * (4 * len(self.body)) + 16 * ((self.r0 + local) // 4 + 1)

    def parity(self, s):
        return (self.c0 + s) % 2

    def split_count(self, it, s):
        return it * self.ns + (self.c0 + s + 1)

    def blocks_before(self, it, panel):
        return it * self.blocks + (self.g0 + sum(b for _, b, _ in self.panels[:panel]))

    def released(self, it, s):
        s -= 2
        end, used = 0, 0
        for p, (n, _, _) in enumerate(self.panels):
            if s < end:
                break
            if s < end + n - 1:
                return "w_used", it * self.u + (self.u0 + used + s - end + 1)
            end += n
            used += n - 1
            if s == end - 1:
                return "blk_done", self.blocks_before(it, p + 1)
        return "blk_done", self.blocks_before(it, 0)

    def bank_free(self, it, panel, b):
        n = {e: self.f0[e] + sum(k for _, k, x in self.panels[:panel] if x == e) for e in "AV"}
        who = self.panels[panel - 1][2]
        if isinstance(it, int) and it + panel == 0:
            who = self.former
        return who, it * self.f[who] + (n[who] - 4 + b + 1)


def phases():
    out, before, former = {}, (0, 0, 0, 0, 0, {"A": 0, "V": 0}), None
    for name, n, body, panels in PHASES:
        out[name] = Phase(name, n, body, panels, before)
        out[name].former = former
        before, former = out[name].after(), panels[-1][2]
    return out


PH = phases()
KINDS = "".join(body * n for _, n, body, _ in PHASES)


def reuse_needs(ph, its, local):
    split, sums = [], []
    for it in its:
        before = KINDS[:max(0, ph.r0 + it * len(ph.body) + local - 3)]
        split.append(before.count("s") - it * ph.ns)
        sums.append(before.count("a") - it * ph.na)
    former = {KINDS[max(0, ph.r0 + it * len(ph.body) + local - 4)] for it in its}
    return max(split), max(sums), former


def build(nc, vecs, cst, rcnt, masks, xT, w_ada, w_in, pool_w, w_br, w_out, w_f1, w_f2, outT):
    with ExitStack() as ctx:
        KB = 1024
        SIZE = 222 * KB + 512
        arena = ctx.enter_context(nc.sbuf_tensor("arena", [P, SIZE // 4], F32))
        base = (nc.sbuf_base - SIZE) // 32 * 32

        def at(name, shape, off, dt=F32):
            return nc.alloc_sbuf_tensor_at(name, shape, dt, offset=base + int(off))

        raw = at("raw", [P, 4, CK, PW], 0)
        whi = at("whi", [P, 2, CK, PW], 32 * KB, F32R)
        wlo = at("wlo", [P, 2, CK, PW], 48 * KB, F32R)
        whi2 = at("whi2", [P, 2, CK, PW], 64 * KB, F32R)
        wlo2 = at("wlo2", [P, 2, CK, PW], 80 * KB, F32R)
        hL = at("hL", [P, KT, 2, T], 64 * KB, F32R)
        acc = at("acc", [P, KT, T], 64 * KB)
        hC = at("hC", [P, KT, 2, C], 96 * KB, F32R)
        mk_in = at("mk_in", [P, 7, P], 96 * KB)
        q_t = at("q_t", [P, HEADS, T], 96 * KB)
        ya = at("ya", [P, HEADS, T], 104 * KB)
        cq = at("cq", [P, HEADS, T], 112 * KB)
        xb = at("xb", [P, HEADS, T], 120 * KB)
        pw_sb = at("pw_sb", [P, 8, 256], 96 * KB)
        rc_sb = at("rc_sb", [P, 4, T], 104 * KB)
        ax = at("ax", [P, KT, T], 96 * KB)
        res = at("res", [P, KT, T], 112 * KB)
        xin = at("xin", [P, KT, 2, T], 128 * KB)
        kk = at("kk", [P, 2 * HEADS, T], 128 * KB)
        lf = at("lf", [P, 2 * HEADS, T], 144 * KB)
        mT = at("mT", [P, KT, T], 128 * KB)
        yR = [at("yR0", [P, HEADS, 2, T], 144 * KB, F32R), at("yR1", [P, HEADS, 2, T], 168 * KB, F32R)]
        h2 = at("h2", [P, KT, 2, T], 128 * KB, F32R)
        vl = at("vl", [P, 2, HEADS * HD], 160 * KB)
        vc = at("vc", [P, 2, HEADS * HD], 168 * KB)
        lv = [at("lv0", [P, 2, 4, T], 168 * KB), at("lv1", [P, 2, 4, T], 200 * KB)]
        st = at("st", [P, 2 * HEADS, HD], 176 * KB)
        sR = at("sR", [P, KT, P], 176 * KB, F32R)
        ak = at("ak", [P, 2, C + T], 184 * KB)
        av = at("av", [P, 4, 256], 188 * KB)
        mR = at("mR", [P, KT, 2, T], 160 * KB, F32R)
        hid = at("hid", [P, KT, 2, T], 160 * KB, F32R)
        am = at("am", [P, 2, PW], 192 * KB)
        ht = at("ht", [P, 2, 2, T], 196 * KB)
        z4 = at("z4", [P, 4, C + T], 192 * KB)
        kc = at("kc", [P, 4, C], 200 * KB)
        kcT = at("kcT", [P, 4 * C], 204 * KB)
        zLs = [at("zL0", [P, C + T], 208 * KB), at("zL1", [P, C + T], 212 * KB)]
        zm = at("zm", [P, C + T], 214 * KB)
        pT = at("pT", [P, 2, 4, T], 192 * KB)
        qr = at("qr", [P, 4, T], 192 * KB)
        qs = at("qs", [P, 4, T], 162 * KB)
        pr = at("pr", [P, 2, C + T], 196 * KB)
        prT = at("prT", [P, 2, 4, T], 200 * KB)
        ks = at("ks", [P, 2, T], 160 * KB)
        gz = at("gz", [P, 2, T], 192 * KB)
        pin = at("pin", [P, 2, 272], 160 * KB)
        win = [at("win0", [P, 2, 272], 160 * KB + 2304), at("win1", [P, 2, 272], 160 * KB + 4608)]
        pd = at("pd", [P, HEADS, T], 200 * KB)
        sqb = at("sqb", [P, KT, T], 192 * KB)
        h4 = at("h4", [P, 4, T], 204 * KB)
        vg = at("vg", [P, 2, PW], 208 * KB)
        sg_st = at("sg_st", [P, 2, PW], 212 * KB)
        avg = at("avg", [P, 4, HD], 208 * KB)
        asum = at("asum", [P, PW], 210 * KB)
        sg = at("sg", [P, 4, T], 212 * KB)
        mu = at("mu", [P, T], 208 * KB)
        rstd = at("rstd", [P, T], 209 * KB)
        cs = at("cs", [P, NK], 216 * KB)
        vv = at("vv", [P, NV], 216 * KB + 3616)
        mk = at("mk", [P, 7, P], 216 * KB + 4480, U8)
        sm = at("sm", [P, 2, KT], 216 * KB + 5376)
        mods1 = at("mods1", [P, 2 * KT, 2], 216 * KB + 5504)
        mods2 = at("mods2", [P, 4 * KT], 216 * KB + 5760)
        col = at("col", [P, 2, 8], 216 * KB + 6080)
        ones = at("ones", [P, P], 222 * KB)

        main = ctx.enter_context(nc.psum_tensor("main", [P, 4, 512], F32))
        side = ctx.enter_context(nc.psum_tensor("side", [P, 4, 512], F32))
        ADA_PS = 448

        def sem(name):
            return ctx.enter_context(nc.semaphore(name))

        raw_full = [sem(f"raw_full{i}") for i in range(4)]
        hi_made, lo_made, ada_used = sem("hi_made"), sem("lo_made"), sem("ada_used")
        released = {"w_used": sem("w_used"), "blk_done": sem("blk_done")}
        w_used, blk_done = released["w_used"], released["blk_done"]
        freed = {"A": sem("freed_by_act"), "V": sem("freed_by_dve")}
        (cst_in, x_in, pool_ld, ax_ld, stored, silu_sig, silu_in, silu_hi, silu_lo, mods_ps, h_tmp, h_hi, h_lo,
         am_used, z_log, z_arg, key_in, key_tr, key_cp, st_ps, st_cp, asum_ps, lv_arg, lv_exp,
         lv_op, lv_sc, lv_cp, vg_in, o_exp, o_op, o_ps, o_sq, o_ms, o_rs, y_done, gs_sig, at_sw, at_rot, at_v,
         at_sc, at_max, at_exp, at_norm, at_tr, at_cp, at_o, at_y, zero_set, y_lo, pool_diff, pool_ps,
         pool_y, m_done, m_lo, ax_in, mean_ps, mu_in, cen_done, sq_done, var_ps, rstd_in, h2_tmp, h2_hi,
         h2_lo, acc_zero, hid_lo, passed, res_done, y_out, cleared) = (sem(x) for x in (
            "cst_in x_in pool_ld ax_ld stored silu_sig silu_in silu_hi silu_lo mods_ps h_tmp h_hi h_lo "
            "am_used z_log z_arg key_in key_tr key_cp st_ps st_cp asum_ps lv_arg lv_exp "
            "lv_op lv_sc lv_cp vg_in o_exp o_op o_ps o_sq o_ms o_rs y_done gs_sig at_sw at_rot at_v "
            "at_sc at_max at_exp at_norm at_tr at_cp at_o at_y zero_set y_lo pool_diff pool_ps "
            "pool_y m_done m_lo ax_in mean_ps mu_in cen_done sq_done var_ps rstd_in h2_tmp h2_hi "
            "h2_lo acc_zero hid_lo passed res_done y_out cleared").split())

        def wait(eng, semaphore, value):
            eng.wait_ge(semaphore, value)
            if not isinstance(value, int):
                eng.sem_inc(passed, 1)

        def head_blocks(t, g, h):
            return t[:, bass.ts(g, 4)].rearrange("p e (n a h) -> p (e n) a h", a=2, h=h)

        def level_blocks(t, h):
            return t.rearrange("p e (n a h) -> p (e n) a h", a=2, h=h)

        def branch_phase(j, h):
            return ("gates", h + 2 * j) if j < 2 else ("last", h)

        def split_place(name, s):
            if name == "ada" and s < 32 and s % 4 >= 2:
                return whi2[:, s % 2], wlo2[:, s % 2]
            par = PH[name].parity(s)
            return whi[:, par], wlo[:, par]

        def keys_of(unit):
            return slice(384, 512) if unit % 2 == 0 else slice(256, 384)

        block = ctx.enter_context(nc.Block())

        @block.sync
        def _(sp):
            def load(name, it, local, src, its=None):
                ph = PH[name]
                split, sums, former = reuse_needs(ph, its or (it,), local)
                slot, _ = ph.raw(0, local)
                first = its[0] if its else it
                if "s" in former and first * ph.ns + split > 0:
                    wait(sp, lo_made, it * ph.ns + split)
                if "a" in former:
                    wait(sp, ada_used, it * ph.na + sums)
                sp.dma_start(raw[:, slot].rearrange("p a b -> p (a b)"), src).then_inc(raw_full[slot], 16)

            for n in range(32):
                load("ada", 0, n, w_ada[n])
            for n, panel in enumerate((PAN_AI, PAN_AI + 1, PAN_CKV)):
                for k in range(4):
                    load("vals", 0, 8 * n + 2 * k, w_in[4 * panel + k])
                    load("vals", 0, 8 * n + 2 * k + 1, w_ada[32 + 4 * n + k])

            def forget(i, its):
                for k in range(4):
                    load("forget", i, 2 * k, w_in[i * 4 + (4 * PAN_AF + k)], its)
                    load("forget", i, 2 * k + 1, w_ada[i * 4 + (44 + k)], its)

            forget(0, None)
            with sp.Fori(1, 4) as i:
                forget(i, (1, 2, 3))
            local = 0
            for n in range(8):
                load("query", 0, local, w_in[4 * PAN_AQ + n])
                local += 1
                if 3 <= n < 7:
                    load("query", 0, local, w_ada[60 + n - 3])
                    local += 1
            with sp.Fori(0, 2) as i:
                for n, panel in enumerate((PAN_AG, PAN_CQ, PAN_B)):
                    for k in range(4):
                        load("mix", i, 4 * n + k, w_in[i * 4 + (4 * panel + k)], (0, 1))
            for j, branch in enumerate(BRANCHES):
                name, its = ("gates", (2 * j, 2 * j + 1)) if j < 2 else ("last", (0, 1))
                with sp.Fori(0, 2) as h:
                    _, it = branch_phase(j, h)
                    local = summed = 0
                    for k in range(12):
                        p, q = k // 6, k % 6
                        if q < 4:
                            src = w_in[h * 8 + (4 * (PAN_GATE + 4 * branch + p) + q)]
                        else:
                            src = w_br[h * 4 + (8 * branch + 2 * p + q - 4)]
                        load(name, it, local, src, its)
                        local += 1
                        if k in SUMMED[name]:
                            n = len(SUMMED[name])
                            load(name, it, local, w_ada[h * n + (64 + 8 * j + summed)], its)
                            local += 1
                            summed += 1
            with sp.Fori(0, 4) as i:
                for k in range(4):
                    load("out", i, k, w_out[i * 4 + k], range(4))
            with sp.Fori(0, 4) as f:
                for half, w in enumerate((w_f1, w_f2)):
                    with sp.Fori(0, 4) as i:
                        for k in range(4):
                            load("mlp", f * 8 + i + 4 * half, k, w[f * 16 + i * 4 + k], range(32))

        @block.scalar
        def _(act):
            A = nc.scalar.activation
            drain = nc.scalar.drain

            def split(name, it, s):
                ph = PH[name]
                slot, full = ph.raw(it, ph.at[s])
                wait(act, raw_full[slot], full)
                ahead = 2 if name == "ada" and s < 32 else 0
                if name != "ada" or s >= 4:
                    which, count = ph.released(it, s - ahead)
                    wait(act, released[which], count)
                nc.scalar.copy(split_place(name, s)[0], raw[:, slot]).then_inc(hi_made, 1)

            def blk(name, it, panel, b):
                wait(act, blk_done, PH[name].blocks_before(it, panel) + (b + 1))

            act.dma_start(vv[:], vecs).then_inc(cst_in, 16)
            act.dma_start(cs[:], cst).then_inc(cst_in, 16)
            act.dma_start(mk_in[:].rearrange("p a b -> p (a b)"), masks).then_inc(cst_in, 16)
            act.dma_start(xin[:].rearrange("p k v t -> p (k v t)"), xT).then_inc(x_in, 16)
            wait(act, cst_in, 48)
            A(sm[:].rearrange("p v k -> p (v k)"), vv[:, V_C:V_C + 2 * KT], ACT.Sigmoid).then_inc(silu_sig, 1)
            wait(act, silu_in, 1)
            nc.scalar.copy(sR[:, :, 0:2], sm[:].rearrange("p v k -> p k v")).then_inc(silu_hi, 1)

            split("ada", 0, 0)
            def sums_out(t):
                blk("ada", 0, t, 0)
                if t >= 2:
                    wait(act, am_used, t - 1)
                nc.scalar.copy(am[0:4, t % 2], main[0:4, t % 4]).then_inc(freed["A"], 1)

            for n in range(32):
                split("ada", 0, n + 1)
                if n % 4 == 1 and n > 4:
                    sums_out(n // 4 - 1)
            sums_out(7)

            for t in range(3):
                for k in range(4):
                    split("vals", 0, 4 * t + k + 1)
                    if t == 0 and k == 0:
                        for kt in range(KT):
                            wait(act, h_tmp, kt + 1)
                            nc.scalar.copy(hC[:, kt, 0], ht[:, kt % 2, 0])
                            nc.scalar.copy(hL[:, kt, 0], ht[:, kt % 2, 1]).then_inc(h_hi, 1)
                for b in range(4):
                    blk("vals", 0, t, b)
                    if t < 2:
                        dst = (vc, vl)[b // 2][:, b % 2, PW * t:PW * (t + 1)]
                    elif b < 2:
                        dst = ak[:, b]
                    else:
                        dst = av[:, 2 * (b - 2):2 * (b - 1)].rearrange("p a n -> p (a n)")
                    nc.scalar.copy(dst, main[:, b]).then_inc(freed["A"], 1)

            def key_copy(it):
                wait(act, key_tr, it + 1)
                nc.scalar.copy(kcT[:], side[:, 0:2].rearrange("p a b -> p (a b)")).then_inc(key_cp, 1)

            def state_copy(it):
                wait(act, st_ps, it + 1)
                nc.scalar.copy(st[:, bass.ts(it, 4)].rearrange("p a b -> p (a b)"), side[:, 2]).then_inc(st_cp, 1)

            def gate_log(it, b):
                L = zLs[b % 2]
                drain()
                A(L[:], z4[:, b], ACT.Abs)
                drain()
                A(L[:], L[:], ACT.Exp, scale=-1.0)
                drain()
                A(L[:], L[:], ACT.Ln, bias=1.0).then_inc(z_log, 1)

            def gate_keys(it, b):
                wait(act, z_arg, it * 4 + (b + 1))
                A(kk[:, it * 4 + b], zm[:, C:], ACT.Exp, scale=-1.0)
                A(kc[:, b], zLs[b % 2][:, 0:C], ACT.Exp).then_inc(key_in, 1)

            def logits_out(it):
                drain()
                for b in range(4):
                    blk("forget", it, 0, b)
                    nc.scalar.copy(z4[:, b], main[:, b]).then_inc(freed["A"], 1)

            nc.scalar.preload_act_table_set("natural_log_exp_and_others")
            def forget(it, second):
                for k in range(4):
                    split("forget", it, k + 1)
                    if second and k == 0:
                        key_copy(it - 2)
                    if second and k == 1:
                        state_copy(it - 2)
                    if k:
                        gate_keys(it - 1, k - 1)
                    gate_log(it - 1, k)
                gate_keys(it - 1, 3)
                logits_out(it)

            for k in range(4):
                split("forget", 0, k + 1)
            logits_out(0)
            forget(1, False)
            with act.Fori(2, 4) as i:
                forget(i, True)

            for k in range(8):
                split("query", 0, k + 1)
                if k == 0:
                    key_copy(2)
                if k == 1:
                    state_copy(2)
                if 1 <= k < 5:
                    gate_keys(3, k - 1)
                if k < 4:
                    gate_log(3, k)
                if k == 3:
                    for b in range(4):
                        blk("query", 0, 0, b)
                        nc.scalar.copy(q_t[:, b], main[:, b, 0:T]).then_inc(freed["A"], 1)
                if k == 5:
                    key_copy(3)
                if k == 6:
                    state_copy(3)

            def inverse_rms(i):
                wait(act, o_ms, i + 1)
                A(lv[1][:, 1].rearrange("p e t -> p (e t)"), side[:, 0:2].rearrange("p a b -> p (a b)"),
                  ACT.Ln, scale=1.0 / HD, bias=RMS_EPS)
                drain()
                A(lv[1][:, 1], lv[1][:, 1], ACT.Exp, scale=-0.5).then_inc(o_rs, 1)

            def swap(h):
                g4 = cq[:, 4 * h:4 * h + 4]
                drain()
                nc.scalar.copy(qs[0:64], g4[64:128])
                nc.scalar.copy(qs[64:128], g4[0:64])
                nc.scalar.copy(ks[0:64, 0], ak[64:128, h, C:])
                nc.scalar.copy(ks[64:128, 0], ak[0:64, h, C:]).then_inc(at_sw, 1)

            for i in range(2):
                for k in range(12):
                    split("mix", i, k + 1)
                    if i and k == 0:
                        inverse_rms(0)
                    if k < 8:
                        wait(act, lv_arg, i * 8 + (k + 1))
                        t = lv[k % 2][:].rearrange("p a e t -> p (a e t)")
                        A(t, t, ACT.Exp).then_inc(lv_exp, 1)
                    if k == 10:
                        wait(act, lv_sc, i * 9 + 9)
                        A(lv[0][:, 0], lf[:, bass.ts(i, 4)], ACT.Exp)
                        A(lv[0][:, 1], lf[:, bass.ts(i + 2, 4)], ACT.Exp).then_inc(o_exp, 1)
                    if k == 11:
                        wait(act, o_ps, i + 1)
                        A(lv[1][:, 0].rearrange("p e t -> p (e t)"), side[:, 2:4].rearrange("p a b -> p (a b)"),
                          ACT.Square).then_inc(o_sq, 1)
                    if k % 4 == 3 and k < 8:
                        for b in range(4):
                            blk("mix", i, k // 4, b)
                            if k == 3:
                                A(ya[:, i * 4 + b], main[:, b, 0:T], ACT.Sigmoid).then_inc(gs_sig, 1)
                            else:
                                nc.scalar.copy(cq[:, i * 4 + b], main[:, b, 0:T]).then_inc(freed["A"], 1)
            wait(act, vg_in, 2)
            swap(0)

            def gates(j, h, between):
                name, it = branch_phase(j, h)
                for k in range(12):
                    split(name, it, k + 1)
                    between(k)
                    if k in (3, 9):
                        p = k // 6
                        for b in range(4):
                            blk(name, it, 2 * p, b)
                            A(sg[:, b], main[:, b, 0:T], ACT.Sigmoid).then_inc(freed["A"], 1)

            for h in range(2):
                def attend(k):
                    if h == 0 and k == 0:
                        inverse_rms(1)
                    if h == 0 and k == 5:
                        wait(act, y_lo, 1)
                        act.dma_start(pw_sb[:], pool_w).then_inc(pool_ld, 16)
                        act.dma_start(rc_sb[:], rcnt).then_inc(pool_ld, 16)
                    if h == 0 and k == 8:
                        wait(act, at_rot, 1)
                        swap(1)
                    if 5 <= k <= 11 and k % 2 == 1:
                        e = (k - 5) // 2
                        wait(act, at_o, h * 4 + (e + 1))
                        nc.scalar.copy(cq[:, h * 4 + e], side[:, 3, 0:T]).then_inc(at_y, 1)
                    u = k - 3
                    if 0 <= u < 8:
                        wait(act, at_tr, h * 8 + (u + 1))
                        nc.scalar.copy(prT[:, (u // 2) % 2, :, (u % 2) * P:(u % 2 + 1) * P],
                                       side[:, 2].rearrange("p (a b) -> p a b", a=4)).then_inc(at_cp, 1)
                    u = k - 2
                    if 0 <= u < 8:
                        wait(act, at_max, h * 8 + (u + 1))
                        c = col[:, u % 2]
                        A(pr[:, u % 2], side[:, u % 2], ACT.Exp, bias=c[:, 2:3], scale=SCALE,
                          accum_out=c[:, 3:4])
                        sink = h * 4 + (V_SINK + u // 2)
                        A(c[:, 4:5], vv[:, bass.ds(sink, 1)], ACT.Exp, bias=c[:, 2:3]).then_inc(at_exp, 1)
                gates(0, h, attend)
            with act.Fori(0, 2) as h:
                gates(1, h, lambda k: None)
            for b in range(8):
                wait(act, pool_ps, b // 2 * 2 + 2 if b < 6 else b + 1)
                A(xb[:, b], side[:, (b % 7) // 2, (b % 7) % 2 * T:(b % 7) % 2 * T + T], ACT.Identity,
                  scale=vv[:, V_PSC + b:V_PSC + b + 1]).then_inc(pool_y, 1)
            act.dma_start(ax[:], xT.rearrange("p (k v t) -> p k v t", v=2, t=T)[:, :, 1]).then_inc(ax_ld, 16)
            with act.Fori(0, 2) as h:
                def residual(k):
                    if k == 5:
                        wait(act, ax_ld, 16)
                        nc.scalar.mul(ax[:, bass.ts(h, 8)], ax[:, bass.ts(h, 8)], ALPHA).then_inc(ax_in, 1)
                gates(2, h, residual)

            with act.Fori(0, 4) as i:
                for k in range(4):
                    split("out", i, k + 1)

            def norm(n):
                nc.scalar.preload_act_table_set("natural_log_exp_and_others")
                wait(act, mean_ps, n + 1)
                A(mu[:], side[:, 0, 0:T], ACT.Copy, scale=1.0 / D).then_inc(mu_in, 1)
                for q in range(4):
                    wait(act, cen_done, 4 * n + q + 1)
                    A(sqb[:, 4 * q:4 * q + 4], res[:, 4 * q:4 * q + 4], ACT.Square).then_inc(sq_done, 1)
                wait(act, var_ps, n + 1)
                A(rstd[:], side[:, 1, 0:T], ACT.Ln, scale=1.0 / D, bias=LN_EPS)
                drain()
                A(rstd[:], rstd[:], ACT.Exp, scale=-0.5).then_inc(rstd_in, 1)

            split("mlp", 0, 1)
            norm(0)
            for q in range(4):
                if q == 3:
                    split("mlp", 0, 2)
                wait(act, h2_tmp, q + 1)
                for k in range(4 * q, 4 * q + 4):
                    last = A(h2[:, k, 0], res[:, k], ACT.Identity, scale=mods2[:, 2 * KT + k:2 * KT + k + 1],
                             bias=mods2[:, KT + k:KT + k + 1])
                last.then_inc(h2_hi, 1)
                for k in range(4 * q, 4 * q + 4):
                    A(ax[:, k], res[:, k], ACT.Identity, scale=vv[:, V_L1G + k:V_L1G + k + 1],
                      bias=vv[:, V_L1B + k:V_L1B + k + 1])

            def mlp(f, last):
                if isinstance(f, int) and f == 0:
                    for k in (2, 3):
                        split("mlp", 0, k + 1)
                with act.Fori(1 if isinstance(f, int) and f == 0 else 0, 4) as i:
                    for k in range(4):
                        split("mlp", f * 8 + i, k + 1)
                with act.Fori(0, 3) as i:
                    for k in range(4):
                        split("mlp", f * 8 + i + 4, k + 1)
                for k in range(3 if last else 4):
                    split("mlp", f * 8 + 7, k + 1)

            mlp(0, False)
            with act.Fori(1, 3) as f:
                mlp(f, False)
            mlp(3, True)
            norm(1)
            for q in range(4):
                wait(act, y_out, q + 1)
                act.dma_start(outT[:, 4 * q:4 * q + 4], acc[:, 4 * q:4 * q + 4]).then_inc(stored, 16)
            wait(act, stored, 64)

        @block.gpsimd
        def _(pool):
            nc.gpsimd.memset(sR[:].rearrange("p k n -> p (k n)").bitcast(F32), 0.0).then_inc(cleared, 1)
            pool.wait_ge(cst_in, 48)
            nc.gpsimd.tensor_copy(mk[:], mk_in[:]).then_inc(cleared, 1)
            TT = nc.gpsimd.tensor_tensor
            drain = nc.gpsimd.drain

            def two_parts(out, src, count):
                one = ones[:, 0:1] if len(src.shape) == 2 else ones[:, 0:1].unsqueeze(2)
                one = one.to_broadcast(list(src.shape))
                TT(out[0], src, one, ALU.mult)
                drain()
                TT(out[1], src, out[0].bitcast(F32), ALU.subtract).then_inc(count, 1)

            def level_args(i, k):
                h = LEVELS[k]
                f, w = head_blocks(lf, i, h), head_blocks(lf, i + 2, h)
                q, key = level_blocks(lv[k % 2][:, 0], h), level_blocks(lv[k % 2][:, 1], h)
                shape = [P, q.shape[1], h]
                f_mid = f[:, :, 0, h - 1:h].to_broadcast(shape)
                w_mid = w[:, :, 1, 0:1].to_broadcast(shape)
                TT(q[:, :, 1], f[:, :, 1], f_mid, ALU.subtract)
                TT(q[:, :, 0], w[:, :, 0], w_mid, ALU.subtract)
                TT(key[:, :, 0], f_mid, f[:, :, 0], ALU.subtract)
                TT(key[:, :, 1], w_mid, w[:, :, 1], ALU.subtract).then_inc(lv_arg, 1)

            pool.wait_ge(st_cp, 4)
            for i in range(2):
                for k in range(8):
                    if k >= 2:
                        pool.wait_ge(lv_sc, i * 9 + (k - 1))
                    elif i:
                        pool.wait_ge((o_ps, y_done)[k], i)
                    level_args(i, k)
                drain()
                if i == 0:
                    pool.wait_ge(asum_ps, 9)
                nc.gpsimd.tensor_copy(vg[:], vl[:, :, bass.ts(i, PW)])
                nc.gpsimd.tensor_copy(sg_st[:, 0], st[:, bass.ts(i, 4)].rearrange("p e d -> p (e d)"))
                nc.gpsimd.tensor_copy(sg_st[:, 1],
                                      st[:, bass.ts(i + 2, 4)].rearrange("p e d -> p (e d)")).then_inc(vg_in, 1)

            def rotate(h):
                cos, sin = cs[:, K_COS:K_COS + T], cs[:, K_SIN:K_SIN + T]
                cos4 = cos.unsqueeze(1).to_broadcast([P, 4, T])
                sin4 = sin.unsqueeze(1).to_broadcast([P, 4, T])
                pool.wait_ge(at_sw, h + 1)
                if h:
                    pool.wait_ge(at_sc, 8)
                TT(qr[:], cq[:, 4 * h:4 * h + 4], cos4, ALU.mult)
                TT(qs[:], qs[:], sin4, ALU.mult)
                TT(ks[:, 1], ak[:, h, C:], cos, ALU.mult)
                TT(ks[:, 0], ks[:, 0], sin, ALU.mult)
                drain()
                TT(qr[:], qr[:], qs[:], ALU.add)
                TT(ak[:, h, C:], ks[:, 0], ks[:, 1], ALU.add).then_inc(at_rot, 1)

            def group_values(h):
                nc.gpsimd.tensor_copy(avg[:], av[:, :, HD * h:HD * (h + 1)]).then_inc(at_v, 1)

            rotate(0)
            pool.wait_ge(o_ps, 2)
            group_values(0)
            pool.wait_ge(y_done, 2)
            two_parts([yR[0][:, :, n] for n in range(2)], ya[:], y_lo)
            rotate(1)
            pool.wait_ge(at_o, 4)
            group_values(1)
            pool.wait_ge(at_y, 8)
            drain()
            two_parts([yR[1][:, :, n] for n in range(2)], cq[:], y_lo)

            pool.wait_ge(pool_ld, 32)
            nc.gpsimd.memset(pin[:], 0.0)
            for n in range(4):
                x2 = xb[:, 2 * n:2 * n + 2]
                drain()
                nc.gpsimd.tensor_copy(pin[:, :, 8:8 + T], x2)
                src, lo, hi = pin, 0, 272
                for step in range(n + 1):
                    left = right = 1 << max(step - 1, 0)
                    if step == 0:
                        left, right = 1, 0
                    lo, hi = lo + left, hi - right
                    drain()
                    TT(win[step % 2][:, :, lo:hi], src[:, :, lo - left:hi - left], src[:, :, lo + right:hi + right],
                       ALU.add)
                    src = win[step % 2]
                drain()
                d2 = pd[:, 2 * n:2 * n + 2]
                TT(d2, src[:, :, 8:8 + T], rc_sb[:, n:n + 1].to_broadcast([P, 2, T]), ALU.mult)
                drain()
                last = TT(d2, d2, x2, ALU.subtract)
            last.then_inc(pool_diff, 1)
            pool.wait_ge(pool_y, 8)
            two_parts([yR[0][:, :, n] for n in range(2)], xb[:], y_lo)

            with pool.Fori(0, 2) as h:
                for p in range(2):
                    rows = bass.ds(h * 8 + 4 * p, 4)
                    drain()
                    wait(pool, m_done, h * 8 + (4 * p + 4))
                    two_parts([mR[:, rows, n] for n in range(2)], mT[:, rows], m_lo)

            nc.gpsimd.memset(acc[:], 0.0).then_inc(acc_zero, 1)

            pool.sem_inc(hid_lo, 4)
            with pool.Fori(0, 4) as f:
                with pool.Fori(0, 4) as i:
                    for b in range(4):
                        drain()
                        wait(pool, freed["V"], f * 32 + i * 4 + (PH["mlp"].f0["V"] + b + 1))
                        TT(sqb[:, b], sqb[:, b], sqb[:, b], ALU.mult)
                        drain()
                        two_parts([hid[:, i * 4 + b, n] for n in range(2)], sqb[:, b], hid_lo)

        @block.vector
        def _(dve):
            TT, TS, STT = nc.vector.tensor_tensor, nc.vector.tensor_scalar, nc.vector.scalar_tensor_tensor
            drain = nc.vector.drain

            def split(name, it, s):
                ph = PH[name]
                dve.wait_ge(hi_made, ph.split_count(it, s))
                slot = ph.raw(0, ph.at[s])[0]
                hi, lo = split_place(name, s)
                TT(lo, raw[:, slot], hi.bitcast(F32), ALU.subtract).then_inc(lo_made, 1)

            def blk(name, it, panel, b):
                dve.wait_ge(blk_done, PH[name].blocks_before(it, panel) + (b + 1))

            def ada_sum(name, it, local, n, k):
                slot, full = PH[name].raw(it, local)
                wait(dve, raw_full[slot], full)
                if k == 0:
                    dve.wait_ge(asum_ps, n + 1)
                for j in range(CK):
                    s = sm[:, 0, k * CK + j:k * CK + j + 1]
                    if k == 0 and j == 0:
                        last = TS(asum[:], raw[:, slot, j], s, None, ALU.mult)
                    else:
                        drain()
                        last = STT(asum[:], raw[:, slot, j], s, asum[:], ALU.mult, ALU.add)
                last.then_inc(ada_used, 1)

            nc.vector.memset(ones[:], 1.0)
            dve.wait_ge(silu_sig, 1)
            dve.wait_ge(cleared, 1)
            TT(sm[:].rearrange("p v k -> p (v k)"), sm[:].rearrange("p v k -> p (v k)"), vv[:, V_C:V_C + 2 * KT],
               ALU.mult).then_inc(silu_in, 1)
            dve.wait_ge(silu_hi, 1)
            TT(sR[:, :, 2:4], sm[:].rearrange("p v k -> p k v"), sR[:, :, 0:2].bitcast(F32),
               ALU.subtract).then_inc(silu_lo, 1)
            for s in range(33):
                split("ada", 0, s)

            def modulate():
                dve.wait_ge(mods_ps, 1)
                TT(mods1[:], side[:, 0, 0:64].rearrange("p (c v) -> p c v", v=2),
                   vv[:, V_BADA:V_BADA + 32].unsqueeze(2).to_broadcast([P, 32, 2]), ALU.add)
                drain()
                TS(mods1[:, KT:], mods1[:, KT:], 1.0, None, ALU.add)
                drain()
                dve.wait_ge(x_in, 16)
                dve.wait_ge(cleared, 2)

                def lo(k):
                    dve.wait_ge(h_hi, k + 1)
                    TT(hC[:, k, 1], ht[:, k % 2, 0], hC[:, k, 0].bitcast(F32), ALU.subtract)
                    TT(hL[:, k, 1], ht[:, k % 2, 1], hL[:, k, 0].bitcast(F32), ALU.subtract).then_inc(h_lo, 1)

                for k in range(KT):
                    if k >= 2:
                        drain()
                    TS(ht[:, k % 2, 0], xin[:, k, 0], mods1[:, KT + k, 1:2], mods1[:, k, 1:2], ALU.mult, ALU.add)
                    TS(ht[:, k % 2, 1], xin[:, k, 1], mods1[:, KT + k, 0:1], mods1[:, k, 0:1],
                       ALU.mult, ALU.add).then_inc(h_tmp, 1)
                    if k:
                        lo(k - 1)
                lo(KT - 1)

            for s in range(1, 13):
                split("vals", 0, s)
                if s == 1:
                    modulate()
                ada_sum("vals", 0, 2 * s - 1, (s - 1) // 4, (s - 1) % 4)

            def gate_block(it, b, backward):
                L, z = zLs[b % 2], z4[:, b]
                drain()
                dve.wait_ge(z_log, it * 4 + (b + 1))
                if b:
                    dve.wait_ge(key_in, it * 4 + b)
                STT(zm[:], z, 0.0, L[:], ALU.max, ALU.add)
                STT(z, z, 0.0, L[:], ALU.min, ALU.subtract)
                drain()
                one = ones[:, 0:1].to_broadcast([P, C])
                dst, lat, ctx_f = lf[:, it * 4 + b], z4[:, b, C:], z4[:, b, 0:C]
                if backward:
                    back = L[:, C:]
                    nc.vector.tensor_tensor_scan(back[:, ::-1], one, lat[:, ::-1], 0.0, ALU.mult, ALU.add)
                    nc.vector.memset(L[:, 0:1], 0.0)
                    nc.vector.tensor_tensor_scan(L[:, 1:C], one[:, 1:], ctx_f[:, 0:C - 1], 0.0,
                                                 ALU.mult, ALU.add)
                else:
                    nc.vector.tensor_tensor_scan(dst, one, lat, 0.0, ALU.mult, ALU.add)
                    nc.vector.memset(L[:, C - 1:C], 0.0)
                    nc.vector.tensor_tensor_scan(L[:, 0:C - 1][:, ::-1], one[:, 1:], ctx_f[:, 1:][:, ::-1], 0.0,
                                                 ALU.mult, ALU.add)
                drain()
                if backward:
                    nc.vector.tensor_copy(dst, back)
                TT(L[:, 0:C], L[:, 0:C], zm[:, 0:C], ALU.subtract).then_inc(z_arg, 1)

            def forget(it, backward):
                for k in range(4):
                    split("forget", it, k + 1)
                    ada_sum("forget", it, 2 * k + 1, it + 3, k)
                    if backward is not None:
                        gate_block(it - 1, k, backward)

            forget(0, None)
            with dve.Fori(1, 3) as i:
                forget(i, False)
            forget(3, True)

            for k in range(8):
                split("query", 0, k + 1)
                if k < 4:
                    gate_block(3, k, True)
                if 3 <= k < 7:
                    ada_sum("query", 0, 4 + 2 * (k - 3), 7, k - 3)
            for b in range(4):
                blk("query", 0, 1, b)
                nc.vector.tensor_copy(q_t[:, 4 + b], main[:, b, 0:T]).then_inc(freed["V"], 1)

            def level_operands(i, k):
                h = LEVELS[k]
                t = lv[k % 2]
                q4 = q_t[:, bass.ts(i, 4)]
                if h:
                    dve.wait_ge(lv_exp, i * 8 + (k + 1))
                    kf, kb = head_blocks(kk, i, h), head_blocks(kk, i + 2, h)
                    key = level_blocks(t[:, 1], h)
                    TT(t[:, 0], t[:, 0], q4, ALU.mult)
                    TT(key[:, :, 0], key[:, :, 0], kf[:, :, 0], ALU.mult)
                    TT(key[:, :, 1], key[:, :, 1], kb[:, :, 1], ALU.mult).then_inc(lv_op, 1)
                else:
                    drain()
                    nc.vector.tensor_copy(t[:, 0], q4)
                    TT(t[:, 1], kk[:, bass.ts(i, 4)], kk[:, bass.ts(i + 2, 4)], ALU.add).then_inc(lv_op, 1)

            def level_scores(i, k):
                h = LEVELS[k]
                drain()
                wait(dve, lv_sc, i * 9 + (k + 1))
                for tile in range(2):
                    src = side[:, tile].rearrange("p (e t) -> p e t", e=4)
                    cols = 1 - tile if h == 128 else tile
                    dst = pT[:, tile, :, cols * P:(cols + 1) * P]
                    if h >= 64:
                        last = nc.vector.tensor_copy(dst, src)
                    else:
                        last = nc.vector.copy_predicated(dst, mk[:, k - 2:k - 1].to_broadcast([P, 4, P]), src)
                last.then_inc(lv_cp, 1)

            def outputs(i):
                wait(dve, o_rs, i + 1)
                t = lv[1][:, 1].rearrange("p e t -> p (e t)")
                TT(t, t, side[:, 2:4].rearrange("p a b -> p (a b)"), ALU.mult)
                drain()
                for e in range(4):
                    last = STT(ya[:, i * 4 + e], lv[1][:, 1, e], vv[:, i * 4 + (V_NORM + e):i * 4 + (V_NORM + e + 1)],
                               ya[:, i * 4 + e], ALU.mult, ALU.mult)
                last.then_inc(y_done, 1)

            for i in range(2):
                for k in range(12):
                    split("mix", i, k + 1)
                    if i == k == 0:
                        dve.wait_ge(asum_ps, 9)
                        TT(mods2[:, 0:2 * KT], side[:, 3, ADA_PS:ADA_PS + 2 * KT], vv[:, V_BADA + 32:V_BADA + 64],
                           ALU.add)
                    if i and k == 0:
                        outputs(0)
                    if 2 <= k < 11:
                        level_scores(i, k - 2)
                    if 1 <= k < 10:
                        level_operands(i, k - 1)
                    if k == 10:
                        dve.wait_ge(o_exp, i + 1)
                        q4 = q_t[:, bass.ts(i, 4)]
                        TT(lv[0][:, 0], lv[0][:, 0], q4, ALU.mult)
                        TT(lv[0][:, 1], lv[0][:, 1], q4, ALU.mult).then_inc(o_op, 1)
                    if k == 3:
                        for b in range(4):
                            blk("mix", i, 0, b)
                            dve.wait_ge(gs_sig, i * 4 + (b + 1))
                            TT(ya[:, i * 4 + b], ya[:, i * 4 + b], main[:, b, 0:T],
                               ALU.mult).then_inc(freed["V"], 1)
                    if k == 11:
                        for b in range(4):
                            blk("mix", i, 2, b)
                            nc.vector.tensor_copy(xb[:, i * 4 + b], main[:, b, 0:T]).then_inc(freed["V"], 1)

            def gates(j, h, between):
                name, it = branch_phase(j, h)
                for k in range(12):
                    split(name, it, k + 1)
                    p, q = k // 6, k % 6
                    if k in SUMMED[name]:
                        done = SUMMED[name].index(k)
                        panels = len(SUMMED[name]) // 4
                        ada_sum(name, it, k + 1 + done, h * panels + (8 + 2 * j + done // 4), done % 4)
                    between(k)
                    if q == 5:
                        for b in range(4):
                            blk(name, it, 2 * p + 1, b)
                            dst = mT[:, h * 8 + (4 * p + b)]
                            if j == 0:
                                dve.wait_ge(freed["A"], it * 8 + (PH[name].f0["A"] + 4 * p + b + 1))
                                TT(dst, sg[:, b], main[:, b, 0:T], ALU.mult).then_inc(freed["V"], 1)
                            else:
                                dve.sem_inc(passed, 1)
                                drain()
                                dve.wait_ge(freed["A"], it * 8 + (PH[name].f0["A"] + 4 * p + b + 1))
                                TT(gz[:, b % 2], sg[:, b], main[:, b, 0:T], ALU.mult).then_inc(freed["V"], 1)
                                drain()
                                last = TT(dst, dst, gz[:, b % 2], ALU.add)
                                if j == 2:
                                    last.then_inc(m_done, 1)

            for h in range(2):
                def attend(k):
                    if h == 0 and k == 0:
                        outputs(1)
                    u = k - 2
                    if 0 <= u < 8:
                        c, s = col[:, u % 2], side[:, u % 2]
                        drain()
                        dve.wait_ge(at_sc, h * 8 + (u + 1))
                        TT(s[:, keys_of(u)], s[:, keys_of(u)],
                           cs[:, K_TRI + P * (u % 2):K_TRI + P * (u % 2 + 1)], ALU.add)
                        drain()
                        nc.vector.reduce_max(c[:, 0:1], s, AX)
                        drain()
                        TS(c[:, 1:2], c[:, 0:1], SCALE, vv[:, bass.ds(h * 4 + (V_SINK + u // 2), 1)],
                           ALU.mult, ALU.max)
                        drain()
                        TS(c[:, 2:3], c[:, 1:2], -1.0, None, ALU.mult).then_inc(at_max, 1)
                        dve.wait_ge(at_exp, h * 8 + (u + 1))
                        TT(c[:, 5:6], c[:, 3:4], c[:, 4:5], ALU.add)
                        drain()
                        nc.vector.reciprocal(c[:, 6:7], c[:, 5:6])
                        drain()
                        TS(pr[:, u % 2], pr[:, u % 2], c[:, 6:7], None, ALU.mult).then_inc(at_norm, 1)
                gates(0, h, attend)
            with dve.Fori(0, 2) as h:
                gates(1, h, lambda k: None)
            with dve.Fori(0, 2) as h:
                gates(2, h, lambda k: None)

            dve.wait_ge(asum_ps, 17)
            drain()
            TT(mods2[:, 2 * KT:], side[:, 3, ADA_PS + 2 * KT:ADA_PS + 4 * KT], vv[:, V_BADA + 64:V_BADA + 96], ALU.add)
            drain()
            l1g, l1b = vv[:, V_L1G:V_L1G + KT], vv[:, V_L1B:V_L1B + KT]
            sh2, sc2 = mods2[:, KT:2 * KT], mods2[:, 2 * KT:3 * KT]
            shift = mods1[:, 0:KT, 0]
            STT(shift, sc2, 1.0, l1b, ALU.add, ALU.mult)
            drain()
            TT(sh2, sh2, shift, ALU.add)
            STT(sc2, sc2, 1.0, l1g, ALU.add, ALU.mult)
            drain()
            TS(vv[:, V_L1G:V_L1G + 2 * KT], vv[:, V_L1G:V_L1G + 2 * KT], ALPHA, None, ALU.mult)
            drain()
            nc.vector.memset(mu[:], 0.0).then_inc(zero_set, 1)
            dve.wait_ge(ax_in, 2)
            with dve.Fori(0, 4) as i:
                for k in range(4):
                    split("out", i, k + 1)
                for b in range(4):
                    blk("out", i, 0, b)
                    n = i * 4 + b
                    STT(res[:, n], main[:, b, 0:T], mods2[:, bass.ds(n, 1)], ax[:, n],
                        ALU.mult, ALU.add).then_inc(freed["V"], 1)

            def norm(n, then):
                dve.wait_ge(mu_in, n + 1)
                for q in range(4):
                    r4 = res[:, 4 * q:4 * q + 4]
                    TT(r4, r4, mu[:].unsqueeze(1).to_broadcast([P, 4, T]), ALU.subtract).then_inc(cen_done, 1)
                dve.wait_ge(rstd_in, n + 1)
                for q in range(4):
                    r4 = res[:, 4 * q:4 * q + 4]
                    drain()
                    last = TT(r4, r4, rstd[:].unsqueeze(1).to_broadcast([P, 4, T]), ALU.mult)
                    then(q, last)

            def to_mlp(q, last):
                last.then_inc(h2_tmp, 1)
                drain()
                for n in range(4):
                    k = 4 * q + n
                    TS(h4[:, n], res[:, k], mods2[:, 2 * KT + k:2 * KT + k + 1], mods2[:, KT + k:KT + k + 1],
                       ALU.mult, ALU.add)
                drain()
                dve.wait_ge(h2_hi, q + 1)
                rows = slice(4 * q, 4 * q + 4)
                TT(h2[:, rows, 1], h4[:], h2[:, rows, 0].bitcast(F32), ALU.subtract).then_inc(h2_lo, 1)
                if q == 2:
                    split("mlp", 0, 2)

            split("mlp", 0, 1)
            norm(0, to_mlp)
            dve.wait_ge(acc_zero, 1)

            def mlp(f, last):
                def first(i, chunks=range(4)):
                    for k in chunks:
                        split("mlp", f * 8 + i, k + 1)
                    for b in range(4):
                        dve.wait_ge(hid_lo, f * 16 + i * 4 + (b + 1))
                        blk("mlp", f * 8 + i, 0, b)
                        nc.vector.tensor_scalar_max(sqb[:, b], main[:, b, 0:T], 0.0).then_inc(freed["V"], 1)

                if isinstance(f, int) and f == 0:
                    first(0, (2, 3))
                with dve.Fori(1 if isinstance(f, int) and f == 0 else 0, 4) as i:
                    first(i)

                def second(i, n):
                    for k in range(n):
                        split("mlp", f * 8 + i + 4, k + 1)
                    for b in range(4):
                        dst = acc[:, i * 4 + b]
                        drain()
                        blk("mlp", f * 8 + i + 4, 0, b)
                        TT(dst, dst, main[:, b, 0:T], ALU.add).then_inc(freed["V"], 1)

                with dve.Fori(0, 3) as i:
                    second(i, 4)
                second(3, 3 if last else 4)

            mlp(0, False)
            with dve.Fori(1, 3) as f:
                mlp(f, False)
            mlp(3, True)

            drain()
            for k in range(KT):
                STT(res[:, k], acc[:, k], mods2[:, 3 * KT + k:3 * KT + k + 1], ax[:, k],
                    ALU.mult, ALU.add).then_inc(res_done, 1)
            drain()

            def to_out(q, last):
                drain()
                for k in range(4 * q, 4 * q + 4):
                    last = TS(acc[:, k], res[:, k], vv[:, V_L2G + k:V_L2G + k + 1], vv[:, V_L2B + k:V_L2B + k + 1],
                              ALU.mult, ALU.add)
                last.then_inc(y_out, 1)

            norm(1, to_out)

        @block.tensor
        def _(pe):
            mm = nc.tensor.matmul

            def bank(name, it, panel, b):
                ph = PH[name]
                who, count = ph.bank_free(it, panel, b)
                pe.wait_ge(freed[who], count)

            def weights(name, it, s):
                ph = PH[name]
                pe.wait_ge(lo_made, ph.split_count(it, s))
                return ph.parity(s)

            def three(out, w_hi, w_lo, x_hi, x_lo, start, stop, skip=False):
                mm(out, w_hi, x_hi, start=start, stop=False, skip_group_check=skip)
                mm(out, w_hi, x_lo, start=False, stop=False, skip_group_check=skip)
                return mm(out, w_lo, x_hi, start=False, stop=stop, skip_group_check=skip)

            def panel(name, it, n, first, x, with_ctx=False, ready=None, between=lambda k: None):
                chunks = PH[name].panels[n][0]
                for k in range(chunks):
                    par = weights(name, it, first + k)
                    if ready is not None:
                        ready(k)
                    for b in range(4):
                        if k == 0:
                            bank(name, it, n, b)
                        for j in range(CK):
                            kt = k * CK + j
                            w_hi, w_lo = (w[:, par, j, P * b:P * (b + 1)] for w in (whi, wlo))
                            start, stop = kt == 0, kt == chunks * CK - 1
                            if with_ctx:
                                mm(main[:, b, 0:C], w_hi, hC[:, kt, 0], start=start, stop=False)
                                mm(main[:, b, 0:C], w_hi, hC[:, kt, 1], start=False, stop=False)
                                mm(main[:, b, 0:C], w_lo, hC[:, kt, 0], start=False, stop=stop)
                                last = three(main[:, b, C:], w_hi, w_lo, hL[:, kt, 0], hL[:, kt, 1],
                                             False, stop, skip=True)
                            else:
                                last = three(main[:, b, 0:T], w_hi, w_lo, x[:, kt, 0], x[:, kt, 1], start, stop)
                        if k == chunks - 1:
                            last.then_inc(blk_done, 1)
                    if k < chunks - 1:
                        last.then_inc(w_used, 1)
                    between(k)

            def turn(t):
                pe.wait_ge(freed["A"], t + 1)
                for b in range(4):
                    last = mm(side[:, 0, (4 * t + b) * 2:(4 * t + b) * 2 + 2], am[0:4, t % 2, P * b:P * (b + 1)],
                              cs[0:4, K_SEL:K_SEL + 2], start=True, stop=True)
                return last

            pe.wait_ge(silu_lo, 1)
            for t in range(8):
                for k in range(4):
                    weights("ada", 0, 4 * t + k)
                    hi, lo = split_place("ada", 4 * t + k)
                    if k == 0 and t >= 4:
                        bank("ada", 0, t, 0)
                    for j in range(CK):
                        kt = k * CK + j
                        mm(main[:, t % 4], sR[:, kt], hi[:, j], start=kt == 0, stop=False)
                        last = mm(main[:, t % 4], sR[:, kt], lo[:, j], start=False, stop=kt == KT - 1)
                    if k < 3:
                        last.then_inc(w_used, 1)
                last.then_inc(blk_done, 1)
                if t:
                    turn(t - 1).then_inc(am_used, 1)
            turn(7).then_inc(mods_ps, 1)

            def ada_turn(n):
                pe.wait_ge(ada_used, n * 4 + 4)
                for b in range(4):
                    last = mm(side[:, 3, bass.ds(n * 4 + (ADA_PS + b), 1)], asum[:, P * b:P * (b + 1)],
                              ones[:, 0:1], start=True, stop=True)
                last.then_inc(asum_ps, 1)

            mm(side[0:1, 3, 511:512], ones[:, 0:1], ones[:, 0:1], start=True, stop=True).then_inc(asum_ps, 1)

            def inputs_ready(k):
                pe.wait_ge(h_lo, 4 * k + 4)

            for t in range(2):
                for k in range(4):
                    par = weights("vals", 0, 4 * t + k)
                    inputs_ready(k)
                    for b in range(4):
                        if k == 0:
                            bank("vals", 0, t, b)
                        x, tile = (hC, hL)[b // 2], slice(P * (b % 2), P * (b % 2) + P)
                        for j in range(CK):
                            kt = k * CK + j
                            mm(main[:, b], x[:, kt, 0, tile], whi[:, par, j], start=kt == 0, stop=False)
                            mm(main[:, b], x[:, kt, 0, tile], wlo[:, par, j], start=False, stop=False)
                            last = mm(main[:, b], x[:, kt, 1, tile], whi[:, par, j], start=False, stop=kt == KT - 1)
                        if k == 3:
                            last.then_inc(blk_done, 1)
                    if k < 3:
                        last.then_inc(w_used, 1)
                    if t and k == 0:
                        ada_turn(t - 1)
            for k in range(4):
                par = weights("vals", 0, 8 + k)
                for b in range(4):
                    if k == 0:
                        bank("vals", 0, 2, b)
                    for j in range(CK):
                        kt = k * CK + j
                        start, stop = kt == 0, kt == KT - 1
                        if b < 2:
                            w_hi, w_lo = (w[:, par, j, P * b:P * (b + 1)] for w in (whi, wlo))
                            three(main[:, b, 0:C], w_hi, w_lo, hC[:, kt, 0], hC[:, kt, 1], start, stop)
                            last = three(main[:, b, C:], w_hi, w_lo, hL[:, kt, 0], hL[:, kt, 1], False, stop, True)
                        else:
                            x = (hC, hL)[b - 2]
                            for tile in range(2):
                                out, cols = main[:, b, 256 * tile:256 * (tile + 1)], slice(P * tile, P * (tile + 1))
                                w_hi, w_lo = whi[:, par, j, 256:512], wlo[:, par, j, 256:512]
                                mm(out, x[:, kt, 0, cols], w_hi, start=start and tile == 0, stop=False,
                                   skip_group_check=tile == 1)
                                mm(out, x[:, kt, 0, cols], w_lo, start=False, stop=False,
                                   skip_group_check=tile == 1)
                                last = mm(out, x[:, kt, 1, cols], w_hi, start=False, stop=stop,
                                          skip_group_check=tile == 1)
                    if k == 3:
                        last.then_inc(blk_done, 1)
                if k < 3:
                    last.then_inc(w_used, 1)
                if k == 0:
                    ada_turn(1)

            def keys_turned(it):
                pe.wait_ge(key_in, it * 4 + 4)
                for n in range(8):
                    last = nc.tensor.transpose(side[:, n // 4, P * (n % 4):P * (n % 4 + 1)],
                                               kc[:, n // 2, P * (n % 2):P * (n % 2 + 1)], cs[:, K_ID:K_ID + P])
                last.then_inc(key_tr, 1)

            def states(it):
                pe.wait_ge(key_cp, it + 1)
                for b in range(4):
                    head = HEADS_OF(it, b)
                    for tile in range(2):
                        last = mm(side[:, 2, HD * b:HD * (b + 1)], kcT[:, C * b + P * tile:C * b + P * (tile + 1)],
                                  vc[:, tile, head], start=tile == 0, stop=tile == 1)
                last.then_inc(st_ps, 1)

            def HEADS_OF(it, b):
                return bass.ds((it % 2) * PW + HD * b, HD)

            def forget(it, second):
                def between(k):
                    if k == 0:
                        ada_turn(it + 2)
                        if second:
                            states(it - 2)
                    if k == 3 and not (isinstance(it, int) and it == 0):
                        keys_turned(it - 1)
                panel("forget", it, 0, 0, None, with_ctx=True, between=between)

            forget(0, False)
            forget(1, False)
            with pe.Fori(2, 4) as i:
                forget(i, True)

            def query(k):
                if k == 0:
                    ada_turn(6)
                    states(2)
                if k == 4:
                    keys_turned(3)
                if k == 5:
                    states(3)
            panel("query", 0, 0, 0, hL, between=query)
            panel("query", 0, 1, 4, hL, between=lambda k: query(k + 4))
            ada_turn(7)

            def level(i, k):
                h = LEVELS[k]
                pe.wait_ge(lv_op, i * 9 + (k + 1))
                if k:
                    pe.wait_ge(lv_cp, i * 9 + k)
                for tile in range(2):
                    other = 1 - tile if h == 128 else tile
                    for e in range(4):
                        last = mm(side[:, tile, P * e:P * (e + 1)], lv[k % 2][:, 1, e, P * tile:P * (tile + 1)],
                                  lv[k % 2][:, 0, e, P * other:P * (other + 1)], start=True, stop=True)
                last.then_inc(lv_sc, 1)

            def outputs(i):
                pe.wait_ge(lv_cp, i * 9 + 9)
                pe.wait_ge(o_op, i + 1)
                pe.wait_ge(vg_in, i + 1)
                for e in range(4):
                    out = side[:, 2 + e // 2, T * (e % 2):T * (e % 2 + 1)]
                    cols = slice(HD * e, HD * (e + 1))
                    mm(out, vg[:, 0, cols], pT[:, 0, e], start=True, stop=False)
                    mm(out, vg[:, 1, cols], pT[:, 1, e], start=False, stop=False)
                    mm(out, sg_st[:, 0, cols], lv[0][:, 0, e], start=False, stop=False)
                    last = mm(out, sg_st[:, 1, cols], lv[0][:, 1, e], start=False, stop=True)
                last.then_inc(o_ps, 1)

            with pe.Fori(0, 2) as i:
                def beside(k):
                    if 1 <= k < 10:
                        level(i, k - 1)
                    if k == 10:
                        outputs(i)
                    if k == 11:
                        pe.wait_ge(o_sq, i + 1)
                        for n in range(2):
                            last = mm(side[:, n], ones[:], lv[1][:, 0].rearrange("p e t -> p (e t)")[:, PW * n:PW * (n + 1)],
                                      start=True, stop=True)
                        last.then_inc(o_ms, 1)
                for n in range(3):
                    panel("mix", i, n, 4 * n, hL, between=lambda k, n=n: beside(4 * n + k))

            def branch(j, h, between):
                name, it = branch_phase(j, h)
                for p in range(2):
                    panel(name, it, 2 * p, 6 * p, hL, between=lambda k: between(6 * p + k))

                    def after(k):
                        between(6 * p + 4 + k)
                        if k == 1 and (p or j == 2):
                            if j == 0:
                                pe.wait_ge(at_y, h * 4 + 4)
                            ada_turn(h + (8 + 2 * j) if j < 2 else h * 2 + (12 + p))

                    panel(name, it, 2 * p + 1, 6 * p + 4, yR[j % 2], ready=lambda k: pe.wait_ge(y_lo, j + 1),
                          between=after)

            with pe.Fori(0, 2) as h:
                def attend(k):
                    u = k
                    if u < 8:
                        if u == 0:
                            pe.wait_ge(at_rot, h + 1)
                            pe.wait_ge(o_rs, 2)
                        if u >= 2:
                            pe.wait_ge(at_exp, h * 8 + (u - 1))
                        mm(side[:, u % 2], qr[:, u // 2, P * (u % 2):P * (u % 2 + 1)], ak[:, h],
                           start=True, stop=True).then_inc(at_sc, 1)
                    u = k - 2
                    if 0 <= u < 8:
                        pe.wait_ge(at_norm, h * 8 + (u + 1))
                        if u:
                            pe.wait_ge(at_cp, h * 8 + u)
                        for n in range(4):
                            last = nc.tensor.transpose(side[:, 2, P * n:P * (n + 1)], pr[:, u % 2, P * n:P * (n + 1)],
                                                       cs[:, K_ID:K_ID + P])
                        last.then_inc(at_tr, 1)
                    u = k - 3
                    if 0 <= u < 8 and u % 2:
                        e = u // 2
                        pe.wait_ge(at_cp, h * 8 + (u + 1))
                        if u == 1:
                            pe.wait_ge(at_v, h + 1)
                        if e:
                            pe.wait_ge(at_y, h * 4 + e)
                        for n in range(4):
                            last = mm(side[:, 3, 0:T], avg[:, n], prT[:, e % 2, n], start=n == 0, stop=n == 3)
                        last.then_inc(at_o, 1)
                branch(0, h, attend)
            with pe.Fori(0, 2) as h:
                branch(1, h, lambda k: None)
            pe.wait_ge(pool_diff, 1)
            for b in range(8):
                if b == 7:
                    pe.wait_ge(pool_y, 2)
                out = side[:, (b % 7) // 2, (b % 7) % 2 * T:(b % 7) % 2 * T + T]
                for n in range(2):
                    last = mm(out, pw_sb[:, b // 2 * 2 + n, P * (b % 2):P * (b % 2 + 1)], pd[:, b // 2 * 2 + n],
                              start=n == 0, stop=n == 1)
                last.then_inc(pool_ps, 1)
            with pe.Fori(0, 2) as h:
                branch(2, h, lambda k: None)

            def sums(b, src, start, stop):
                return mm(side[:, b, 0:T], ones[:], src, start=start, stop=stop)

            def squares(n):
                for k in range(KT):
                    if k % 4 == 0:
                        pe.wait_ge(sq_done, 4 * n + k // 4 + 1)
                    last = sums(1, sqb[:, k], k == 0, k == KT - 1)
                last.then_inc(var_ps, 1)

            pe.wait_ge(zero_set, 1)
            sums(0, mu[:], True, False)
            with pe.Fori(0, 4) as i:
                panel("out", i, 0, 0, mR, ready=lambda k: pe.wait_ge(m_lo, k + 1))
                for b in range(4):
                    pe.wait_ge(freed["V"], i * 4 + (PH["out"].f0["V"] + b + 1))
                    sums(0, res[:, i * 4 + b], False, False)
            sums(0, mu[:], False, True).then_inc(mean_ps, 1)
            squares(0)

            with pe.Fori(0, 4) as f:
                with pe.Fori(0, 4) as i:
                    panel("mlp", f * 8 + i, 0, 0, h2, ready=lambda k: pe.wait_ge(h2_lo, k + 1))
                with pe.Fori(0, 4) as i:
                    panel("mlp", f * 8 + i + 4, 0, 0, hid, ready=lambda k: pe.wait_ge(hid_lo, f * 16 + (4 * k + 8)))
            for k in range(KT):
                pe.wait_ge(res_done, k + 1)
                last = sums(0, res[:, k], k == 0, k == KT - 1)
            last.then_inc(mean_ps, 1)
            squares(1)


def constants():
    cst = np.zeros((P, NK), np.float32)
    cst[:, K_ID:K_ID + P] = np.eye(P)
    q, k = np.arange(P)[:, None], np.arange(P)[None, :]
    cst[:, K_TRI:K_TRI + P] = np.where(k <= q, 0.0, NEG)
    cst[:, K_TRI + P:K_TRI + 2 * P] = np.where(k >= q, 0.0, NEG)
    freq = (10000.0 ** (-np.arange(HD // 4, dtype=np.float32) / (HD // 4))).astype(np.float32)
    t = np.arange(T)
    ang = np.concatenate([(t // GRID_W).astype(np.float32)[:, None] * freq,
                          (t % GRID_W).astype(np.float32)[:, None] * freq], -1).T
    cst[:, K_COS:K_COS + T] = np.concatenate([np.cos(ang)] * 2)
    cst[:, K_SIN:K_SIN + T] = np.concatenate([-np.sin(ang), np.sin(ang)])
    cst[0:4, K_SEL:K_SEL + 2] = np.eye(2)[[0, 1, 0, 1]]
    rcnt = np.zeros((P, 4, T), np.float32)
    for n, w in enumerate(WINDOWS):
        rcnt[:, n] = 1.0 / (np.clip(t + w // 2, 0, T) - np.clip(t - w // 2, 0, T))
    masks = np.zeros((P, 7, P), np.float32)
    for n, size in enumerate((64, 32, 16, 8, 4, 2, 1)):
        masks[:, n] = q // size == k // size
    return cst, rcnt, masks.reshape(P, 7 * P)


def chunks(w):
    K, N = w.shape
    w = w.reshape(K // (CK * P), CK, P, N // PW, PW).transpose(3, 0, 2, 1, 4)
    return np.ascontiguousarray(w).reshape(-1, P, CK * PW)


def columns(v):
    return v.reshape(-1, P).T


def kernel(**inputs):
    import concourse.bacc as bacc
    from concourse.bass_utils import run_bass_kernel_spmd

    a = {k: np.asarray(v) for k, v in inputs.items()}
    cst, rcnt, masks = constants()
    vecs = np.concatenate([columns(a["c"][0]), columns(a["c_ctx"]), columns(a["b_ada"][0]),
                           columns(a["hgrn_norm"][0]), columns(a["pool_scale"][0]), columns(a["ln1_g"][0]),
                           columns(a["ln1_b"][0]), columns(a["ln2_g"][0]), columns(a["ln2_b"][0]),
                           np.broadcast_to(a["attn_sink"][0], (P, HEADS))], axis=1)
    x2 = np.stack([a["ctx"][0], a["x"][0]])
    xT = x2.reshape(2, T, KT, P).transpose(3, 2, 0, 1).reshape(P, KT * 2 * T)
    f2 = a["w_ff2"][0].reshape(4, D, D)
    arrays = {
        "vecs": vecs, "cst": cst, "rcnt": rcnt, "masks": masks, "xT": xT,
        "w_ada": chunks(a["w_ada"][0]), "w_in": chunks(a["w_in"][0]),
        "pool_w": a["pool_w"][0].reshape(8, P, 256).transpose(1, 0, 2),
        "w_br": np.concatenate([chunks(w) for w in a["w_branch"][0]]),
        "w_out": chunks(a["w_out"][0]), "w_f1": chunks(a["w_ff1"][0]),
        "w_f2": np.concatenate([chunks(w) for w in f2]),
    }
    arrays = {f"in_{k}": np.ascontiguousarray(v) for k, v in arrays.items()}
    nc = bacc.Bacc("TRN2", target_bir_lowering=False, num_devices=1, dynamic_dma_scratch_size=1024)
    args = [nc.dram_tensor(k, v.shape, mybir.dt.from_np(v.dtype), kind="ExternalInput").ap()
            for k, v in arrays.items()]
    args.append(nc.dram_tensor("out_0", (P, KT, T), F32, kind="ExternalOutput").ap())
    build(nc, *args)
    r = run_bass_kernel_spmd(nc, [arrays], core_ids=[0])
    out = np.asarray(r.results[0]["out_0"])
    return out.transpose(2, 1, 0).reshape(1, T, D)
```
